# Optimizing a Trainium2 kernel written in Bass

```python
import math
import jax, jax.numpy as jnp
from jax import lax
import numpy as np

D_MODEL = 2048
BATCH = 1
SEQ = 256
DEPTH = 1

N_META = 16
GRID_W = 64
Q_BLOCK = 128
HEAD_DIM = 128
MIX_WIDTH = D_MODEL
A_WIDTH = MIX_WIDTH // 2
A_HEADS = A_WIDTH // HEAD_DIM
A_KV_HEADS = 2
A_GROUP = A_HEADS // A_KV_HEADS
B_WIDTH = MIX_WIDTH - A_WIDTH
B_V_DIM = HEAD_DIM
B_QK_DIM = HEAD_DIM // 2
B_HEADS = B_WIDTH // B_V_DIM

ROPE_THETA = 10000.0
NORM_EPS = 1e-6

A_Q_COLS = A_HEADS * HEAD_DIM
A_KV_COLS = A_KV_HEADS * HEAD_DIM
A_GATE_COLS = A_WIDTH
B_QK_COLS = B_HEADS * 2 * B_QK_DIM
B_V_COLS = B_HEADS * B_V_DIM
B_GATE_COLS = B_WIDTH
IN_PROJ_SIZES = (A_Q_COLS, A_KV_COLS, A_KV_COLS, A_GATE_COLS,
                 B_QK_COLS, B_QK_COLS, B_V_COLS, B_GATE_COLS)
IN_PROJ_WIDTH = sum(IN_PROJ_SIZES)
SPLIT_POINTS = tuple(int(c) for c in np.cumsum(IN_PROJ_SIZES)[:-1])


def rmsnorm(x, g):
    xf = x.astype(jnp.float32)
    r = lax.rsqrt(jnp.mean(xf * xf, axis=-1, keepdims=True) + NORM_EPS)
    return (xf * r * g.astype(jnp.float32)).astype(x.dtype)

def alibi_slopes(n_heads):
    return 2.0 ** (-8.0 * (jnp.arange(n_heads, dtype=jnp.float32) + 1.0) / n_heads)

def axial_angles(grid_pos):
    axis_dim = HEAD_DIM // 2
    inv_freq = ROPE_THETA ** (-jnp.arange(0, axis_dim, 2, dtype=jnp.float32) / axis_dim)
    return grid_pos.astype(jnp.float32)[:, None] * inv_freq[None, :]

def rope_half(x, ang):
    x1, x2 = jnp.split(x, 2, axis=-1)
    c, s = jnp.cos(ang), jnp.sin(ang)
    return jnp.concatenate([x1 * c - x2 * s, x2 * c + x1 * s], axis=-1)

def axial_rope(x, ang_row, ang_col):
    xf = x.astype(jnp.float32)
    xr, xc = jnp.split(xf, 2, axis=-1)
    return jnp.concatenate([rope_half(xr, ang_row), rope_half(xc, ang_col)], axis=-1).astype(x.dtype)

def sweep_query_blocks(attend, qs, qpos):
    meta_out = attend(tuple(q[..., :N_META, :] for q in qs), qpos[:N_META])
    n_real = qpos.shape[0] - N_META
    n_blk = n_real // Q_BLOCK

    def to_blocks(a):
        a = a[..., N_META:, :]
        a = a.reshape(a.shape[:-2] + (n_blk, Q_BLOCK, a.shape[-1]))
        return jnp.moveaxis(a, -3, 0)

    blk_q = tuple(to_blocks(q) for q in qs)
    blk_pos = qpos[N_META:].reshape(n_blk, Q_BLOCK)
    out = lax.map(lambda args: attend(args[0], args[1]), (blk_q, blk_pos))
    out = jnp.moveaxis(out, 0, -3)
    out = out.reshape(out.shape[:-3] + (n_real, out.shape[-1]))
    return jnp.concatenate([meta_out, out], axis=-2)

def heads_first(t, n_heads, d):
    b, l, _ = t.shape
    return t.reshape(b, l, n_heads, d).transpose(0, 2, 1, 3)

def gqa_axial_mixer(qa, ka, va, q_g, k_g, ang_row, ang_col, pos):
    b, l, _ = qa.shape
    q = axial_rope(rmsnorm(heads_first(qa, A_HEADS, HEAD_DIM), q_g), ang_row, ang_col)
    k = axial_rope(rmsnorm(heads_first(ka, A_KV_HEADS, HEAD_DIM), k_g), ang_row, ang_col)
    v = heads_first(va, A_KV_HEADS, HEAD_DIM)
    q = q.reshape(b, A_KV_HEADS, A_GROUP, l, HEAD_DIM)
    scale = 1.0 / math.sqrt(HEAD_DIM)

    def attend(qs, qpos):
        s = jnp.einsum('bkgqd,bksd->bkgqs', qs[0], k).astype(jnp.float32) * scale
        p = jax.nn.softmax(s, axis=-1)
        return jnp.einsum('bkgqs,bksd->bkgqd', p.astype(v.dtype), v)

    o = sweep_query_blocks(attend, (q,), pos)
    return o.transpose(0, 3, 1, 2, 4).reshape(b, l, A_WIDTH)

def diff_attn_mixer(qb, kb, vb, lq1, lk1, lq2, lk2, sub_g, lambda_init, pos):
    b, l, _ = qb.shape
    q = qb.reshape(b, l, B_HEADS, 2, B_QK_DIM).transpose(0, 2, 3, 1, 4)
    k = kb.reshape(b, l, B_HEADS, 2, B_QK_DIM).transpose(0, 2, 3, 1, 4)
    q1, q2 = q[:, :, 0], q[:, :, 1]
    k1, k2 = k[:, :, 0], k[:, :, 1]
    v = heads_first(vb, B_HEADS, B_V_DIM)
    lam = (jnp.exp(jnp.sum(lq1.astype(jnp.float32) * lk1.astype(jnp.float32)))
           - jnp.exp(jnp.sum(lq2.astype(jnp.float32) * lk2.astype(jnp.float32)))
           + lambda_init)
    slopes = alibi_slopes(B_HEADS)
    kpos = pos.astype(jnp.float32)
    scale = 1.0 / math.sqrt(B_QK_DIM)

    def attend(qs, qpos):
        dist = jnp.abs(qpos.astype(jnp.float32)[:, None] - kpos[None, :])
        bias = -slopes[:, None, None] * dist[None]
        s1 = jnp.einsum('bhqd,bhkd->bhqk', qs[0], k1).astype(jnp.float32) * scale + bias
        s2 = jnp.einsum('bhqd,bhkd->bhqk', qs[1], k2).astype(jnp.float32) * scale + bias
        a = jax.nn.softmax(s1, axis=-1) - lam * jax.nn.softmax(s2, axis=-1)
        return jnp.einsum('bhqk,bhkd->bhqd', a.astype(v.dtype), v)

    o = sweep_query_blocks(attend, (q1, q2), pos)
    o = rmsnorm(o, sub_g) * (1.0 - lambda_init)
    return o.transpose(0, 2, 1, 3).reshape(b, l, B_WIDTH)

def first_inputs(seed: int = 0) -> dict:
    key = jax.random.key(seed)
    ks = jax.random.split(key, 13)
    f32 = jnp.float32
    return {
        "x": jax.random.normal(ks[0], (BATCH, SEQ, D_MODEL), f32),
        "meta_tokens": jax.random.normal(ks[1], (N_META, D_MODEL), f32),
        "pre_norm_g": 1.0 + 0.02 * jax.random.normal(ks[2], (DEPTH, D_MODEL), f32),
        "w_in": jax.random.normal(ks[3], (DEPTH, D_MODEL, IN_PROJ_WIDTH), f32) * D_MODEL ** -0.5,
        "q_norm_g": 1.0 + 0.02 * jax.random.normal(ks[4], (DEPTH, HEAD_DIM), f32),
        "k_norm_g": 1.0 + 0.02 * jax.random.normal(ks[5], (DEPTH, HEAD_DIM), f32),
        "lambda_q1": 0.1 * jax.random.normal(ks[6], (DEPTH, B_QK_DIM), f32),
        "lambda_k1": 0.1 * jax.random.normal(ks[7], (DEPTH, B_QK_DIM), f32),
        "lambda_q2": 0.1 * jax.random.normal(ks[8], (DEPTH, B_QK_DIM), f32),
        "lambda_k2": 0.1 * jax.random.normal(ks[9], (DEPTH, B_QK_DIM), f32),
        "subln_g": 1.0 + 0.02 * jax.random.normal(ks[10], (DEPTH, B_V_DIM), f32),
        "w_out": jax.random.normal(ks[11], (DEPTH, MIX_WIDTH, D_MODEL), f32) * MIX_WIDTH ** -0.5,
        "post_norm_g": 1.0 + 0.02 * jax.random.normal(ks[12], (DEPTH, D_MODEL), f32),
    }

def first_block(x, meta_tokens, pre_norm_g, w_in, q_norm_g, k_norm_g, lambda_q1, lambda_k1,
              lambda_q2, lambda_k2, subln_g, w_out, post_norm_g):
    b, n_real, _ = x.shape
    meta = jnp.broadcast_to(meta_tokens.astype(x.dtype)[None], (b, N_META, D_MODEL))
    h = jnp.concatenate([meta, x], axis=1)
    seq_len = N_META + n_real
    pos = jnp.arange(seq_len, dtype=jnp.int32)

    rows = n_real // GRID_W
    grid_row = jnp.concatenate([jnp.zeros((N_META,), jnp.int32),
                                jnp.repeat(jnp.arange(rows, dtype=jnp.int32), GRID_W)])
    grid_col = jnp.concatenate([jnp.zeros((N_META,), jnp.int32),
                                jnp.tile(jnp.arange(GRID_W, dtype=jnp.int32), rows)])
    ang_row = axial_angles(grid_row)
    ang_col = axial_angles(grid_col)

    for layer in range(DEPTH):
        lambda_init = 0.8 - 0.6 * math.exp(-0.3 * layer)
        hn = rmsnorm(h, pre_norm_g[layer])
        proj = jnp.einsum('bld,dc->blc', hn, w_in[layer])
        qa, ka, va, ga, qb, kb, vb, gb = jnp.split(proj, SPLIT_POINTS, axis=-1)
        ya = gqa_axial_mixer(qa, ka, va, q_norm_g[layer], k_norm_g[layer],
                             ang_row, ang_col, pos) * jax.nn.silu(ga)
        yb = diff_attn_mixer(qb, kb, vb, lambda_q1[layer], lambda_k1[layer], lambda_q2[layer],
                             lambda_k2[layer], subln_g[layer], lambda_init, pos) * jax.nn.silu(gb)
        y = jnp.einsum('blc,cd->bld', jnp.concatenate([ya, yb], axis=-1), w_out[layer])
        h = h + rmsnorm(y, post_norm_g[layer])

    return h[:, N_META:, :]


CHUNK = 64
LEFT_CHUNKS = 8
BAND = LEFT_CHUNKS + 1
N_HEADS = 16
HEAD_DIM_2 = 64
ATTN_WIDTH = N_HEADS * HEAD_DIM_2
MAX_REL = 128
POOL_WINDOWS = (2, 4, 8, 16)
N_POOL_GROUPS = len(POOL_WINDOWS)
POOL_WIDTH = D_MODEL // 2
POOL_GROUP = POOL_WIDTH // N_POOL_GROUPS
IN_WIDTH = 3 * ATTN_WIDTH + POOL_WIDTH + 2 * D_MODEL
D_FF = ((8 * D_MODEL + 3 * 256 - 1) // (3 * 256)) * 256
EPS = 1e-6
NEG_INF = -1e30


def rms_norm(x, g):
    xf = x.astype(jnp.float32)
    y = xf * lax.rsqrt(jnp.mean(xf * xf, axis=-1, keepdims=True) + EPS)
    return (y * g.astype(jnp.float32)).astype(x.dtype)

def chunked_rel_attention(q, k, v, rel_bias):
    B, S, _ = q.shape
    nc = S // CHUNK
    qc = q.reshape(B, nc, CHUNK, N_HEADS, HEAD_DIM_2)
    pad = ((0, 0), (LEFT_CHUNKS * CHUNK, 0), (0, 0))
    kp = jnp.pad(k, pad).reshape(B, nc + LEFT_CHUNKS, CHUNK, N_HEADS, HEAD_DIM_2)
    vp = jnp.pad(v, pad).reshape(B, nc + LEFT_CHUNKS, CHUNK, N_HEADS, HEAD_DIM_2)
    band_idx = jnp.arange(nc)[:, None] + jnp.arange(BAND)[None, :]
    kb = kp[:, band_idx].reshape(B, nc, BAND * CHUNK, N_HEADS, HEAD_DIM_2)
    vb = vp[:, band_idx].reshape(B, nc, BAND * CHUNK, N_HEADS, HEAD_DIM_2)
    scale = 1.0 / math.sqrt(HEAD_DIM_2)
    s = jnp.einsum('bnihd,bnjhd->bhnij', qc, kb).astype(jnp.float32) * scale
    i = jnp.arange(CHUNK)
    j = jnp.arange(BAND * CHUNK)
    dist = LEFT_CHUNKS * CHUNK + i[:, None] - j[None, :]
    rel_idx = jnp.clip(dist, -MAX_REL, MAX_REL) + MAX_REL
    bias = rel_bias.astype(jnp.float32)[:, rel_idx]
    key_pos = (jnp.arange(nc)[:, None] - LEFT_CHUNKS) * CHUNK + j[None, :]
    valid = key_pos >= 0
    s = s + bias[None, :, None]
    s = jnp.where(valid[None, None, :, None, :], s, NEG_INF)
    p = jax.nn.softmax(s, axis=-1).astype(v.dtype)
    o = jnp.einsum('bhnij,bnjhd->bnihd', p, vb)
    return o.reshape(B, S, ATTN_WIDTH)

def multiscale_pool(u, pool_w, pool_scale):
    B, S, _ = u.shape
    uf = u.astype(jnp.float32)
    cs = jnp.concatenate([jnp.zeros((B, 1, POOL_WIDTH), jnp.float32),
                          jnp.cumsum(uf, axis=1)], axis=1)
    t = jnp.arange(S)
    outs = []
    for g, w in enumerate(POOL_WINDOWS):
        sl = slice(g * POOL_GROUP, (g + 1) * POOL_GROUP)
        lo = jnp.maximum(t + 1 - w, 0)
        cnt = (t + 1 - lo).astype(jnp.float32)[None, :, None]
        mean = (cs[:, 1:, sl] - cs[:, lo, sl]) / cnt
        outs.append(mean - uf[..., sl])
    d = jnp.stack(outs, axis=2).astype(u.dtype)
    y = jnp.einsum('bsgc,gce->bsge', d, pool_w).reshape(B, S, POOL_WIDTH)
    return y * pool_scale

def swiglu(h, w_gate_up, w_down):
    gu = h @ w_gate_up
    gate, up = gu[..., :D_FF], gu[..., D_FF:]
    return (jax.nn.silu(gate) * up) @ w_down

def second_inputs(seed: int = 0) -> dict:
    key = jax.random.key(seed)
    ks = jax.random.split(key, 16)
    f32 = jnp.float32

    def nrm(k, shape, fan_in):
        return jax.random.normal(k, shape, f32) * (fan_in ** -0.5)

    def gain(k, shape):
        return 1.0 + 0.02 * jax.random.normal(k, shape, f32)

    return {
        "x": jax.random.normal(ks[0], (BATCH, SEQ, D_MODEL), f32),
        "norm_mix": gain(ks[1], (DEPTH, D_MODEL)),
        "w_in": nrm(ks[2], (DEPTH, D_MODEL, IN_WIDTH), D_MODEL),
        "rel_bias": 0.1 * jax.random.normal(ks[3], (DEPTH, N_HEADS, 2 * MAX_REL + 1), f32),
        "pool_w": nrm(ks[4], (DEPTH, N_POOL_GROUPS, POOL_GROUP, POOL_GROUP), POOL_GROUP),
        "pool_scale": gain(ks[5], (DEPTH, POOL_WIDTH)),
        "w_branch_a": nrm(ks[6], (DEPTH, ATTN_WIDTH, D_MODEL), ATTN_WIDTH),
        "w_branch_b": nrm(ks[7], (DEPTH, POOL_WIDTH, D_MODEL), POOL_WIDTH),
        "w_out": nrm(ks[8], (DEPTH, D_MODEL, D_MODEL), D_MODEL),
        "norm_ffn": gain(ks[9], (DEPTH, D_MODEL)),
        "w_gate_up": nrm(ks[10], (DEPTH, D_MODEL, 2 * D_FF), D_MODEL),
        "w_down": nrm(ks[11], (DEPTH, D_FF, D_MODEL), D_FF),
        "norm_final": gain(ks[12], (D_MODEL,)),
    }

def second_block(x, norm_mix, w_in, rel_bias, pool_w, pool_scale, w_branch_a, w_branch_b,
              w_out, norm_ffn, w_gate_up, w_down, norm_final):
    a0 = 3 * ATTN_WIDTH
    a1 = a0 + POOL_WIDTH
    a2 = a1 + D_MODEL
    for l in range(DEPTH):
        h = rms_norm(x, norm_mix[l])
        z = h @ w_in[l]
        q = z[..., :ATTN_WIDTH]
        k = z[..., ATTN_WIDTH:2 * ATTN_WIDTH]
        v = z[..., 2 * ATTN_WIDTH:a0]
        u = z[..., a0:a1]
        gate_a = jax.nn.sigmoid(z[..., a1:a2])
        gate_b = jax.nn.sigmoid(z[..., a2:])
        y_a = chunked_rel_attention(q, k, v, rel_bias[l])
        y_b = multiscale_pool(u, pool_w[l], pool_scale[l])
        merged = gate_a * (y_a @ w_branch_a[l]) + gate_b * (y_b @ w_branch_b[l])
        x = x + merged @ w_out[l]
        x = x + swiglu(rms_norm(x, norm_ffn[l]), w_gate_up[l], w_down[l])
    return rms_norm(x, norm_final)


def setup_inputs(seed=0):
    out = dict(first_inputs(seed))
    for name, value in second_inputs(seed + 1).items():
        if name != "x":
            out[name + "_2"] = value
    return out


def reference(
    x, meta_tokens, pre_norm_g, w_in, q_norm_g, k_norm_g, lambda_q1, lambda_k1, lambda_q2,
    lambda_k2, subln_g, w_out, post_norm_g, norm_mix_2, w_in_2, rel_bias_2, pool_w_2,
    pool_scale_2, w_branch_a_2, w_branch_b_2, w_out_2, norm_ffn_2, w_gate_up_2, w_down_2,
    norm_final_2,
):
    x = first_block(
        x, meta_tokens, pre_norm_g, w_in, q_norm_g, k_norm_g, lambda_q1, lambda_k1, lambda_q2,
        lambda_k2, subln_g, w_out, post_norm_g,
    )
    return second_block(
        x, norm_mix_2, w_in_2, rel_bias_2, pool_w_2, pool_scale_2, w_branch_a_2, w_branch_b_2,
        w_out_2, norm_ffn_2, w_gate_up_2, w_down_2, norm_final_2,
    )


_drawn_inputs = setup_inputs


def setup_inputs(seed=0):
    import zlib

    import numpy as np

    out = dict(_drawn_inputs(seed))
    spreads = {}
    factors = {'q_norm_g': 8.0,
     'k_norm_g': 8.0,
     'lambda_q1': 2.761,
     'lambda_k2': 8.0,
     'subln_g': 3.221,
     'post_norm_g': 3.805,
     'norm_mix_2': 7.481,
     'rel_bias_2': 30.648,
     'pool_scale_2': 8.0,
     'norm_ffn_2': 21.121,
     'norm_final_2': 7.42}
    for name, (base, spread) in spreads.items():
        noise = np.random.default_rng([zlib.crc32(name.encode()), seed]).standard_normal(out[name].shape)
        drawn = base * np.exp(spread * noise) if base else spread * noise
        out[name] = __import__('jax').numpy.asarray(drawn.astype(out[name].dtype))
    for name, factor in factors.items():
        out[name] = (out[name] * factor).astype(out[name].dtype)
    return out
```

```python
import numpy as np

import concourse.bass as bass
from concourse import mybir
from concourse.alu_op_type import AluOpType as ALU

F32 = mybir.dt.float32
F32R = mybir.dt.float32r
ACT = mybir.ActivationFunctionType
AX = mybir.AxisListType.X

P = 128
D = 2048
KT = D // P
TOK = 256
TT = TOK // P
META = 16
KEYS = TOK + META
CW = 512
EPS = 1e-6
HD = 128
B_HEADS = 8
LAMBDA_INIT = 0.2
SCALE_A = float(1.0 / np.sqrt(np.float32(HD)))
SCALE_B = 0.125
HEADS2 = 16
REL = 384
DFF = 5632
FF_CHUNKS = DFF // CW
MASKED = -1e30

W1 = (("qb", 0, 5), ("kb", 0, 7), ("vb", 0, 9), ("kva", 0, 2), ("kb", 1, 8), ("vb", 1, 10), ("qb", 1, 6),
      ("qa", 0, 0), ("qa", 1, 1), ("ga", 0, 3), ("ga", 1, 4), ("gb", 0, 11), ("gb", 1, 12))
W1_META = tuple(b for b, w in enumerate(W1) if w[0] in ("kb", "vb", "kva"))
KVA = 3
Q_WOUT = len(W1)
Q_W2 = Q_WOUT + 4
Q_MIX = Q_W2 + 12
Q_WO2 = Q_MIX + 8
Q_FF = Q_WO2 + 4
Q_LOOP = Q_FF + 3
LOOPS = FF_CHUNKS - 2
Q_TAIL = Q_LOOP + 3 * LOOPS
B_W2 = Q_W2
B_MIX = Q_MIX
B_WO2 = B_MIX + 12
B_FF = B_WO2 + 4
B_LOOP = B_FF + 3
B_TAIL = B_LOOP + 6 * LOOPS

ITEMS1, ITEMS = 24, 40
START1, START2 = 49, 8 * 21 + 6


def start_of(n):
    return START1 + 2 * n if n < ITEMS1 else START2 + 2 * (n - ITEMS1)


def item_at(g, after):
    for n in range(ITEMS):
        if start_of(n) + after == g:
            return n
    return None


def is_b(n):
    return n < 16


def is_a(n):
    return 16 <= n < ITEMS1


G_X, G_Y, G_H1, G_POOL, G_ATT, G_MERGED, G_H2, G_FF = 0, 8, 16, 24, 28, 32, 40, 48
LATE = {26: G_POOL, 27: G_POOL + 2, 28: G_ATT, 29: G_ATT + 2}
LATE.update({31 + 2 * c: G_MERGED + 2 * c for c in range(4)})
LATE.update({Q_WO2 + 1 + c: G_H2 + 2 * c for c in range(4)})


def dims(ap, *free):
    return bass.AP(tensor=ap.tensor, offset=ap.offset, ap=[list(ap.ap[0])] + [list(f) for f in free])


class Chain:

    def __init__(self, engine, sem):
        self.engine, self.sem, self.n = engine, sem, 0

    def step(self, instruction):
        instruction.then_inc(self.sem, 1)
        self.n = self.n + 1
        return self.n

    def after(self, n):
        self.engine.wait_ge(self.sem, n)


def build(nc, t, out):
    from contextlib import ExitStack

    ctx = ExitStack()
    with ctx:
        base = (nc.sbuf_base + 63) // 64 * 64
        top = [base]

        def place(name, shape, dt=F32, at=None):
            size = 4 * int(np.prod(shape[1:]))
            if at is None:
                at = top[0]
                top[0] = at + (size + 31) // 32 * 32
            return nc.alloc_sbuf_tensor_at(name, shape, dt, offset=at)

        raw = place("raw", [P, 4, 4, CW])
        whi = place("whi", [P, 4, 2, CW], F32R)
        wlo = place("wlo", [P, 4, 2, CW], F32R)
        hhi = place("hhi", [P, KT, TOK], F32R)
        hlo = place("hlo", [P, KT, TOK], F32R)
        xres = place("xres", [P, TT, D])
        o_ybuf = top[0]
        ybuf = place("ybuf", [P, TT, D])
        o_r = top[0]
        place("region", [P, 64 * 256])
        MW = KT * 2 * META + P
        o_mhl = top[0]
        mhl = place("mhl", [P, MW], F32R)
        stg = place("stg", [P, TT, CW])
        ident = place("ident", [P, P])
        gcol = place("gcol", [P, 56])
        foldm = place("foldm", [2 * META, META])
        pbuf = place("pbuf", [P, 2, 2, KEYS])
        pt = place("pt", [P, 2, 3 * P])
        sm = place("sm", [P, ITEMS, 5])
        st = place("st", [P, 112])
        assert top[0] <= nc.sbuf_usable_end, (top[0], nc.sbuf_usable_end)
        qtb = place("qtb", [P, B_HEADS, TOK], at=o_r)
        ktb = place("ktb", [P, B_HEADS, KEYS], at=o_r + 8192)
        vb = place("vb", [P, TT, 1024], at=o_r + 16896)
        vbm = place("vbm", [META, 1024], at=o_r + 25088)
        qta = place("qta", [P, 8, TOK], at=o_r + 29184)
        kta = place("kta", [P, 2, KEYS], at=o_r + 37376)
        va = place("va", [P, TT, 256], at=o_r + 39552)
        vam = place("vam", [META, 256], at=o_r + 41600)
        rope = place("rope", [P, 10, P], at=o_r + 42624)
        dist = place("dist", [P, TT, KEYS], at=o_r + 47744)
        alibi = place("alibi", [P, 2, KEYS], at=o_r + 49920)
        junk = place("junk", [P, P], at=o_r + 52096)
        junk2 = place("junk2", [P, P], at=o_mhl)
        subg = place("subg", [P, P], at=o_r + 52608)
        tmp = place("tmp", [P, TT, CW], at=o_r + 53248)
        grow = place("grow", [P, D], at=o_r + 57344)
        yhi = place("yhi", [P, 8, TOK], F32R, at=o_r)
        ylo = place("ylo", [P, 8, TOK], F32R, at=o_r + 8192)
        metax = place("metax", [META, D], at=o_ybuf)
        grows = place("grows", [56, P], at=o_ybuf + 8192)
        mtmp = place("mtmp", [P, KT, META], at=o_ybuf + 8704)
        msb = place("msb", [2 * META, CW], at=o_ybuf + 9728)
        stgm = place("stgm", [META, CW], at=o_ybuf + 11776)
        lamt = place("lamt", [P, 4, 64], at=o_ybuf + 13824)
        gq = place("gq", [P, 2, P], at=o_ybuf + 14848)
        q2t = place("q2t", [P, 8, TOK], at=o_r)
        k2t = place("k2t", [P, 8, TOK], at=o_r + 8192)
        v2 = place("v2", [P, TT, 1024], at=o_r + 16384)
        ya = place("ya", [P, TT, 1024], at=o_r + 24576)
        ut = place("ut", [P, 8, TOK], at=o_r + 32768)
        poolw = place("poolw", [P, 8, TOK], at=o_r + 40960)
        ahi = place("ahi", [P, 8, TOK], F32R, at=o_r + 32768)
        alo = place("alo", [P, 8, TOK], F32R, at=o_r + 40960)
        bhi = place("bhi", [P, 8, TOK], F32R, at=o_r + 49152)
        blo = place("blo", [P, 8, TOK], F32R, at=o_r + 57344)
        mhi = place("mhi", [P, KT, TOK], F32R, at=o_r)
        mlo = place("mlo", [P, KT, TOK], F32R, at=o_r + 16384)
        bias2 = place("bias2", [P, HEADS2, TOK], at=o_ybuf)
        wina = place("wina", [P, 2, TOK], at=o_mhl)
        winb = place("winb", [P, 2, TOK], at=o_r + 57344 + 6144)
        reltab = place("reltab", [HEADS2, REL], at=o_r + 32768)
        fhi = [place(f"fhi{i}", [P, 4, TOK], F32R, at=o_r + 49152 + 8192 * i) for i in range(2)]
        flo = [place(f"flo{i}", [P, 4, TOK], F32R, at=o_r + 53248 + 8192 * i) for i in range(2)]
        gfin = place("gfin", [P, D], at=o_r + 32768)
        fgate = place("fgate", [P, TT, CW], at=o_ybuf)
        fup = place("fup", [P, TT, CW], at=o_ybuf + 4096)
        sqj = place("sqj", [P, CW], at=o_ybuf + 8192)
        outb = place("outb", [P, TT, D], at=o_r)
        invc = place("invc", [P, 4, 16], at=o_mhl + 2048)

        acc = [[ctx.enter_context(nc.psum_tensor(f"acc{p}{i}", [P, CW], F32)) for i in range(TT)] for p in range(2)]
        sbank = [ctx.enter_context(nc.psum_tensor(f"scores{i}", [P, CW], F32)) for i in range(2)]
        aux = [ctx.enter_context(nc.psum_tensor(f"aux{i}", [P, CW], F32)) for i in range(2)]

        ss = st[:, 0:3]
        nr1 = st[:, 4:6]
        lam = st[:, 6:7]
        lsum = st[:, 8:10]
        half = st[:, 12:32]
        rss = st[:, 32:60].rearrange("p (r h) -> p r h", h=4)
        ssy = st[:, 60:68].rearrange("p (i c) -> p i c", c=4)
        rp = st[:, 68:70]
        ssx = st[:, 70:78].rearrange("p (i c) -> p i c", c=4)
        r2 = st[:, 78:80]
        nr2 = st[:, 80:82]
        ssf = st[:, 82:90].rearrange("p (i c) -> p i c", c=4)
        r3 = st[:, 90:92]
        sso = st[:, 92:100].rearrange("p (i c) -> p i c", c=4)
        r4 = st[:, 100:102]

        def sem(name):
            return ctx.enter_context(nc.semaphore(name))

        raw_in = [sem(f"raw_in{u}") for u in range(4)]
        hi_ready, lo_ready, piece_used = sem("hi_ready"), sem("lo_ready"), sem("piece_used")
        stat_hi, stat_ready = sem("stat_hi"), sem("stat_ready")
        meta_scaled, meta_hi, meta_stat = sem("meta_scaled"), sem("meta_hi"), sem("meta_stat")
        aux_ready = sem("aux_ready")
        x_in = [sem(f"x_in{c}") for c in range(4)]
        meta_in, ident_in, gains_in, consts_in = sem("meta_in"), sem("ident_in"), sem("gains_in"), sem("consts_in")
        lam_in, grow_in, poolw_in, gfin_in = sem("lam_in"), sem("grow_in"), sem("poolw_in"), sem("gfin_in")
        rel_in, rel_out, bias2_in = sem("rel_in"), sem("rel_out"), sem("bias2_in")
        out_done = sem("out_done")
        gcol_ready, squares1, var1, rstd1, nrstd1 = sem("gcol_ready"), sem("squares1"), sem("var1"), sem("rstd1"), sem("nrstd1")
        rope_tables, mhl_zero, half_set, lam_sums, lam_exp, lam_ready = (
            sem("rope_tables"), sem("mhl_zero"), sem("half_set"), sem("lam_sums"), sem("lam_exp"), sem("lam_ready"))
        evicted = sem("evicted")
        meta_raw, meta_evicted = sem("meta_raw"), sem("meta_evicted")
        scores_ready, biased, negmax, exped, probs = sem("scores_ready"), sem("biased"), sem("negmax"), sem("exped"), sem("probs")
        pt_ready, osq, ovar, orstd, attended = sem("pt_ready"), sem("osq"), sem("ovar"), sem("orstd"), sem("attended")
        alibi_ready, rope_var, rope_rot, roped = sem("alibi_ready"), sem("rope_var"), sem("rope_rot"), sem("roped")
        qk_taken = sem("qk_taken")
        gated = sem("gated")
        ysq, post_scaled, yvar, yrstd, h1_ready, h1sq, h1var, h1rstd, nr2_ready = (
            sem("ysq"), sem("post_scaled"), sem("yvar"), sem("yrstd"), sem("h1_ready"), sem("h1sq"), sem("h1var"),
            sem("h1rstd"), sem("nr2_ready"))
        rel_fill, rel_filled, mask_set, pooled, gate_b, merged_a, merged, gate_a_done = (
            sem("rel_fill"), sem("rel_filled"), sem("mask_set"), sem("pooled"), sem("gate_b"), sem("merged_a"),
            sem("merged"), sem("gate_a_done"))
        h2_added, h2sq, h2var, h2rstd = sem("h2_added"), sem("h2sq"), sem("h2var"), sem("h2rstd")
        ff_gate, ff_up, down_added = sem("ff_gate"), sem("ff_up"), sem("down_added")
        last_sq, last_var, last_rstd, out_ready = sem("last_sq"), sem("last_var"), sem("last_rstd"), sem("out_ready")
        out_gained, out_last = sem("out_gained"), sem("out_last")
        dve_steps, pool_steps, act_steps = sem("dve_steps"), sem("pool_steps"), sem("act_steps")

        block = ctx.enter_context(nc.Block())
        use = {}

        def ff_bank(s):
            return aux[(use["ff"] + s) % 2]

        def taken_mix(b):
            if b < B_MIX:
                return evicted, b - B_W2 + Q_WOUT + 1
            c, what = (b - B_MIX) // 3, (b - B_MIX) % 3
            return ((gate_b, c + 1), (merged_a, c + 1), (merged, c + 1))[what]

        def late(q, j, transpose_group, aux_bank, aux_used, pe):
            if q not in LATE or j != 4:
                return
            for s in (LATE[q], LATE[q] + 1):
                if s < G_ATT:
                    w = s - G_POOL
                    pe.wait_ge(pooled, w + 1)
                    pe.wait_ge(poolw_in, 32)
                    bank = aux_bank()
                    for e in range(2):
                        for k in range(2):
                            done = nc.tensor.matmul(bank[:, e * TOK:(e + 1) * TOK], poolw[:, 2 * w + k, e * P:(e + 1) * P],
                                                    ut[:, 2 * w + k, :], start=k == 0, stop=k == 1)
                    done.then_inc(aux_ready, 1)
                    aux_used(("stat", s), (stat_ready, s + 1))
                elif s < G_MERGED:
                    pe.wait_ge(attended, ITEMS)
                    transpose_group(s, ya, 2 * (s - G_ATT))
                elif s < G_H2:
                    pe.wait_ge(merged, (s - G_MERGED) // 2 + 1)
                    transpose_group(s, ybuf, 2 * (s - G_MERGED))
                else:
                    pe.wait_ge(h2_added, (s - G_H2) // 2 + 1)
                    transpose_group(s, xres, 2 * (s - G_H2))

        def stat_home(s):
            if s < G_Y:
                return hhi[:, 2 * s:2 * s + 2, :], hlo[:, 2 * s:2 * s + 2, :], 2 * s
            if s < G_H1:
                k = 2 * (s - G_Y)
                if k < 8:
                    return yhi[:, k:k + 2, :], ylo[:, k:k + 2, :], None
                return hhi[:, k:k + 2, :], hlo[:, k:k + 2, :], None
            if s < G_POOL:
                k = 2 * (s - G_H1)
                return hhi[:, k:k + 2, :], hlo[:, k:k + 2, :], 16 + k
            if s < G_ATT:
                k = 2 * (s - G_POOL)
                return bhi[:, k:k + 2, :], blo[:, k:k + 2, :], 48 + k
            if s < G_MERGED:
                k = 2 * (s - G_ATT)
                return ahi[:, k:k + 2, :], alo[:, k:k + 2, :], None
            if s < G_H2:
                k = 2 * (s - G_MERGED)
                return mhi[:, k:k + 2, :], mlo[:, k:k + 2, :], None
            k = 2 * (s - G_H2)
            return hhi[:, k:k + 2, :], hlo[:, k:k + 2, :], 32 + k

        def y_squares(act, b):
            act.wait_ge(piece_used, 8 * b + 8)
            c = b - Q_WOUT
            for i in range(TT):
                if c or i:
                    act.wait_ge(ysq, TT * c + i)
                nc.scalar.activation(tmp[:, 0, :], acc[b % 2][i][:], ACT.Square, accum_out=ssy[:, i, c:c + 1]).then_inc(ysq, 1)

        def evict2(act, prev, banks, pieces):
            act.wait_ge(piece_used, pieces)
            if prev == 0:
                act.wait_ge(h1rstd, 1)
                act.wait_ge(nr2_ready, 1)
            for i in range(TT):
                if prev in (4, 5):
                    dst = v2[:, i, (prev - 4) * CW:(prev - 3) * CW]
                elif prev < 8:
                    dst = stg[:, i, :]
                else:
                    if prev == 8 and i == 0:
                        act.wait_ge(biased, 32)
                    dst = ybuf[:, i, (prev - 8) * CW:(prev - 7) * CW]
                if prev < 8:
                    done = nc.scalar.activation(dst, banks[i][:], ACT.Copy, scale=r2[:, i:i + 1])
                else:
                    done = nc.scalar.activation(dst, banks[i][:], ACT.Exp, scale=nr2[:, i:i + 1])
            done.then_inc(evicted, 1)

        def gate_a(dve, chain, prev, part):
            if part == 0:
                dve.wait_ge(evicted, Q_WOUT + prev + 1)
            y = ybuf[:, part // 2, (prev - 8) * CW + part % 2 * 256:(prev - 8) * CW + (part % 2 + 1) * 256]
            chain.after(chain.step(nc.vector.tensor_scalar(y, y, 1.0, None, ALU.add)))
            nc.vector.reciprocal(y, y).then_inc(gate_a_done, 1)

        def branch_a(dve, c):
            dve.wait_ge(piece_used, 8 * (Q_MIX + 2 * c + 1) + 4)
            dve.wait_ge(gate_a_done, 16)
            for i in range(TT):
                y = ybuf[:, i, c * CW:(c + 1) * CW]
                done = nc.vector.tensor_tensor(y, acc[(B_MIX + 3 * c + 1) % 2][i][:], y, ALU.mult)
            done.then_inc(merged_a, 1)

        def branch_b(dve, chain, c):
            dve.wait_ge(piece_used, 8 * (Q_MIX + 2 * c + 2))
            dve.wait_ge(gate_b, c + 1)
            dve.wait_ge(merged_a, c + 1)
            for i in range(TT):
                s = chain.step(nc.vector.tensor_tensor(stg[:, i, :], acc[(B_MIX + 3 * c + 2) % 2][i][:], stg[:, i, :], ALU.mult))
            chain.after(s)
            y = ybuf[:, :, c * CW:(c + 1) * CW]
            nc.vector.tensor_tensor(y, y, stg[:], ALU.add).then_inc(merged, 1)

        @block.tensor
        def _(pe):
            uses = [0]
            free_at = [None, None]

            def aux_bank():
                b = uses[0] % 2
                if free_at[b] is not None:
                    pe.wait_ge(*free_at[b])
                return aux[b]

            def aux_used(name, free):
                free_at[uses[0] % 2] = free
                use[name] = uses[0] + 1
                uses[0] += 1

            def piece(g, slot, first, last, banks, stat, kt0, meta=None):
                for k in range(2):
                    start, stop = first and k == 0, last and k == 1
                    hi, lo = whi[:, slot, k, :], wlo[:, slot, k, :]
                    for i in range(TT):
                        sh, sl = stat(kt0 + k, i)
                        nc.tensor.matmul(banks[i][:], sh, hi, start=start, stop=False)
                        nc.tensor.matmul(banks[i][:], sh, lo, start=False, stop=False)
                        done = nc.tensor.matmul(banks[i][:], sl, hi, start=False, stop=stop)
                    if meta is not None:
                        m = mhl[:, (kt0 + k) * 2 * META:(kt0 + k) * 2 * META + P]
                        nc.tensor.matmul(meta[:], m, hi, start=start, stop=False)
                        done = nc.tensor.matmul(meta[:], m, lo, start=False, stop=stop)
                done.then_inc(piece_used, 1)

            def h_stat(kt, i):
                return hhi[:, kt, i * P:(i + 1) * P], hlo[:, kt, i * P:(i + 1) * P]

            def y_stat(kt, i):
                hi, lo = (yhi, ylo) if kt < 8 else (hhi, hlo)
                return hi[:, kt, i * P:(i + 1) * P], lo[:, kt, i * P:(i + 1) * P]

            def m_stat(kt, i):
                return mhi[:, kt, i * P:(i + 1) * P], mlo[:, kt, i * P:(i + 1) * P]

            def a_stat(kt, i):
                return ahi[:, kt, i * P:(i + 1) * P], alo[:, kt, i * P:(i + 1) * P]

            def b_stat(kt, i):
                return bhi[:, kt, i * P:(i + 1) * P], blo[:, kt, i * P:(i + 1) * P]

            def transpose_group(s, src, kt):
                bank = aux_bank()
                for k in range(2):
                    for i in range(TT):
                        done = nc.tensor.transpose(bank[:, k * TOK + i * P:k * TOK + (i + 1) * P],
                                                   src[:, i, (kt + k) * P:(kt + k + 1) * P], ident[:])
                done.then_inc(aux_ready, 1)
                aux_used(("stat", s), (stat_ready, s + 1))

            def scores(n):
                if n == 0:
                    pe.wait_ge(meta_raw, len(W1_META))
                else:
                    pe.wait_ge(*((exped, n) if is_a(n - 1) else (biased, n if n <= 16 else n - 8)))
                if is_b(n):
                    h, i = n // 2, n % 2
                    for m in range(2):
                        done = nc.tensor.matmul(sbank[m][:, 0:KEYS], qtb[64 * m:64 * m + 64, h, i * P:(i + 1) * P],
                                                ktb[64 * m:64 * m + 64, h, :], start=True, stop=True)
                elif is_a(n):
                    h = n - 16
                    for i in range(TT):
                        done = nc.tensor.matmul(sbank[i][:, 0:KEYS], qta[:, h, i * P:(i + 1) * P],
                                                kta[:, h // 4, :], start=True, stop=True)
                else:
                    h = n - ITEMS1
                    r = slice(64 * (h % 2), 64 * (h % 2) + 64)
                    for i in range(TT):
                        keys = P * (i + 1)
                        done = nc.tensor.matmul(sbank[i][:, 0:keys], q2t[r, h // 2, i * P:(i + 1) * P],
                                                k2t[r, h // 2, 0:keys], start=True, stop=True)
                done.then_inc(scores_ready, 1)

            def transpose_probs(n):
                pe.wait_ge(*((probs, n + 1) if is_b(n) else (exped, n + 1)))
                if n < ITEMS1:
                    for i in range(1 if is_b(n) else 2):
                        bank = aux_bank()
                        p = pbuf[:, n % 2, i, :]
                        for k in range(2):
                            nc.tensor.transpose(bank[:, k * P:(k + 1) * P], p[:, k * P:(k + 1) * P], ident[:])
                        nc.tensor.transpose(bank[0:META, TOK:TOK + P], p[:, TOK:KEYS], ident[:]).then_inc(aux_ready, 1)
                        aux_used(("pt", n, i), (pt_ready, n + 1))
                else:
                    bank = aux_bank()
                    nc.tensor.transpose(bank[:, 0:P], pbuf[:, n % 2, 0, 0:P], ident[:])
                    for k in range(2):
                        done = nc.tensor.transpose(bank[:, (k + 1) * P:(k + 2) * P], pbuf[:, n % 2, 1, k * P:(k + 1) * P], ident[:])
                    done.then_inc(aux_ready, 1)
                    aux_used(("pt", n, 0), (pt_ready, n + 1))

            def attend(n):
                bank = aux_bank()
                pe.wait_ge(pt_ready, n + 1)
                if n < ITEMS1:
                    h = n // 2 if is_b(n) else (n - 16) // 4
                    v, vm = (vb, vbm) if is_b(n) else (va, vam)
                    c = slice(h * HD, (h + 1) * HD)
                    for i in range(1 if is_b(n) else 2):
                        o, w = bank[:, i * HD:(i + 1) * HD], pt[:, i, :]
                        for k in range(2):
                            nc.tensor.matmul(o, w[:, k * P:(k + 1) * P], v[:, k, c], start=k == 0, stop=False)
                        done = nc.tensor.matmul(o, w[0:META, TOK:TOK + P], vm[0:META, c], start=False, stop=True)
                else:
                    c = slice((n - ITEMS1) * 64, (n - ITEMS1 + 1) * 64)
                    nc.tensor.matmul(bank[:, 0:64], pt[:, 0, 0:P], v2[:, 0, c], start=True, stop=True)
                    nc.tensor.matmul(bank[:, 64:128], pt[:, 0, P:2 * P], v2[:, 0, c], start=True, stop=False)
                    done = nc.tensor.matmul(bank[:, 64:128], pt[:, 0, 2 * P:3 * P], v2[:, 1, c], start=False, stop=True)
                done.then_inc(aux_ready, 1)
                aux_used(("o", n), (attended, n + 1))

            def attention(g):
                n = item_at(g, 4)
                if n is not None:
                    transpose_probs(n)
                n = item_at(g, 0)
                if n is not None:
                    scores(n)
                n = item_at(g, 5)
                if n is not None:
                    attend(n)

            taken = [0]

            def transpose_heads(name, tiles):
                bank = aux_bank()
                at = 0
                for tile, rows in tiles:
                    done = nc.tensor.transpose(bank[:, at:at + rows], tile, ident[0:rows, 0:rows])
                    at += rows
                done.then_inc(aux_ready, 1)
                taken[0] += 1
                aux_used(name, (qk_taken, taken[0]))

            def head_pair(name, c):
                transpose_heads(name, [(stg[:, i, (c + k) * P:(c + k + 1) * P], P) for k in range(2) for i in range(TT)])

            pe.wait_ge(ident_in, 16)
            pe.wait_ge(gains_in, 64)
            nc.tensor.transpose(aux_bank()[:, 0:56], grows[:], ident[0:56, 0:56]).then_inc(aux_ready, 1)
            aux_used("gains", (gcol_ready, 1))
            for s in range(2):
                pe.wait_ge(x_in[0], 16)
                transpose_group(G_X + s, xres, 2 * s)

            def meta_transposes():
                pe.wait_ge(meta_in, 16)
                bank = aux_bank()
                for kt in range(KT):
                    done = nc.tensor.transpose(bank[:, kt * META:(kt + 1) * META], metax[:, kt * P:(kt + 1) * P],
                                               ident[0:META, 0:META])
                done.then_inc(aux_ready, 1)
                aux_used("meta", (meta_scaled, 1))

            for b in range(Q_WOUT):
                for j in range(8):
                    g = 8 * b + j
                    attention(g)
                    if b == 0 and j in (1, 3, 5):
                        pe.wait_ge(x_in[(j + 1) // 2], 16)
                        transpose_group(G_X + j + 1, xres, 2 * (j + 1))
                        transpose_group(G_X + j + 2, xres, 2 * (j + 2))
                    if b == 0 and j == 6:
                        meta_transposes()
                    if b == Q_WOUT - 1 and j in (1, 2, 6):
                        k = (1, 2, 6).index(j)
                        pe.wait_ge(attended, (20, 20, 22)[k])
                        transpose_group(G_Y + k, ybuf, 2 * k)
                    prev = b - 1
                    if prev in W1_META and j == 2:
                        m = W1_META.index(prev)
                        pe.wait_ge(meta_raw, m + 1)
                        if m == 0:
                            pe.wait_ge(consts_in, 96)
                        nc.tensor.matmul(aux_bank()[0:META, :], foldm[:], msb[:], start=True, stop=True).then_inc(aux_ready, 1)
                        aux_used(("fold", m), (meta_evicted, m + 1))
                    what = W1[prev][0] if b else None
                    if what == "kva" and j == 6:
                        pe.wait_ge(roped, 3)
                        head_pair(("ka", 0), 0)
                        transpose_heads(("kam", 0), [(stgm[:, k * P:(k + 1) * P], META) for k in range(2)])
                    if what in ("qb", "kb") and j in (4, 5):
                        pe.wait_ge(evicted, prev + 1)
                        head_pair(("t", prev, j - 4), 2 * (j - 4))
                    if what == "kb" and j == 6:
                        pe.wait_ge(meta_evicted, W1_META.index(prev) + 1)
                        transpose_heads(("tm", prev), [(stgm[:, k * P:(k + 1) * P], META) for k in range(4)])
                    if what == "qa" and j in (6, 7):
                        pe.wait_ge(roped, 3 + 2 * (prev - 6))
                        head_pair(("t", prev, j - 6), 2 * (j - 6))
                    if b == 0:
                        pe.wait_ge(stat_ready, G_X + j + 1)
                    if j == 0 and b >= 2:
                        pe.wait_ge(evicted, b - 1)
                    if j == 0 and b in W1_META:
                        m = W1_META.index(b)
                        if m == 0:
                            pe.wait_ge(meta_stat, 1)
                        elif m >= 2:
                            pe.wait_ge(meta_raw, m - 1)
                    pe.wait_ge(lo_ready, g + 1)
                    piece(g, g % 4, j == 0, j == 7, acc[b % 2], h_stat, 2 * j,
                          meta=sbank[W1_META.index(b) % 2] if b in W1_META else None)

            def y_group(s):
                if s == G_Y + 3:
                    pe.wait_ge(attended, ITEMS1)
                elif s > G_Y + 3:
                    pe.wait_ge(gated, 3 + (s - G_Y) // 6)
                transpose_group(s, ybuf, 2 * (s - G_Y))

            for c in range(4):
                b = Q_WOUT + c
                for j in range(8):
                    g = 8 * b + j
                    if c == 0 and j in (0, 1, 5):
                        for s in {0: (3, 4), 1: (5,), 5: (6, 7)}[j]:
                            y_group(G_Y + s)
                    if c == 0:
                        pe.wait_ge(stat_ready, G_Y + j + 1)
                    if j == 0:
                        pe.wait_ge(*((evicted, b - 1) if b - 2 < Q_WOUT else (post_scaled, b - 2 - Q_WOUT + 1)))
                    pe.wait_ge(lo_ready, g + 1)
                    piece(g, g % 4, j == 0, j == 7, acc[b % 2], y_stat, 2 * j)

            def h1_chunk(s):
                pe.wait_ge(h1_ready, 2 * ((s - G_H1) // 2 + 1))

            for s in range(G_H1, G_H1 + 2):
                h1_chunk(s)
                transpose_group(s, xres, 2 * (s - G_H1))
            for c in range(12):
                b = B_W2 + c
                for j in range(8):
                    g = 8 * b + j
                    attention(g)
                    prev = c - 1
                    if c == 0 and 1 <= j < 7:
                        h1_chunk(G_H1 + j + 1)
                        transpose_group(G_H1 + j + 1, xres, 2 * (j + 1))
                    if prev in (0, 1, 2, 3, 6, 7) and j in (4, 5):
                        pe.wait_ge(evicted, Q_WOUT + prev + 1)
                        head_pair(("t2", prev, j - 4), 2 * (j - 4))
                    late(b, j, transpose_group, aux_bank, aux_used, pe)
                    if c == 0:
                        pe.wait_ge(stat_ready, G_H1 + j + 1)
                    if j == 0:
                        pe.wait_ge(*((post_scaled, b - 2 - Q_WOUT + 1) if c < 2 else (evicted, Q_WOUT + c - 1)))
                    pe.wait_ge(lo_ready, g + 1)
                    piece(g, g % 4, j == 0, j == 7, acc[b % 2], h_stat, 2 * j)

            for c in range(4):
                for half_q in range(2):
                    q = Q_MIX + 2 * c + half_q
                    for j in range(8):
                        g = 8 * q + j
                        late(q, j, transpose_group, aux_bank, aux_used, pe)
                        b = B_MIX + 3 * c + (0 if half_q == 0 else 1 + j // 4)
                        if j == 0 or (half_q == 1 and j == 4):
                            pe.wait_ge(*taken_mix(b - 2))
                        pe.wait_ge(lo_ready, g + 1)
                        if half_q == 0:
                            piece(g, g % 4, j == 0, j == 7, acc[b % 2], h_stat, 2 * j)
                        else:
                            if c == 0 and j == 0:
                                pe.wait_ge(stat_ready, G_ATT + 4)
                            piece(g, g % 4, j % 4 == 0, j % 4 == 3, acc[b % 2], a_stat if j < 4 else b_stat, 2 * (j % 4))

            for c in range(4):
                q, b = Q_WO2 + c, B_WO2 + c
                for j in range(8):
                    g = 8 * q + j
                    late(q, j, transpose_group, aux_bank, aux_used, pe)
                    if c == 0 and j % 2 == 0:
                        pe.wait_ge(stat_ready, G_MERGED + j + 2)
                    if j == 0:
                        pe.wait_ge(*(taken_mix(b - 2) if c < 2 else (h2_added, c - 1)))
                    pe.wait_ge(lo_ready, g + 1)
                    piece(g, g % 4, j == 0, j == 7, acc[b % 2], m_stat, 2 * j)

            for c in range(3):
                q, b = Q_FF + c, B_FF + c
                for j in range(8):
                    g = 8 * q + j
                    late(q, j, transpose_group, aux_bank, aux_used, pe)
                    if c == 0 and j % 2 == 0:
                        pe.wait_ge(stat_ready, G_H2 + j + 2)
                    if c == 2 and j == 4:
                        pe.wait_ge(ff_up, 1)
                        for s in range(2):
                            transpose_group(G_FF + s, fgate, 2 * s)
                    if j == 0:
                        pe.wait_ge(*((h2_added, c + 3) if c < 2 else (ff_gate, 1)))
                    pe.wait_ge(lo_ready, g + 1)
                    piece(g, g % 4, j == 0, j == 7, acc[b % 2], h_stat, 2 * j)

            def f_stat(buf):
                return lambda kt, i: (fhi[buf][:, kt, i * P:(i + 1) * P], flo[buf][:, kt, i * P:(i + 1) * P])

            use["ff"] = uses[0]

            def ff_groups(i, base_use):
                pe.wait_ge(ff_up, i + 1)
                for s in range(2):
                    pe.wait_ge(stat_ready, G_FF + 2 * i - 1 + s)
                    for k in range(2):
                        for tt in range(TT):
                            done = nc.tensor.transpose(ff_bank(s)[:, k * TOK + tt * P:k * TOK + (tt + 1) * P],
                                                       fgate[:, tt, (2 * s + k) * P:(2 * s + k + 1) * P], ident[:])
                    done.then_inc(aux_ready, 1)

            with pe.Fori(0, LOOPS) as i:
                g0 = 8 * Q_LOOP + 24 * i
                for j in range(8):
                    m = j // 2
                    if j == 0:
                        pe.wait_ge(stat_ready, G_FF + 2 * i + 2)
                        pe.wait_ge(ff_up, i + 1)
                    if j == 2:
                        pe.wait_ge(ff_gate, i + 2)
                    if j in (4, 6):
                        pe.wait_ge(down_added, 4 * i + m - 1)
                    pe.wait_ge(lo_ready, g0 + j + 1)
                    piece(None, j % 4, j % 2 == 0, j % 2 == 1, acc[m % 2], f_stat(0), 2 * (j % 2))
                for j in range(8):
                    if j == 0:
                        pe.wait_ge(down_added, 4 * i + 3)
                    pe.wait_ge(lo_ready, g0 + 8 + j + 1)
                    piece(None, j % 4, j == 0, j == 7, acc[0], h_stat, 2 * j)
                for j in range(8):
                    if j == 0:
                        pe.wait_ge(down_added, 4 * i + 4)
                    if j == 4:
                        ff_groups(i + 1, None)
                    pe.wait_ge(lo_ready, g0 + 16 + j + 1)
                    piece(None, j % 4, j == 0, j == 7, acc[1], h_stat, 2 * j)

            last = FF_CHUNKS - 1
            for j in range(8):
                if j == 0:
                    pe.wait_ge(ff_up, last)
                pe.wait_ge(lo_ready, 8 * Q_TAIL + j + 1)
                piece(None, j % 4, j == 0, j == 7, acc[0], h_stat, 2 * j)
            for j in range(8):
                m = j // 2
                if j == 0:
                    pe.wait_ge(ff_gate, last + 1)
                if j == 2:
                    pe.wait_ge(ff_up, last + 1)
                if j == 4:
                    ff_groups(last, None)
                if j in (4, 6):
                    pe.wait_ge(down_added, 4 * (last - 1) + m - 1)
                pe.wait_ge(lo_ready, 8 * (Q_TAIL + 1) + j + 1)
                piece(None, j % 4, j % 2 == 0, j % 2 == 1, acc[(m + 1) % 2], f_stat(0), 2 * (j % 2))
            for j in range(8):
                m = j // 2
                if j == 0:
                    pe.wait_ge(stat_ready, G_FF + 2 * last + 2)
                if j % 2 == 0:
                    pe.wait_ge(down_added, 4 * last + m - 1)
                pe.wait_ge(lo_ready, 8 * (Q_TAIL + 2) + j + 1)
                piece(None, j % 4, j % 2 == 0, j % 2 == 1, acc[(m + 1) % 2], f_stat(1), 2 * (j % 2))

        @block.sync
        def _(sp):
            def rows(ap, n):
                return bass.AP(tensor=ap.tensor, offset=0, ap=[[0, P], [1, n]])

            def quad(q, srcs):
                for u in range(4):
                    sp.wait_ge(lo_ready, 8 * (q - 1) + 2 * u + 2)
                    sp.dma_start(raw[:, u], srcs[u].rearrange("(k p) n -> p k n", p=P)).then_inc(raw_in[u], 16)

            def column_block(w, c0):
                return [w[u * CW:(u + 1) * CW, bass.ds(c0, CW)] for u in range(4)]

            def row_block(w, r0):
                return [w[bass.ds(r0, CW), u * CW:(u + 1) * CW] for u in range(4)]

            w1, w2, wgu, wdn = t["w_in"][0], t["w_in_2"][0], t["w_gate_up_2"][0], t["w_down_2"][0]
            first = column_block(w1, W1[0][2] * CW)
            xs = t["x"][0].rearrange("(i p) d -> p i d", p=P)
            for u in range(4):
                sp.dma_start(xres[:, :, u * CW:(u + 1) * CW], xs[:, :, u * CW:(u + 1) * CW]).then_inc(x_in[u], 16)
                sp.dma_start(raw[:, u], first[u].rearrange("(k p) n -> p k n", p=P)).then_inc(raw_in[u], 16)
            for name, dst in (("rope_t", rope[:]), ("dist_t", dist[:]), ("fold_t", foldm[:])):
                sp.dma_start(dst, t[name]).then_inc(consts_in, 16)
            sp.dma_start(gq[:, 0, :], rows(t["q_norm_g"], P)).then_inc(consts_in, 16)
            sp.dma_start(gq[:, 1, :], rows(t["k_norm_g"], P)).then_inc(consts_in, 16)
            sp.dma_start(subg[:], rows(t["subln_g"], P)).then_inc(consts_in, 16)
            for n, name in enumerate(("lambda_q1", "lambda_k1", "lambda_q2", "lambda_k2")):
                sp.dma_start(lamt[:, n, :], rows(t[name], 64)).then_inc(lam_in, 16)
            sp.dma_start(grow[:], rows(t["post_norm_g"], D)).then_inc(grow_in, 16)
            for q in range(1, Q_WOUT):
                quad(q, column_block(w1, W1[q][2] * CW))
            for c in range(4):
                quad(Q_WOUT + c, column_block(t["w_out"][0], c * CW))
            for c in range(12):
                quad(Q_W2 + c, column_block(w2, c * CW))
                if c == 1:
                    sp.wait_ge(stat_ready, G_Y + 8)
                    sp.dma_start(invc[:], t["invc_t"]).then_inc(poolw_in, 16)
                    sp.dma_start(poolw[:], t["pool_w_2"][0].rearrange("g (k p) e -> p (g k) e", p=P)).then_inc(poolw_in, 16)
            for c in range(4):
                quad(Q_MIX + 2 * c, column_block(w2, (12 + c) * CW))
                wa, wb = t["w_branch_a_2"][0], t["w_branch_b_2"][0]
                cs = slice(c * CW, (c + 1) * CW)
                quad(Q_MIX + 2 * c + 1, [wa[0:CW, cs], wa[CW:2 * CW, cs], wb[0:CW, cs], wb[CW:2 * CW, cs]])
            for c in range(4):
                quad(Q_WO2 + c, column_block(t["w_out_2"][0], c * CW))
            quad(Q_FF, column_block(wgu, 0))
            quad(Q_FF + 1, column_block(wgu, DFF))
            quad(Q_FF + 2, column_block(wgu, CW))
            sp.wait_ge(merged, 4)
            sp.dma_start(gfin[:], rows(t["norm_final_2"], D)).then_inc(gfin_in, 16)
            with sp.Fori(0, LOOPS) as i:
                quad(Q_LOOP + 3 * i, row_block(wdn, i * CW))
                quad(Q_LOOP + 1 + 3 * i, column_block(wgu, DFF + (i + 1) * CW))
                quad(Q_LOOP + 2 + 3 * i, column_block(wgu, (i + 2) * CW))
            quad(Q_TAIL, column_block(wgu, DFF + 10 * CW))
            quad(Q_TAIL + 1, row_block(wdn, 9 * CW))
            quad(Q_TAIL + 2, row_block(wdn, 10 * CW))
            for n, (i, c) in enumerate(((0, 0), (0, 1), (1, 0))):
                cs = slice(c * 1024, (c + 1) * 1024)
                sp.wait_ge(out_ready, n + 1)
                sp.dma_start(out[0, i * P:(i + 1) * P, cs], outb[:, i, cs]).then_inc(out_done, 16)
            sp.wait_ge(out_done, 16 * 4)

        @block.scalar
        def _(act):
            chain = Chain(act, act_steps)

            def split(q, j):
                g = 8 * q + j
                if j % 2 == 0:
                    act.wait_ge(raw_in[j // 2], 16 * (q + 1))
                if not isinstance(g, int) or g >= 4:
                    act.wait_ge(piece_used, g - 3)
                nc.scalar.activation(whi[:, j % 4], raw[:, j // 2, 2 * (j % 2):2 * (j % 2) + 2, :], ACT.Copy).then_inc(hi_ready, 1)

            def stat_group(s):
                hi, _, g = stat_home(s)
                act.wait_ge(aux_ready, use["stat", s])
                bank = aux[(use["stat", s] - 1) % 2]
                if g is None:
                    nc.scalar.activation(hi, bank[:], ACT.Copy).then_inc(stat_hi, 1)
                else:
                    nc.scalar.activation(hi[:, 0, :], bank[:, 0:TOK], ACT.Copy, scale=gcol[:, g:g + 1])
                    nc.scalar.activation(hi[:, 1, :], bank[:, TOK:CW], ACT.Copy, scale=gcol[:, g + 1:g + 2]).then_inc(stat_hi, 1)

            def attention(g):
                n = item_at(g, 6)
                if n is not None:
                    for i in range(2 if is_a(n) else 1):
                        act.wait_ge(aux_ready, use["pt", n, i])
                        bank = aux[(use["pt", n, i] - 1) % 2]
                        if n < ITEMS1:
                            nc.scalar.activation(pt[:, i, 0:TOK], bank[:, 0:TOK], ACT.Copy)
                            done = nc.scalar.activation(pt[0:META, i, TOK:TOK + P], bank[0:META, TOK:TOK + P], ACT.Copy)
                        else:
                            done = nc.scalar.activation(pt[:, 0, :], bank[:, 0:3 * P], ACT.Copy)
                    done.then_inc(pt_ready, 1)
                n = item_at(g, 3)
                if n is not None:
                    act.wait_ge(negmax, n + 1)
                    for i in range(2):
                        keys = KEYS if n < ITEMS1 else P * (i + 1)
                        e = pbuf[:, n % 2, i, 0:keys]
                        done = nc.scalar.activation(e, sbank[i][:, 0:KEYS] if is_a(n) else e, ACT.Exp,
                                                    bias=sm[:, n, i:i + 1], scale=SCALE_A if is_a(n) else 1.0,
                                                    accum_out=sm[:, n, 2 + i:3 + i])
                    done.then_inc(exped, 1)
                n = item_at(g, 7)
                if n is not None and is_b(n):
                    act.wait_ge(aux_ready, use["o", n])
                    nc.scalar.activation(junk2[:], aux[(use["o", n] - 1) % 2][:, 0:HD], ACT.Square,
                                         accum_out=sm[:, n, 4:5]).then_inc(osq, 1)

            act.dma_start(ident[:], t["ident"]).then_inc(ident_in, 16)
            for n, (name, rows) in enumerate((("pre_norm_g", 16), ("norm_mix_2", 16), ("norm_ffn_2", 16), ("pool_scale_2", 8))):
                act.dma_start(grows[16 * n:16 * n + rows, :], t[name][0].rearrange("(k p) -> k p", p=P)).then_inc(gains_in, 16)
            act.dma_start(metax[:], t["meta_tokens"]).then_inc(meta_in, 16)
            act.wait_ge(aux_ready, use["gains"])
            nc.scalar.activation(gcol[:], aux[0][:, 0:56], ACT.Copy).then_inc(gcol_ready, 1)
            mview = mhl[:, 0:KT * 2 * META].rearrange("p (k m) -> p k m", m=2 * META)
            act.wait_ge(gcol_ready, 1)
            for s in range(2):
                stat_group(G_X + s)

            def meta_hi_part():
                mview = mhl[:, 0:KT * 2 * META].rearrange("p (k m) -> p k m", m=2 * META)
                act.wait_ge(meta_scaled, 1)
                act.wait_ge(mhl_zero, 1)
                nc.scalar.activation(mview[:, :, 0:META], mtmp[:], ACT.Copy).then_inc(meta_hi, 1)

            def block1_side(b, j):
                prev = b - 1
                if j == 2:
                    act.wait_ge(piece_used, 8 * b)
                    if prev == 0:
                        act.wait_ge(rstd1, 1)
                        act.wait_ge(nrstd1, 1)
                    if prev in W1_META:
                        m = W1_META.index(prev)
                        if m:
                            act.wait_ge(meta_evicted, m)
                        nc.scalar.activation(msb[:], sbank[m % 2][0:2 * META, :], ACT.Copy).then_inc(meta_raw, 1)
                    what, part = W1[prev][:2]
                    cs = slice(part * CW, (part + 1) * CW)
                    if what in ("ga", "gb"):
                        act.wait_ge(*((roped, 7) if (what, part) == ("ga", 0) else (gated, prev - 9)))
                    for i in range(TT):
                        src, r = acc[prev % 2][i], ss[:, i:i + 1]
                        if what == "kva":
                            nc.scalar.activation(va[:, i, :], src[:, 256:512], ACT.Copy, scale=r)
                            done = nc.scalar.activation(stg[:, i, 0:256], src[:, 0:256], ACT.Copy, scale=r)
                        elif what == "vb":
                            done = nc.scalar.activation(vb[:, i, cs], src[:], ACT.Copy, scale=r)
                        else:
                            if what in ("ga", "gb"):
                                nc.scalar.activation(tmp[:, i, :], src[:], ACT.Exp, scale=nr1[:, i:i + 1])
                            done = nc.scalar.activation(stg[:, i, :], src[:], ACT.Copy, scale=r)
                    done.then_inc(evicted, 1)
                if prev in W1_META and j == 4:
                    m = W1_META.index(prev)
                    act.wait_ge(aux_ready, use["fold", m])
                    bank, r = aux[(use["fold", m] - 1) % 2], ss[0:META, 2:3]
                    what, part = W1[prev][:2]
                    if what == "kva":
                        nc.scalar.activation(vam[:], bank[0:META, 256:512], ACT.Copy, scale=r)
                        done = nc.scalar.activation(stgm[:, 0:256], bank[0:META, 0:256], ACT.Copy, scale=r)
                    elif what == "vb":
                        done = nc.scalar.activation(vbm[:, part * CW:(part + 1) * CW], bank[0:META, :], ACT.Copy, scale=r)
                    else:
                        done = nc.scalar.activation(stgm[:], bank[0:META, :], ACT.Copy, scale=r)
                    done.then_inc(meta_evicted, 1)

            def take(name, dst, width, scale=1.0):
                act.wait_ge(aux_ready, use[name])
                nc.scalar.activation(dst, aux[(use[name] - 1) % 2][:, 0:width], ACT.Copy, scale=scale).then_inc(qk_taken, 1)

            def block1_take(b, j):
                prev = b - 1
                what, part = W1[prev][:2]
                h = 4 * part + 2 * (j - 6)
                if what == "kva" and j == 7:
                    take(("ka", 0), kta[:, :, 0:TOK], CW)
                    take(("kam", 0), kta[:, :, TOK:KEYS], 2 * META)
                if what == "kb" and j in (6, 7):
                    take(("t", prev, j - 6), ktb[:, h:h + 2, 0:TOK], CW)
                    if j == 7:
                        take(("tm", prev), ktb[:, 4 * part:4 * part + 4, TOK:KEYS], 4 * META)
                if what == "qb" and j in (6, 7):
                    take(("t", prev, j - 6), qtb[:, h:h + 2, :], CW, SCALE_B)

            def block1_take_late(b, j):
                if b >= 2 and W1[b - 2][0] == "qa" and j in (0, 1):
                    h = 4 * (b - 9) + 2 * j
                    take(("t", b - 2, j), qta[:, h:h + 2, :], CW)

            for b in range(Q_WOUT):
                for j in range(8):
                    split(b, j)
                    if b == 0 and j in (1, 3, 5):
                        stat_group(G_X + j + 1)
                        stat_group(G_X + j + 2)
                    if b == 0 and j == 6:
                        meta_hi_part()
                    if b == 0 and j in (5, 6, 7):
                        i = j - 5
                        if i < TT:
                            nc.scalar.activation((qtb, qta)[i][:].rearrange("p a b -> p (a b)"), xres[:, i, :], ACT.Square, accum_out=ss[:, i:i + 1]).then_inc(squares1, 1)
                        else:
                            nc.scalar.activation(vb[0:META].rearrange("p a b -> p (a b)"), metax[:], ACT.Square, accum_out=ss[0:META, 2:3]).then_inc(squares1, 1)
                    if b == 2 and j == 0:
                        act.wait_ge(lam_sums, 1)
                        nc.scalar.activation(lsum, lsum, ACT.Exp).then_inc(lam_exp, 1)
                    block1_take_late(b, j)
                    if b == Q_WOUT - 1 and j in (4, 5):
                        stat_group(G_Y + j - 4)
                    attention(8 * b + j)
                    if b:
                        block1_side(b, j)
                        block1_take(b, j)

            for c in range(4):
                b = Q_WOUT + c
                for j in range(8):
                    split(b, j)
                    if c == 0 and j == 1:
                        stat_group(G_Y + 2)
                    if c == 0 and j == 2:
                        block1_side(b, 2)
                        stat_group(G_Y + 3)
                        stat_group(G_Y + 4)
                    if c == 0 and j == 3:
                        stat_group(G_Y + 5)
                    if c == 0 and j == 7:
                        stat_group(G_Y + 6)
                        stat_group(G_Y + 7)
                    if c and j == 2:
                        y_squares(act, b - 1)

            for c in range(12):
                b = B_W2 + c
                for j in range(8):
                    split(b, j)
                    if c == 0 and j == 2:
                        y_squares(act, b - 1)
                        stat_group(G_H1)
                        stat_group(G_H1 + 1)
                    if c == 1 and j == 0:
                        stat_group(G_H1 + 7)
                    if c == 0 and j > 2:
                        stat_group(G_H1 + j - 1)
                        if j >= 4:
                            k = j - 4
                            for i in range(TT):
                                act.wait_ge(h1_ready, TT * k + i + 1)
                                done = nc.scalar.activation(tmp[:, 0, :], xres[:, i, k * CW:(k + 1) * CW], ACT.Square,
                                                            accum_out=ssx[:, i, k:k + 1])
                                chain.after(chain.step(done)) if (i, k) != (TT - 1, 3) else done.then_inc(h1sq, 1)
                    attention(8 * b + j)
                    prev = c - 1
                    if c == 1 and j == 3:
                        act.wait_ge(stat_ready, G_H1)
                        act.wait_ge(h1_ready, 8)
                        act.dma_start(reltab[:, 127:REL], t["rel_rev"]).then_inc(rel_in, 16)
                    if c == 1 and j == 7:
                        row = HEADS2 * REL
                        scratch = t["rel_scratch"].tensor
                        act.wait_ge(rel_filled, 1)
                        act.dma_start(bass.AP(tensor=scratch, offset=0, ap=[[REL, HEADS2], [row, P], [1, REL]]),
                                      dims(reltab[:], [0, P], [1, REL])).then_inc(rel_out, 16)
                    if c == 2 and j == 7:
                        act.wait_ge(rel_out, 16)
                        act.dma_start(bias2[:], bass.AP(tensor=scratch, offset=127,
                                                        ap=[[row - 1, P], [REL, HEADS2], [1, TOK]])).then_inc(bias2_in, 16)
                    if c and j == 2:
                        evict2(act, prev, acc[(b - 1) % 2], 8 * b)
                    if prev in (0, 1, 2, 3, 6, 7) and j in (6, 7):
                        k = 4 * (prev % 2) + 2 * (j - 6)
                        if prev < 2:
                            take(("t2", prev, j - 6), q2t[:, k:k + 2, :], CW, SCALE_B)
                        elif prev < 4:
                            take(("t2", prev, j - 6), k2t[:, k:k + 2, :], CW)
                        else:
                            take(("t2", prev, j - 6), ut[:, k:k + 2, :], CW)
                    if b in LATE and j == 6:
                        stat_group(LATE[b])
                        stat_group(LATE[b] + 1)

            for c in range(4):
                for half_q in range(2):
                    q = Q_MIX + 2 * c + half_q
                    for j in range(8):
                        split(q, j)
                        if c == 0 and half_q == 0 and j == 2:
                            evict2(act, 11, acc[(B_MIX - 1) % 2], 8 * q)
                        if half_q == 1 and j == 2:
                            act.wait_ge(piece_used, 8 * q)
                            if c:
                                act.wait_ge(merged, c)
                            b = B_MIX + 3 * c
                            for i in range(TT):
                                done = nc.scalar.activation(stg[:, i, :], acc[b % 2][i][:], ACT.Sigmoid, scale=r2[:, i:i + 1])
                            done.then_inc(gate_b, 1)
                        if q in LATE and j == 6:
                            stat_group(LATE[q])
                            stat_group(LATE[q] + 1)

            def h2_squares(k):
                act.wait_ge(h2_added, k + 1)
                for i in range(TT):
                    done = nc.scalar.activation(sqj[:], xres[:, i, k * CW:(k + 1) * CW], ACT.Square, accum_out=ssf[:, i, k:k + 1])
                    if (i, k) == (TT - 1, 3):
                        done.then_inc(h2sq, 1)
                    else:
                        chain.after(chain.step(done))

            def gate_silu(i_wait, piece):
                act.wait_ge(piece_used, piece)
                if i_wait is not None:
                    act.wait_ge(ff_up, i_wait)
                for i in range(TT):
                    done = nc.scalar.activation(fup[:, i, :], acc[1][i][:], ACT.Silu, scale=r3[:, i:i + 1])
                done.then_inc(ff_gate, 1)

            def ff_stat(i, s, buf, ready):
                act.wait_ge(aux_ready, ready)
                nc.scalar.activation(fhi[buf][:, 2 * s:2 * s + 2, :], ff_bank(s)[:], ACT.Copy).then_inc(stat_hi, 1)

            for c in range(4):
                q = Q_WO2 + c
                for j in range(8):
                    split(q, j)
                    if q in LATE and j == 6:
                        stat_group(LATE[q])
                        stat_group(LATE[q] + 1)
                    if c and j == 7:
                        h2_squares(c - 1)
            for c in range(3):
                q = Q_FF + c
                for j in range(8):
                    split(q, j)
                    if q in LATE and j == 6:
                        stat_group(LATE[q])
                        stat_group(LATE[q] + 1)
                    if c == 0 and j == 7:
                        h2_squares(3)
                    if c == 1 and j == 2:
                        act.wait_ge(h2rstd, 1)
                        gate_silu(None, 8 * q)
                    if c == 2 and j == 6:
                        for s in range(2):
                            ff_stat(0, s, 0, use["stat", G_FF + s])
            u0 = use["ff"]

            with act.Fori(0, LOOPS) as i:
                q0 = Q_LOOP + 3 * i
                for j in range(8):
                    split(q0, j)
                    if j == 2:
                        gate_silu(i + 1, 8 * q0)
                for j in range(8):
                    split(q0 + 1, j)
                for j in range(8):
                    split(q0 + 2, j)
                    if j == 6:
                        for s in range(2):
                            ff_stat(i + 1, s, 0, u0 + 2 * i + s + 1)
            last = FF_CHUNKS - 1
            for j in range(8):
                split(Q_TAIL, j)
                if j == 2:
                    gate_silu(last, 8 * Q_TAIL)
            for j in range(8):
                split(Q_TAIL + 1, j)
                if j == 6:
                    for s in range(2):
                        ff_stat(last, s, 1, u0 + 2 * (last - 1) + s + 1)
            for j in range(8):
                split(Q_TAIL + 2, j)
            for k in range(4):
                act.wait_ge(down_added, 4 * last + k + 1)
                for i in range(TT):
                    done = nc.scalar.activation(sqj[:], xres[:, i, k * CW:(k + 1) * CW], ACT.Square, accum_out=sso[:, i, k:k + 1])
                    if (i, k) == (TT - 1, 3):
                        done.then_inc(last_sq, 1)
                    else:
                        chain.after(chain.step(done))
            act.wait_ge(last_rstd, 1)
            act.wait_ge(out_gained, 1)
            o = outb[:, 1, 1024:2048]
            nc.scalar.activation(o, o, ACT.Copy, scale=r4[:, 1:2]).then_inc(out_last, 1)
            act.wait_ge(out_last, 1)
            act.dma_start(out[0, P:2 * P, 1024:2048], o).then_inc(out_done, 16)

        @block.vector
        def _(dve):
            chain = Chain(dve, dve_steps)

            def split(q, j):
                g = 8 * q + j
                dve.wait_ge(hi_ready, g + 1)
                nc.vector.tensor_tensor(wlo[:, j % 4], raw[:, j // 2, 2 * (j % 2):2 * (j % 2) + 2, :],
                                        whi[:, j % 4].bitcast(F32), ALU.subtract).then_inc(lo_ready, 1)

            def stat_group(s):
                hi, lo, g = stat_home(s)
                dve.wait_ge(stat_hi, s + 1)
                bank = aux[(use["stat", s] - 1) % 2]
                if g is None:
                    nc.vector.tensor_tensor(lo, bank[:], hi.bitcast(F32), ALU.subtract).then_inc(stat_ready, 1)
                else:
                    nc.vector.scalar_tensor_tensor(lo[:, 0, :], bank[:, 0:TOK], gcol[:, g:g + 1], hi[:, 0, :].bitcast(F32),
                                                   ALU.mult, ALU.subtract)
                    nc.vector.scalar_tensor_tensor(lo[:, 1, :], bank[:, TOK:CW], gcol[:, g + 1:g + 2], hi[:, 1, :].bitcast(F32),
                                                   ALU.mult, ALU.subtract).then_inc(stat_ready, 1)

            def part1(n):
                dve.wait_ge(scores_ready, n + 1)
                mx = sm[:, n, 0:2]
                if is_a(n):
                    for i in range(2):
                        s = chain.step(nc.vector.reduce_max(mx[:, i:i + 1], sbank[i][:, 0:KEYS], AX))
                    chain.after(s)
                else:
                    if is_b(n):
                        dve.wait_ge(alibi_ready, n + 1)
                    else:
                        dve.wait_ge(bias2_in, 16)
                        dve.wait_ge(mask_set, 1)
                    for i in range(2):
                        if is_b(n):
                            bias, keys = alibi[:, n % 2, :], KEYS
                        else:
                            keys = P * (i + 1)
                            bias = bias2[:, n - ITEMS1, TOK - keys:TOK]
                        done = nc.vector.tensor_tensor_reduce(pbuf[:, n % 2, i, 0:keys], sbank[i][:, 0:keys], bias, 1.0, -3e38,
                                                              ALU.add, ALU.max, mx[:, i:i + 1])
                        if i == 0:
                            s = chain.step(done)
                    done.then_inc(biased, 1)
                    chain.after(s)
                    dve.wait_ge(biased, n + 1 if is_b(n) else n - 7)
                nc.vector.tensor_scalar(mx, mx, -SCALE_A if is_a(n) else -1.0, None, ALU.mult).then_inc(negmax, 1)

            rinv_step = {}
            y_scaled = [0]

            def part2(n):
                dve.wait_ge(exped, n + 1)
                rs = sm[:, n, 2:4]
                s = chain.step(nc.vector.reciprocal(rs, rs))
                rinv_step[n] = s
                if is_b(n):
                    if n == 0:
                        dve.wait_ge(lam_ready, 1)
                    chain.after(s)
                    chain.after(chain.step(nc.vector.tensor_tensor(rs[:, 1:2], rs[:, 1:2], lam, ALU.mult)))
                    p = pbuf[:, n % 2]
                    chain.after(chain.step(nc.vector.tensor_scalar(p[:, 1, :], p[:, 1, :], rs[:, 1:2], None, ALU.mult)))
                    nc.vector.scalar_tensor_tensor(p[:, 0, :], p[:, 0, :], rs[:, 0:1], p[:, 1, :],
                                                   ALU.mult, ALU.subtract).then_inc(probs, 1)

            def part3(n):
                dve.wait_ge(aux_ready, use["o", n])
                bank = aux[(use["o", n] - 1) % 2]
                if is_b(n):
                    h, i = n // 2, n % 2
                    done = nc.vector.tensor_tensor(ybuf[:, i, 1024 + h * HD:1024 + (h + 1) * HD], bank[:, 0:HD], subg[:], ALU.mult)
                elif is_a(n):
                    h = n - 16
                    dve.wait_ge(gated, 1 + h // 4)
                    chain.after(rinv_step[n])
                    for i in range(TT):
                        y = ybuf[:, i, h * HD:(h + 1) * HD]
                        done = nc.vector.scalar_tensor_tensor(y, bank[:, i * HD:(i + 1) * HD], sm[:, n, 2 + i:3 + i], y,
                                                              ALU.mult, ALU.mult)
                else:
                    h = n - ITEMS1
                    chain.after(rinv_step[n])
                    for i in range(TT):
                        done = nc.vector.tensor_scalar(ya[:, i, h * 64:(h + 1) * 64], bank[:, i * 64:(i + 1) * 64],
                                                       sm[:, n, 2 + i:3 + i], None, ALU.mult)
                done.then_inc(attended, 1)

            def attention(g):
                n = item_at(g, 5)
                if n is not None:
                    part2(n)
                n = item_at(g, 3)
                if n is not None:
                    part1(n)
                n = item_at(g, 7)
                if n is not None and is_b(n):
                    dve.wait_ge(osq, n + 1)
                    nc.vector.tensor_scalar(sm[:, n, 4:5], sm[:, n, 4:5], 1.0 / HD, EPS, ALU.mult, ALU.add).then_inc(ovar, 1)
                    part3(n)
                n = item_at(g, 8)
                if n is not None and not is_b(n):
                    part3(n)
                n = item_at(g, 10)
                if n is not None and is_b(n):
                    dve.wait_ge(orstd, n + 1)
                    dve.wait_ge(attended, n + 1)
                    y = ybuf[:, n % 2, 1024 + n // 2 * HD:1024 + (n // 2 + 1) * HD]
                    y_scaled[0] = chain.step(nc.vector.tensor_scalar(y, y, sm[:, n, 4:5], None, ALU.mult))

            nc.vector.memset(half, -0.5).then_inc(half_set, 1)
            nc.vector.memset(mhl[:].bitcast(F32), 0.0).then_inc(mhl_zero, 1)
            dve.wait_ge(gcol_ready, 1)
            for s in range(2):
                stat_group(G_X + s)

            def meta_parts():
                mview = mhl[:, 0:KT * 2 * META].rearrange("p (k m) -> p k m", m=2 * META)
                dve.wait_ge(aux_ready, use["meta"])
                nc.vector.tensor_tensor(mtmp[:], aux[(use["meta"] - 1) % 2][:, 0:KT * META].rearrange("p (k m) -> p k m", m=META),
                                        dims(gcol[:, 0:KT], [1, KT], [0, META]), ALU.mult).then_inc(meta_scaled, 1)
                dve.wait_ge(meta_scaled, 1)
                dve.wait_ge(mhl_zero, 1)
                dve.wait_ge(meta_hi, 1)
                nc.vector.tensor_tensor(mview[:, :, META:2 * META], mtmp[:], mview[:, :, 0:META].bitcast(F32),
                                        ALU.subtract).then_inc(meta_stat, 1)

            def rope_sums(r, src, rows, heads):
                for h in range(heads):
                    s = chain.step(nc.vector.tensor_tensor_reduce(junk[0:rows, :], src[:, h * HD:(h + 1) * HD], src[:, h * HD:(h + 1) * HD],
                                                                  1.0, 0.0, ALU.mult, ALU.add, rss[0:rows, r, h:h + 1]))
                    chain.after(s)
                v = rss[0:rows, r, 0:heads]
                nc.vector.tensor_scalar(v, v, 1.0 / HD, EPS, ALU.mult, ALU.add).then_inc(rope_var, 1)

            def rope_scale(r, dst, rows, heads):
                dve.wait_ge(rope_rot, r + 1)
                nc.vector.tensor_tensor(dst.rearrange("p (h d) -> p h d", d=HD),
                                        tmp[0:rows, 0, 0:heads * HD].rearrange("p (h d) -> p h d", d=HD),
                                        dims(rss[0:rows, r, 0:heads], [1, heads], [0, HD]), ALU.mult).then_inc(roped, 1)

            def gate1(prev, part):
                if part == 0:
                    dve.wait_ge(evicted, prev + 1)
                if part < 4:
                    e = tmp[:, part // 2, part % 2 * 256:(part % 2 + 1) * 256]
                    chain.after(chain.step(nc.vector.tensor_scalar(e, e, 1.0, None, ALU.add)))
                    chain.step(nc.vector.reciprocal(e, e))
                    return
                chain.after(chain.n)
                if prev < 11:
                    nc.vector.tensor_tensor(ybuf[:, :, (prev - 9) * CW:(prev - 8) * CW], stg[:], tmp[:], ALU.mult).then_inc(gated, 1)
                else:
                    y = ybuf[:, :, 1024 + (prev - 11) * CW:1024 + (prev - 10) * CW]
                    chain.after(chain.step(nc.vector.tensor_tensor(tmp[:], stg[:], tmp[:], ALU.mult)))
                    nc.vector.tensor_tensor(y, y, tmp[:], ALU.mult).then_inc(gated, 1)

            def block1_side(b, j):
                prev = b - 1
                what = W1[prev][0]
                if what == "kva":
                    if j == 3:
                        dve.wait_ge(evicted, prev + 1)
                        rope_sums(0, stg[:, 0, 0:256], P, 2)
                        rope_sums(1, stg[:, 1, 0:256], P, 2)
                    if j == 4:
                        dve.wait_ge(meta_evicted, W1_META.index(prev) + 1)
                        rope_sums(2, stgm[:, 0:256], META, 2)
                        rope_scale(0, stg[:, 0, 0:256], P, 2)
                    if j == 5:
                        rope_scale(1, stg[:, 1, 0:256], P, 2)
                        rope_scale(2, stgm[:, 0:256], META, 2)
                if what == "qa":
                    r = 3 + 2 * (prev - 7)
                    if j in (3, 4):
                        dve.wait_ge(evicted, prev + 1)
                        rope_sums(r + j - 3, stg[:, j - 3, :], P, 4)
                    if j in (5, 6):
                        rope_scale(r + j - 5, stg[:, j - 5, :], P, 4)
                if what in ("ga", "gb") and j >= 3:
                    gate1(prev, j - 3)

            for b in range(Q_WOUT):
                for j in range(8):
                    split(b, j)
                    if b == 0 and j in (1, 3, 5):
                        stat_group(G_X + j + 1)
                        stat_group(G_X + j + 2)
                    if b == 0 and j == 6:
                        meta_parts()
                    if b == 1 and j == 5:
                        dve.wait_ge(lam_in, 64)
                        for k in range(2):
                            done = nc.vector.tensor_tensor_reduce(junk[:, 64 * k:64 * k + 64], lamt[:, 2 * k, :], lamt[:, 2 * k + 1, :], 1.0, 0.0,
                                                                  ALU.mult, ALU.add, lsum[:, k:k + 1])
                            if k == 0:
                                s = chain.step(done)
                        done.then_inc(lam_sums, 1)
                    if b == 1 and j == 6:
                        dve.wait_ge(consts_in, 96)
                        for n in range(10):
                            g = gq[:, 0 if n < 4 else 1, :]
                            tab = rope[:, n, :]
                            if n in (0, 1, 4, 5, 6):
                                s = chain.step(nc.vector.tensor_tensor(tab, tab, g, ALU.mult))
                            else:
                                tv = tab.rearrange("p (c s i) -> p c s i", c=2, s=2)
                                gv = g.rearrange("p (c s i) -> p c s i", c=2, s=2)
                                for k in range(2):
                                    s = chain.step(nc.vector.tensor_tensor(tv[:, :, k, :], tv[:, :, k, :], gv[:, :, 1 - k, :], ALU.mult))
                        chain.after(s)
                        nc.vector.tensor_scalar(subg[:], subg[:], 1.0 - LAMBDA_INIT, None, ALU.mult).then_inc(rope_tables, 1)
                    if b == 1 and j == 0:
                        dve.wait_ge(squares1, 3)
                        chain.after(chain.step(nc.vector.tensor_scalar(ss[:, 0:2], ss[:, 0:2], 1.0 / D, EPS, ALU.mult, ALU.add)))
                        nc.vector.tensor_scalar(ss[0:META, 2:3], ss[0:META, 2:3], 1.0 / D, EPS, ALU.mult, ALU.add).then_inc(var1, 1)
                        dve.wait_ge(rstd1, 1)
                        nc.vector.tensor_scalar(nr1, ss[:, 0:2], -1.0, None, ALU.mult).then_inc(nrstd1, 1)
                    if b == 2 and j == 1:
                        dve.wait_ge(lam_exp, 1)
                        chain.after(chain.step(nc.vector.tensor_tensor(lam, lsum[:, 0:1], lsum[:, 1:2], ALU.subtract)))
                        nc.vector.tensor_scalar(lam, lam, LAMBDA_INIT, None, ALU.add).then_inc(lam_ready, 1)
                    if b == Q_WOUT - 1 and j in (4, 5):
                        stat_group(G_Y + j - 4)
                    attention(8 * b + j)
                    if b:
                        block1_side(b, j)

            def post_scale(b):
                c = b - Q_WOUT
                if c == 0:
                    dve.wait_ge(grow_in, 16)
                    dve.wait_ge(stat_ready, G_Y + 8)
                cs = slice(c * CW, (c + 1) * CW)
                for i in range(TT):
                    dve.wait_ge(ysq, TT * c + i + 1)
                    done = nc.vector.tensor_tensor(ybuf[:, i, cs], acc[b % 2][i][:], grow[:, cs], ALU.mult)
                    if c == 3 and i == 0:
                        chain.step(done)
                        total(ssy, rp, yvar, ysq, 8)
                done.then_inc(post_scaled, 1)

            def total(src, dst, sem_out, sq, n):
                dve.wait_ge(sq, n)
                chain.after(chain.step(nc.vector.reduce_sum(dst, src, AX)))
                nc.vector.tensor_scalar(dst, dst, 1.0 / D, EPS, ALU.mult, ALU.add).then_inc(sem_out, 1)

            for c in range(4):
                b = Q_WOUT + c
                for j in range(8):
                    split(b, j)
                    if c == 0 and j == 1:
                        stat_group(G_Y + 2)
                    if c == 0 and j == 2:
                        stat_group(G_Y + 3)
                        stat_group(G_Y + 4)
                        gate1(12, 0)
                    if c == 0 and j == 3:
                        stat_group(G_Y + 5)
                        gate1(12, 1)
                        gate1(12, 2)
                    if c == 0 and j == 4:
                        gate1(12, 3)
                        gate1(12, 4)
                    if c == 0 and j == 7:
                        stat_group(G_Y + 6)
                        stat_group(G_Y + 7)
                    if c and j == 2:
                        post_scale(b - 1)

            def h1_chunk(c):
                cs = slice(c * CW, (c + 1) * CW)
                for i in range(TT):
                    x = xres[:, i, cs]
                    nc.vector.scalar_tensor_tensor(x, ybuf[:, i, cs], rp[:, i:i + 1], x, ALU.mult, ALU.add).then_inc(h1_ready, 1)

            for c in range(12):
                b = B_W2 + c
                for j in range(8):
                    split(b, j)
                    if c == 0 and j == 2:
                        post_scale(b - 1)
                        dve.wait_ge(post_scaled, 4)
                        dve.wait_ge(yrstd, 1)
                        h1_chunk(0)
                        stat_group(G_H1)
                        stat_group(G_H1 + 1)
                        h1_chunk(1)
                    if c == 0 and j > 2:
                        stat_group(G_H1 + j - 1)
                        if j in (3, 5):
                            h1_chunk((j + 1) // 2)
                    if c == 1 and j == 0:
                        stat_group(G_H1 + 7)
                    if c == 1 and j == 0:
                        total(ssx, r2, h1var, h1sq, 1)
                        dve.wait_ge(h1rstd, 1)
                        nc.vector.tensor_scalar(nr2, r2, -1.0, None, ALU.mult).then_inc(nr2_ready, 1)
                    if c == 3 and j == 4:
                        dve.wait_ge(bias2_in, 16)
                        nc.vector.memset(bias2[0:64, :, 192:256], MASKED).then_inc(mask_set, 1)
                    attention(8 * b + j)
                    if c - 1 in (8, 9, 10) and 3 <= j < 7:
                        gate_a(dve, chain, c - 1, j - 3)
                    if b in LATE and j == 6:
                        stat_group(LATE[b])
                        stat_group(LATE[b] + 1)

            for c in range(4):
                for half_q in range(2):
                    q = Q_MIX + 2 * c + half_q
                    for j in range(8):
                        split(q, j)
                        if c == 0 and half_q == 0 and 3 <= j < 7:
                            gate_a(dve, chain, 11, j - 3)
                        if half_q == 1 and j == 6:
                            branch_a(dve, c)
                        if half_q == 0 and c and j == 2:
                            branch_b(dve, chain, c - 1)
                        if q in LATE and j == 6:
                            stat_group(LATE[q])
                            stat_group(LATE[q] + 1)

            def h2_add(c):
                dve.wait_ge(piece_used, 8 * (Q_WO2 + c) + 8)
                for i in range(TT):
                    x = xres[:, i, c * CW:(c + 1) * CW]
                    done = nc.vector.tensor_tensor(x, acc[(B_WO2 + c) % 2][i][:], x, ALU.add)
                done.then_inc(h2_added, 1)

            def up_times_gate(i_wait, piece):
                dve.wait_ge(piece_used, piece)
                dve.wait_ge(ff_gate, i_wait)
                for i in range(TT):
                    done = nc.vector.scalar_tensor_tensor(fgate[:, i, :], acc[0][i][:], r3[:, i:i + 1], fup[:, i, :], ALU.mult, ALU.mult)
                done.then_inc(ff_up, 1)

            def ff_stat(s, buf, groups):
                dve.wait_ge(stat_hi, groups)
                nc.vector.tensor_tensor(flo[buf][:, 2 * s:2 * s + 2, :], ff_bank(s)[:], fhi[buf][:, 2 * s:2 * s + 2, :].bitcast(F32),
                                        ALU.subtract).then_inc(stat_ready, 1)

            def down_add(m, par, piece):
                dve.wait_ge(piece_used, piece)
                for i in range(TT):
                    x = xres[:, i, m * CW:(m + 1) * CW]
                    done = nc.vector.tensor_tensor(x, acc[par][i][:], x, ALU.add)
                done.then_inc(down_added, 1)

            for c in range(4):
                q = Q_WO2 + c
                for j in range(8):
                    split(q, j)
                    if c == 0 and j == 2:
                        branch_b(dve, chain, 3)
                    if c and j == 2:
                        h2_add(c - 1)
                    if q in LATE and j == 6:
                        stat_group(LATE[q])
                        stat_group(LATE[q] + 1)
            for c in range(3):
                q = Q_FF + c
                for j in range(8):
                    split(q, j)
                    if c == 0 and j == 2:
                        h2_add(3)
                    if q in LATE and j == 6:
                        stat_group(LATE[q])
                        stat_group(LATE[q] + 1)
                    if c == 1 and j == 0:
                        total(ssf, r3, h2var, h2sq, 1)
                    if c == 2 and j == 2:
                        dve.wait_ge(h2rstd, 1)
                        up_times_gate(1, 8 * q)
                        dve.wait_ge(h2_added, 4)
                    if c == 2 and j == 6:
                        for s in range(2):
                            ff_stat(s, 0, G_FF + s + 1)
            with dve.Fori(0, LOOPS) as i:
                q0 = Q_LOOP + 3 * i
                for j in range(8):
                    split(q0, j)
                    if j in (4, 6):
                        m = (j - 4) // 2
                        down_add(m, m, 8 * q0 + 2 * m + 2)
                for j in range(8):
                    split(q0 + 1, j)
                    if j in (0, 2):
                        m = 2 + j // 2
                        down_add(m, m % 2, 8 * q0 + 2 * m + 2)
                for j in range(8):
                    split(q0 + 2, j)
                    if j == 2:
                        up_times_gate(i + 2, 8 * q0 + 16)
                    if j == 6:
                        for s in range(2):
                            ff_stat(s, 0, G_FF + 2 * i + 2 + s + 1)
            last = FF_CHUNKS - 1
            gained = [0]

            def times_gain(m):
                cs = slice(m * CW, (m + 1) * CW)
                dve.wait_ge(down_added, 4 * last + m + 1)
                if m == 0:
                    dve.wait_ge(gfin_in, 16)
                for i in range(TT):
                    done = nc.vector.tensor_tensor(outb[:, i, cs], xres[:, i, cs], gfin[:, cs], ALU.mult)
                    if m == 3 and i == TT - 1:
                        done.then_inc(out_gained, 1)
                    else:
                        gained[0] = chain.step(done)

            for j in range(8):
                split(Q_TAIL, j)
            for j in range(8):
                split(Q_TAIL + 1, j)
                if j == 2:
                    up_times_gate(last + 1, 8 * Q_TAIL + 8)
                if j in (4, 6):
                    m = (j - 4) // 2
                    down_add(m, (m + 1) % 2, 8 * (Q_TAIL + 1) + 2 * m + 2)
                if j == 6:
                    for s in range(2):
                        ff_stat(s, 1, G_FF + 2 * last + s + 1)
            for j in range(8):
                split(Q_TAIL + 2, j)
                if j in (0, 2):
                    m = 2 + j // 2
                    down_add(m, (m + 1) % 2, 8 * (Q_TAIL + 1) + 2 * m + 2)
                if j in (4, 6):
                    m = (j - 4) // 2
                    down_add(m, (m + 1) % 2, 8 * (Q_TAIL + 2) + 2 * m + 2)
                    times_gain(m)
            down_add(2, 1, 8 * (Q_TAIL + 2) + 6)
            times_gain(2)
            down_add(3, 0, 8 * (Q_TAIL + 2) + 8)
            times_gain(3)
            total(sso, r4, last_var, last_sq, 1)
            dve.wait_ge(last_rstd, 1)
            chain.after(gained[0])
            dve.wait_ge(out_gained, 1)
            for i, c in ((0, 0), (0, 1), (1, 0)):
                o = outb[:, i, c * 1024:(c + 1) * 1024]
                nc.vector.tensor_scalar(o, o, r4[:, i:i + 1], None, ALU.mult).then_inc(out_ready, 1)

        @block.gpsimd
        def _(pool):
            chain = Chain(pool, pool_steps)

            def rsqrt(v):
                shape = v.shape[1]
                return nc.gpsimd.tensor_tensor(v, v, half[0:v.shape[0], 0:shape], ALU.pow)

            def rotate(r, src, rows, heads, table):
                pool.wait_ge(rope_var, r + 1)
                if r:
                    pool.wait_ge(roped, r)
                if r == 0:
                    pool.wait_ge(rope_tables, 1)
                chain.after(chain.step(rsqrt(rss[0:rows, r, 0:heads])))
                w = heads * HD
                cos, sin = rope[0:rows, table[0], :], rope[0:rows, table[1], :]
                t0, t1 = tmp[0:rows, 0, 0:w], tmp[0:rows, 1, 0:w]
                chain.after(chain.step(nc.gpsimd.tensor_tensor(t0.rearrange("p (h d) -> p h d", d=HD), src.rearrange("p (h d) -> p h d", d=HD),
                                                   dims(cos, [0, heads], [1, HD]), ALU.mult)))
                for c in range(2):
                    for k in range(2):
                        at = c * 64 + k * 32
                        other = c * 64 + (1 - k) * 32
                        s = chain.step(nc.gpsimd.tensor_tensor(dims(t1[:, at:at + 32], [HD, heads], [1, 32]), dims(src[:, other:other + 32], [HD, heads], [1, 32]),
                                                               dims(sin[:, at:at + 32], [0, heads], [1, 32]), ALU.mult))
                chain.after(s)
                nc.gpsimd.tensor_tensor(t0, t0, t1, ALU.add).then_inc(rope_rot, 1)

            def block1(g):
                n = item_at(g, -2)
                if n is not None and is_b(n):
                    if n == 0:
                        pool.wait_ge(consts_in, 96)
                    if n >= 2:
                        pool.wait_ge(biased, n - 1)
                    nc.gpsimd.tensor_scalar(alibi[:, n % 2, :], dist[:, n % 2, :], -(2.0 ** -(n // 2 + 1)), None, ALU.mult).then_inc(alibi_ready, 1)
                n = item_at(g, 7)
                if n is not None and is_b(n):
                    pool.wait_ge(ovar, n + 1)
                    rsqrt(sm[:, n, 4:5]).then_inc(orstd, 1)
                b, j = g // 8, g % 8
                if b == 1:
                    if j == 0:
                        pool.wait_ge(var1, 1)
                        chain.after(chain.step(rsqrt(ss[:, 0:2])))
                        rsqrt(ss[0:META, 2:3]).then_inc(rstd1, 1)
                if b == KVA + 1:
                    if j in (3, 4):
                        rotate(j - 3, stg[:, j - 3, 0:256], P, 2, (4 + j - 3, 7 + j - 3))
                    if j == 5:
                        rotate(2, stgm[:, 0:256], META, 2, (6, 9))
                if b and W1[b - 1][0] == "qa" and j in (3, 4):
                    rotate(3 + 2 * (b - 8) + j - 3, stg[:, j - 3, :], P, 4, (j - 3, 2 + j - 3))

            pool.wait_ge(half_set, 1)
            for g in range(8 * Q_WOUT):
                block1(g)
            pool.wait_ge(yvar, 1)
            rsqrt(rp).then_inc(yrstd, 1)
            pool.wait_ge(h1var, 1)
            rsqrt(r2).then_inc(h1rstd, 1)
            pool.wait_ge(rel_in, 16)
            nc.gpsimd.tensor_copy(reltab[:, 0:127], dims(reltab[:, 127:128], [0, 127])).then_inc(rel_filled, 1)
            pool.wait_ge(poolw_in, 32)
            for w in range(4):
                pool.wait_ge(qk_taken, 16 + 8 + w + 1)
                u = ut[:, 2 * w:2 * w + 2, :]
                bufs = [wina[:], winb[:]]
                src = u
                if w:
                    pool.wait_ge(pooled, w)
                for level in range(w + 1):
                    d = 1 << level
                    dst = bufs[level % 2]
                    s1 = chain.step(nc.gpsimd.tensor_copy(dst[:, :, 0:d], src[:, :, 0:d]))
                    s2 = chain.step(nc.gpsimd.tensor_tensor(dst[:, :, d:TOK], src[:, :, d:TOK], src[:, :, 0:TOK - d], ALU.add))
                    chain.after(s2)
                    src = dst
                win = 2 << w
                s1 = chain.step(nc.gpsimd.tensor_tensor(src[:, :, 0:16], src[:, :, 0:16],
                                                        dims(invc[:, w, :], [0, 2], [1, 16]), ALU.mult))
                s2 = chain.step(nc.gpsimd.tensor_scalar(src[:, :, 16:TOK], src[:, :, 16:TOK], 1.0 / win, None, ALU.mult))
                chain.after(s2)
                nc.gpsimd.tensor_tensor(u, src, u, ALU.subtract).then_inc(pooled, 1)
            pool.wait_ge(h2var, 1)
            rsqrt(r3).then_inc(h2rstd, 1)
            pool.wait_ge(last_var, 1)
            rsqrt(r4).then_inc(last_rstd, 1)


def tables():
    f = np.float32
    inv_freq = (np.float64(10000.0) ** (-np.arange(0, 64, 2) / 64.0)).astype(f)
    real = np.arange(TOK)
    row = np.concatenate([real // 64, np.zeros(META)]).astype(f)
    col = np.concatenate([real % 64, np.zeros(META)]).astype(f)
    ang = [(v[:, None] * inv_freq[None, :]).astype(f).astype(np.float64) for v in (row, col)]
    cos = np.concatenate([np.cos(a) for a in ang for _ in range(2)], 1).astype(f)
    sin = np.concatenate([s * np.sin(a) for a in ang for s in (-1, 1)], 1).astype(f)
    rope = np.zeros((P, 10, P), f)
    for n, (tab, i) in enumerate([(cos, 0), (cos, 1), (sin, 0), (sin, 1), (cos, 0), (cos, 1), (cos, 2), (sin, 0), (sin, 1), (sin, 2)]):
        part = tab[i * P:(i + 1) * P]
        rope[:len(part), n] = part
    qpos = META + np.arange(TOK).reshape(TT, P).T
    kpos = np.concatenate([META + np.arange(TOK), np.arange(META)])
    dist = np.abs(qpos[:, :, None] - kpos[None, None, :]).astype(f)
    fold = np.concatenate([np.eye(META)] * 2).astype(f)
    count = np.minimum(np.arange(16)[None, :] + 1, 2 << np.arange(4)[:, None])
    invc = np.broadcast_to((1.0 / count).astype(f), (P, 4, 16)).copy()
    return {"ident": np.eye(P, dtype=f), "rope_t": rope, "dist_t": dist, "fold_t": fold, "invc_t": invc}


INPUTS = ("x", "meta_tokens", "pre_norm_g", "w_in", "q_norm_g", "k_norm_g", "lambda_q1", "lambda_k1", "lambda_q2",
          "lambda_k2", "subln_g", "w_out", "post_norm_g", "norm_mix_2", "w_in_2", "pool_w_2", "pool_scale_2",
          "w_branch_a_2", "w_branch_b_2", "w_out_2", "norm_ffn_2", "w_gate_up_2", "w_down_2", "norm_final_2")


def kernel(**inputs):
    import numpy as np
    from concourse import bacc
    from concourse.bass_utils import run_bass_kernel_spmd

    nc = bacc.Bacc("TRN2", target_bir_lowering=False, num_devices=1)
    arrays = {name: np.ascontiguousarray(inputs[name]) for name in INPUTS}
    arrays["rel_rev"] = np.ascontiguousarray(inputs["rel_bias_2"][0][:, ::-1])
    arrays.update(tables())
    t = {name: nc.dram_tensor(name, a.shape, F32, kind="ExternalInput").ap() for name, a in arrays.items()}
    t["rel_scratch"] = nc.dram_tensor("rel_scratch", (P, HEADS2, REL), F32, kind="Internal").ap()
    out = nc.dram_tensor("out", (1, TOK, D), F32, kind="ExternalOutput").ap()
    build(nc, t, out)
    return run_bass_kernel_spmd(nc, [arrays], core_ids=[0]).results[0]["out"]
```

```python
import numpy as np

import concourse.bass as bass
from concourse import mybir
from concourse.alu_op_type import AluOpType as ALU

F32 = mybir.dt.float32
F32R = mybir.dt.float32r
ACT = mybir.ActivationFunctionType
AX = mybir.AxisListType.X

P = 128
D = 2048
KT = D // P
TOK = 256
TT = TOK // P
META = 16
KEYS = TOK + META
CW = 512
EPS = 1e-6
HD = 128
B_HEADS = 8
LAMBDA_INIT = 0.2
SCALE_A = float(1.0 / np.sqrt(np.float32(HD)))
SCALE_B = 0.125
HEADS2 = 16
REL = 384
DFF = 5632
FF_CHUNKS = DFF // CW
MASKED = -1e30

W1 = (("qb", 0, 5), ("kb", 0, 7), ("kb", 1, 8), ("vb", 0, 9), ("kva", 0, 2), ("vb", 1, 10), ("qb", 1, 6),
      ("qa", 0, 0), ("qa", 1, 1), ("ga", 0, 3), ("ga", 1, 4), ("gb", 0, 11), ("gb", 1, 12))
W1_META = tuple(b for b, w in enumerate(W1) if w[0] in ("vb", "kva"))
KVA = 4
Q_WOUT = len(W1)
Q_W2 = Q_WOUT + 4
Q_MIX = Q_W2 + 12
Q_WO2 = Q_MIX + 8
Q_FF = Q_WO2 + 4
Q_LOOP = Q_FF + 3
LOOPS = FF_CHUNKS - 2
Q_TAIL = Q_LOOP + 3 * LOOPS
B_W2 = Q_W2
B_MIX = Q_MIX
B_WO2 = B_MIX + 12
B_FF = B_WO2 + 4
B_LOOP = B_FF + 3
B_TAIL = B_LOOP + 6 * LOOPS

TURNED_ORDER = ((0, 1), (1, 0), (1, 1), (2, 0), (2, 1), (6, 1)) + tuple((Q_W2 + c, 1) for c in (0, 1, 2, 3, 6, 7))
TURNED = {key: n + 1 for n, key in enumerate(TURNED_ORDER)}
EVICTED = {b: n + 1 for n, b in enumerate((3, 4, 5, 7, 8, 9, 10, 11, 12) + tuple(Q_W2 + c for c in (4, 5, 8, 9, 10, 11)))}


def is_kb(q):
    return q < Q_WOUT and W1[q][0] == "kb"


ITEMS1, ITEMS = 24, 40
START1, START2 = 49, 8 * 21 + 6


def start_of(n):
    return START1 + 2 * n if n < ITEMS1 else START2 + 2 * (n - ITEMS1)


def item_at(g, after1, after2=None):
    for n in range(ITEMS):
        if start_of(n) + (after1 if n < ITEMS1 or after2 is None else after2) == g:
            return n
    return None


def is_b(n):
    return n < 16


def is_a(n):
    return 16 <= n < ITEMS1


G_X, G_Y, G_H1, G_POOL, G_ATT, G_MERGED, G_H2, G_FF = 0, 8, 16, 24, 28, 32, 40, 48
LATE = {26: G_POOL, 27: G_POOL + 2, 28: G_ATT, 29: G_ATT + 2}
LATE.update({31 + 2 * c: G_MERGED + 2 * c for c in range(4)})
LATE.update({Q_WO2 + 1 + c: G_H2 + 2 * c for c in range(4)})


def dims(ap, *free):
    return bass.AP(tensor=ap.tensor, offset=ap.offset, ap=[list(ap.ap[0])] + [list(f) for f in free])


class Chain:

    def __init__(self, engine, sem):
        self.engine, self.sem, self.n = engine, sem, 0

    def step(self, instruction):
        instruction.then_inc(self.sem, 1)
        self.n = self.n + 1
        return self.n

    def after(self, n):
        self.engine.wait_ge(self.sem, n)


def build(nc, t, out):
    from contextlib import ExitStack

    ctx = ExitStack()
    with ctx:
        base = (nc.sbuf_base + 63) // 64 * 64
        top = [base]

        def place(name, shape, dt=F32, at=None):
            size = 4 * int(np.prod(shape[1:]))
            if at is None:
                at = top[0]
                top[0] = at + (size + 31) // 32 * 32
            return nc.alloc_sbuf_tensor_at(name, shape, dt, offset=at)

        raw = place("raw", [P, 4, 4, CW])
        whi = place("whi", [P, 4, 2, CW], F32R)
        wlo = place("wlo", [P, 4, 2, CW], F32R)
        xres = place("xres", [P, TT, D])
        o_ybuf = top[0]
        ybuf = place("ybuf", [P, TT, D])
        o_h = top[0]
        hhi = place("hhi", [P, KT, TOK], F32R)
        hlo = place("hlo", [P, KT, TOK], F32R)
        o_r = top[0]
        place("region", [P, 64 * 256])
        MW = KT * 2 * META + P
        o_mhl = top[0]
        mhl = place("mhl", [P, MW], F32R)
        stg = place("stg", [P, TT, CW])
        start_c = place("start_c", [P, P + 56])
        ident, gcol = start_c[:, 0:P], start_c[:, P:P + 56]
        foldm = place("foldm", [2 * META, META])
        pbuf = place("pbuf", [P, 2, 2, KEYS])
        pt = place("pt", [P, 2, 3 * P])
        sm = place("sm", [P, ITEMS, 5])
        st = place("st", [P, 112])
        assert top[0] <= nc.sbuf_usable_end, (top[0], nc.sbuf_usable_end)
        xhi = place("xhi", [P, KT, KEYS], F32R, at=o_h)
        xlo = place("xlo", [P, KT, KEYS], F32R, at=o_h + 4 * KT * KEYS)
        o_1 = o_r + 2 * 4 * KT * META
        qtb = place("qtb", [P, B_HEADS, TOK], at=o_1)
        ktb = place("ktb", [P, B_HEADS, KEYS], at=o_1 + 8192)
        vb = place("vb", [P, TT, 1024], at=o_1 + 16896)
        vbm = place("vbm", [META, 1024], at=o_1 + 25088)
        qta = place("qta", [P, 8, TOK], at=o_1 + 29184)
        kta = place("kta", [P, 2, KEYS], at=o_1 + 37376)
        va = place("va", [P, TT, 256], at=o_1 + 39552)
        vam = place("vam", [META, 256], at=o_1 + 41600)
        rope = place("rope", [P, 10, P], at=o_1 + 42624)
        dist = place("dist", [P, TT, KEYS], at=o_1 + 47744)
        alibi = place("alibi", [P, 4, KEYS], at=o_1 + 49920)
        junk = place("junk", [P, P], at=o_1 + 54272)
        junk2 = place("junk2", [P, P], at=o_mhl)
        subg = place("subg", [P, P], at=o_1 + 54784)
        tmp = place("tmp", [P, TT, CW], at=o_1 + 55296)
        pbuf3 = place("pbuf3", [P, 2, KEYS], at=o_1 + 59392)
        rbc = place("rbc", [P, KEYS], at=o_1 + 61568)
        grow = place("grow", [P, D], at=o_h)
        yhi = place("yhi", [P, 8, TOK], F32R, at=o_1)
        ylo = place("ylo", [P, 8, TOK], F32R, at=o_1 + 8192)
        metax = place("metax", [META, D], at=o_ybuf)
        mtmp = place("mtmp", [P, KT, META], at=o_ybuf + 8704)
        msb = place("msb", [2 * META, CW], at=o_ybuf + 9728)
        stgm = place("stgm", [META, CW], at=o_ybuf + 11776)
        lamt = place("lamt", [P, 4, 64], at=o_ybuf + 13824)
        gq = place("gq", [P, 2, P], at=o_ybuf + 14848)
        q2t = place("q2t", [P, 8, TOK], at=o_r)
        k2t = place("k2t", [P, 8, TOK], at=o_r + 8192)
        v2 = place("v2", [P, TT, 1024], at=o_r + 16384)
        ya = place("ya", [P, TT, 1024], at=o_r + 24576)
        ut = place("ut", [P, 8, TOK], at=o_r + 32768)
        poolw = place("poolw", [P, 8, TOK], at=o_r + 40960)
        ahi = place("ahi", [P, 8, TOK], F32R, at=o_r + 32768)
        alo = place("alo", [P, 8, TOK], F32R, at=o_r + 40960)
        bhi = place("bhi", [P, 8, TOK], F32R, at=o_r + 49152)
        blo = place("blo", [P, 8, TOK], F32R, at=o_r + 57344)
        mhi = place("mhi", [P, KT, TOK], F32R, at=o_r)
        mlo = place("mlo", [P, KT, TOK], F32R, at=o_r + 16384)
        bias2 = place("bias2", [P, HEADS2, TOK], at=o_ybuf)
        wina = place("wina", [P, 2, TOK], at=o_mhl)
        winb = place("winb", [P, 2, TOK], at=o_r + 57344 + 6144)
        rbc2 = place("rbc2", [P, TOK], at=o_r + 57344)
        reltab = place("reltab", [HEADS2, REL], at=o_r + 32768)
        fhi = [place(f"fhi{i}", [P, 4, TOK], F32R, at=o_r + 49152 + 8192 * i) for i in range(2)]
        flo = [place(f"flo{i}", [P, 4, TOK], F32R, at=o_r + 53248 + 8192 * i) for i in range(2)]
        gfin = place("gfin", [P, D], at=o_r + 32768)
        fgate = place("fgate", [P, 4, TOK], at=o_ybuf)
        fprod = place("fprod", [P, 4, TOK], at=o_ybuf + 4096)
        rbc3 = place("rbc3", [P, TOK], at=o_ybuf + 10240)
        sqj = place("sqj", [P, CW], at=o_ybuf + 8192)
        outb = place("outb", [P, TT, D], at=o_r)
        invc = place("invc", [P, 4, 16], at=o_mhl + 2048)

        acc = [[ctx.enter_context(nc.psum_tensor(f"acc{p}{i}", [P, CW], F32)) for i in range(TT)] for p in range(2)]
        sbank = [ctx.enter_context(nc.psum_tensor(f"scores{i}", [P, CW], F32)) for i in range(2)]
        aux = [ctx.enter_context(nc.psum_tensor(f"aux{i}", [P, CW], F32)) for i in range(2)]

        def pslot(n):
            if n < ITEMS1 and n % 3 == 2:
                return pbuf3
            return pbuf[:, n % 3 if n < ITEMS1 else n % 2]

        ss = st[:, 0:3]
        nr1 = st[:, 4:6]
        lam = st[:, 6:7]
        lsum = st[:, 8:10]
        half = st[:, 12:32]
        rss = st[:, 32:60].rearrange("p (r h) -> p r h", h=4)
        ssy = st[:, 60:68].rearrange("p (i c) -> p i c", c=4)
        rp = st[:, 68:70]
        ssx = st[:, 70:78].rearrange("p (i c) -> p i c", c=4)
        r2 = st[:, 78:80]
        ssf = st[:, 82:90].rearrange("p (i c) -> p i c", c=4)
        r3 = st[:, 90:92]
        sso = st[:, 92:100].rearrange("p (i c) -> p i c", c=4)
        r4 = st[:, 100:102]

        def sem(name):
            return ctx.enter_context(nc.semaphore(name))

        raw_in = [sem(f"raw_in{u}") for u in range(4)]
        hi_ready, lo_ready, piece_used = sem("hi_ready"), sem("lo_ready"), sem("piece_used")
        stat_hi, stat_ready = sem("stat_hi"), sem("stat_ready")
        meta_scaled, meta_hi, meta_stat = sem("meta_scaled"), sem("meta_hi"), sem("meta_stat")
        aux_ready = sem("aux_ready")
        x_in = [sem(f"x_in{c}") for c in range(4)]
        meta_in, start_in, consts_in = sem("meta_in"), sem("start_in"), sem("consts_in")
        lam_in, grow_in, poolw_in, gfin_in = sem("lam_in"), sem("grow_in"), sem("poolw_in"), sem("gfin_in")
        rel_in, rel_out, bias2_in = sem("rel_in"), sem("rel_out"), sem("bias2_in")
        out_done = sem("out_done")
        squares1, var1, rstd1, nrstd1 = sem("squares1"), sem("var1"), sem("rstd1"), sem("nrstd1")
        rope_tables, mhl_zero, half_set, lam_sums, lam_exp, lam_ready = (
            sem("rope_tables"), sem("mhl_zero"), sem("half_set"), sem("lam_sums"), sem("lam_exp"), sem("lam_ready"))
        evicted = sem("evicted")
        turned = sem("turned")
        rbc_ready = sem("rbc_ready")
        meta_raw, meta_evicted = sem("meta_raw"), sem("meta_evicted")
        scores_ready, biased, negmax, exped, probs = sem("scores_ready"), sem("biased"), sem("negmax"), sem("exped"), sem("probs")
        pt_ready, osq, ovar, attended, y_scaled = sem("pt_ready"), sem("osq"), sem("ovar"), sem("attended"), sem("y_scaled")
        alibi_ready, rope_squares, roped = sem("alibi_ready"), sem("rope_squares"), sem("roped")
        qk_taken = sem("qk_taken")
        gate_parts, gated = sem("gate_parts"), sem("gated")
        ysq, post_scaled, yvar, yrstd, h1_ready, h1sq, h1var, h1rstd = (
            sem("ysq"), sem("post_scaled"), sem("yvar"), sem("yrstd"), sem("h1_ready"), sem("h1sq"), sem("h1var"),
            sem("h1rstd"))
        rel_fill, rel_filled, mask_set, pooled, gate_b, merged_a, merged = (
            sem("rel_fill"), sem("rel_filled"), sem("mask_set"), sem("pooled"), sem("gate_b"), sem("merged_a"),
            sem("merged"))
        h2_added, h2sq, h2var, h2rstd = sem("h2_added"), sem("h2sq"), sem("h2var"), sem("h2rstd")
        ff_out, ff_silu, ff_gate, ff_up = sem("ff_out"), sem("ff_silu"), sem("ff_gate"), sem("ff_up")
        down_added = sem("down_added")
        last_sq, last_var, last_rstd, out_ready = sem("last_sq"), sem("last_var"), sem("last_rstd"), sem("out_ready")
        out_gained, out_last = sem("out_gained"), sem("out_last")
        dve_steps, pool_steps, act_steps = sem("dve_steps"), sem("pool_steps"), sem("act_steps")

        block = ctx.enter_context(nc.Block())
        use = {}

        def block_taken(b):
            return (evicted, EVICTED[b]) if b in EVICTED else (turned, TURNED[b, 1])

        def taken_mix(b):
            if b < B_MIX:
                return block_taken(b)
            c, what = (b - B_MIX) // 3, (b - B_MIX) % 3
            return ((gate_b, c + 1), (merged_a, c + 1), (merged, c + 1))[what]

        def late(q, j, transpose_group, aux_bank, aux_used, pe):
            if q not in LATE or j != 4:
                return
            for s in (LATE[q], LATE[q] + 1):
                if s < G_ATT:
                    w = s - G_POOL
                    pe.wait_ge(pooled, w + 1)
                    pe.wait_ge(poolw_in, 32)
                    bank = aux_bank()
                    for e in range(2):
                        for k in range(2):
                            done = nc.tensor.matmul(bank[:, e * TOK:(e + 1) * TOK], poolw[:, 2 * w + k, e * P:(e + 1) * P],
                                                    ut[:, 2 * w + k, :], start=k == 0, stop=k == 1)
                    done.then_inc(aux_ready, 1)
                    aux_used(("stat", s), (stat_ready, s + 1))
                elif s < G_MERGED:
                    pe.wait_ge(attended, ITEMS)
                    transpose_group(s, ya, 2 * (s - G_ATT))
                elif s < G_H2:
                    pe.wait_ge(merged, (s - G_MERGED) // 2 + 1)
                    transpose_group(s, ybuf, 2 * (s - G_MERGED))
                else:
                    pe.wait_ge(h2_added, (s - G_H2) // 2 + 1)
                    transpose_group(s, xres, 2 * (s - G_H2))

        def stat_home(s):
            if s < G_Y:
                return xhi[:, 2 * s:2 * s + 2, 0:TOK], xlo[:, 2 * s:2 * s + 2, 0:TOK], 2 * s
            if s < G_H1:
                k = 2 * (s - G_Y)
                if k < 8:
                    return yhi[:, k:k + 2, :], ylo[:, k:k + 2, :], None
                return hhi[:, k:k + 2, :], hlo[:, k:k + 2, :], None
            if s < G_POOL:
                k = 2 * (s - G_H1)
                return hhi[:, k:k + 2, :], hlo[:, k:k + 2, :], 16 + k
            if s < G_ATT:
                k = 2 * (s - G_POOL)
                return bhi[:, k:k + 2, :], blo[:, k:k + 2, :], 48 + k
            if s < G_MERGED:
                k = 2 * (s - G_ATT)
                return ahi[:, k:k + 2, :], alo[:, k:k + 2, :], None
            if s < G_H2:
                k = 2 * (s - G_MERGED)
                return mhi[:, k:k + 2, :], mlo[:, k:k + 2, :], None
            k = 2 * (s - G_H2)
            return hhi[:, k:k + 2, :], hlo[:, k:k + 2, :], 32 + k

        def y_squares(act, b):
            act.wait_ge(piece_used, 8 * b + 8)
            c = b - Q_WOUT
            for i in range(TT):
                if c or i:
                    act.wait_ge(ysq, TT * c + i)
                nc.scalar.activation(tmp[:, 0, :], acc[b % 2][i][:], ACT.Square, accum_out=ssy[:, i, c:c + 1]).then_inc(ysq, 1)

        def evict2(act, prev, banks, pieces):
            act.wait_ge(piece_used, pieces)
            if prev == 4:
                act.wait_ge(h1rstd, 1)
            if prev == 8:
                act.wait_ge(biased, 32)
            for i in range(TT):
                if prev < 8:
                    done = nc.scalar.activation(v2[:, i, (prev - 4) * CW:(prev - 3) * CW], banks[i][:], ACT.Copy, scale=r2[:, i:i + 1])
                else:
                    done = nc.scalar.activation(ybuf[:, i, (prev - 8) * CW:(prev - 7) * CW], banks[i][:], ACT.Sigmoid, scale=r2[:, i:i + 1])
            done.then_inc(evicted, 1)

        def branch_a(dve, c):
            dve.wait_ge(piece_used, 8 * (Q_MIX + 2 * c + 1) + 4)
            dve.wait_ge(evicted, EVICTED[Q_W2 + 11])
            for i in range(TT):
                y = ybuf[:, i, c * CW:(c + 1) * CW]
                done = nc.vector.tensor_tensor(y, acc[(B_MIX + 3 * c + 1) % 2][i][:], y, ALU.mult)
            done.then_inc(merged_a, 1)

        def branch_b(dve, chain, c):
            dve.wait_ge(piece_used, 8 * (Q_MIX + 2 * c + 2))
            dve.wait_ge(gate_b, c + 1)
            dve.wait_ge(merged_a, c + 1)
            for i in range(TT):
                s = chain.step(nc.vector.tensor_tensor(stg[:, i, :], acc[(B_MIX + 3 * c + 2) % 2][i][:], stg[:, i, :], ALU.mult))
            chain.after(s)
            y = ybuf[:, :, c * CW:(c + 1) * CW]
            nc.vector.tensor_tensor(y, y, stg[:], ALU.add).then_inc(merged, 1)

        @block.tensor
        def _(pe):
            uses = [0]
            free_at = [None, None]

            def aux_bank():
                b = uses[0] % 2
                if free_at[b] is not None:
                    pe.wait_ge(*free_at[b])
                return aux[b]

            def aux_used(name, free):
                free_at[uses[0] % 2] = free
                use[name] = uses[0] + 1
                uses[0] += 1

            def piece(g, slot, first, last, banks, stat, kt0, meta=None):
                for k in range(2):
                    start, stop = first and k == 0, last and k == 1
                    hi, lo = whi[:, slot, k, :], wlo[:, slot, k, :]
                    for i in range(TT):
                        sh, sl = stat(kt0 + k, i)
                        nc.tensor.matmul(banks[i][:], sh, hi, start=start, stop=False)
                        nc.tensor.matmul(banks[i][:], sh, lo, start=False, stop=False)
                        done = nc.tensor.matmul(banks[i][:], sl, hi, start=False, stop=stop)
                    if meta is not None:
                        m = mhl[:, (kt0 + k) * 2 * META:(kt0 + k) * 2 * META + P]
                        nc.tensor.matmul(meta[:], m, hi, start=start, stop=False)
                        done = nc.tensor.matmul(meta[:], m, lo, start=False, stop=stop)
                done.then_inc(piece_used, 1)

            def piece_turned(j, banks, hi_of, lo_of):
                for k in range(2):
                    kt = 2 * j + k
                    for c in range(4):
                        o = banks[c // 2][:, c % 2 * TOK:(c % 2 + 1) * TOK]
                        hi, lo = (w[:, j % 4, k, c * P:(c + 1) * P] for w in (whi, wlo))
                        nc.tensor.matmul(o, hi, hi_of[:, kt, 0:TOK], start=kt == 0 and c % 2 == 0, stop=False)
                        nc.tensor.matmul(o, hi, lo_of[:, kt, 0:TOK], start=False, stop=False)
                        done = nc.tensor.matmul(o, lo, hi_of[:, kt, 0:TOK], start=False, stop=kt == KT - 1 and c % 2 == 1)
                done.then_inc(piece_used, 1)

            def piece_kb(j):
                banks = acc[1 - j // 4]
                for k in range(4):
                    kt = 4 * (j % 4) + k
                    for h in range(2):
                        at = 256 * (k % 2) + h * P
                        hi, lo = (w[:, j % 4, k // 2, at:at + P] for w in (whi, wlo))
                        o = banks[h][:, 0:KEYS]
                        nc.tensor.matmul(o, hi, xhi[:, kt, :], start=kt == 0, stop=False)
                        nc.tensor.matmul(o, hi, xlo[:, kt, :], start=False, stop=False)
                        done = nc.tensor.matmul(o, lo, xhi[:, kt, :], start=False, stop=kt == KT - 1)
                done.then_inc(piece_used, 1)

            def broadcast_r(r, name, meta=False):
                bank = aux_bank()
                for i in range(TT):
                    done = nc.tensor.matmul(bank[:, i * P:(i + 1) * P], dims(r[:, i:i + 1], [0, P]), ident, start=True, stop=True)
                if meta:
                    done = nc.tensor.matmul(bank[:, TOK:KEYS], dims(r[0:META, 2:3], [0, P]), ident[0:META, 0:META], start=True, stop=True)
                done.then_inc(aux_ready, 1)
                aux_used(name, (rbc_ready, {"rbc": 1, "rbc2": 2, "rbc3": 3}[name]))

            def x_stat(kt, i):
                return xhi[:, kt, i * P:(i + 1) * P], xlo[:, kt, i * P:(i + 1) * P]

            def h_stat(kt, i):
                return hhi[:, kt, i * P:(i + 1) * P], hlo[:, kt, i * P:(i + 1) * P]

            def y_stat(kt, i):
                hi, lo = (yhi, ylo) if kt < 8 else (hhi, hlo)
                return hi[:, kt, i * P:(i + 1) * P], lo[:, kt, i * P:(i + 1) * P]

            def m_stat(kt, i):
                return mhi[:, kt, i * P:(i + 1) * P], mlo[:, kt, i * P:(i + 1) * P]

            def a_stat(kt, i):
                return ahi[:, kt, i * P:(i + 1) * P], alo[:, kt, i * P:(i + 1) * P]

            def b_stat(kt, i):
                return bhi[:, kt, i * P:(i + 1) * P], blo[:, kt, i * P:(i + 1) * P]

            def transpose_group(s, src, kt):
                bank = aux_bank()
                for k in range(2):
                    for i in range(TT):
                        done = nc.tensor.transpose(bank[:, k * TOK + i * P:k * TOK + (i + 1) * P],
                                                   src[:, i, (kt + k) * P:(kt + k + 1) * P], ident)
                done.then_inc(aux_ready, 1)
                aux_used(("stat", s), (stat_ready, s + 1))

            def scores(n):
                if n in (0, 8):
                    pe.wait_ge(turned, TURNED[(2, 6)[n // 8], 1])
                if n in (ITEMS1, ITEMS1 + 8):
                    pe.wait_ge(turned, TURNED[Q_W2 + 2 + (n - ITEMS1) // 8, 1])
                if n == 0:
                    pe.wait_ge(meta_raw, len(W1_META))
                else:
                    pe.wait_ge(*((exped, n) if is_a(n - 1) else (biased, n if n <= 16 else n - 8)))
                if is_b(n):
                    h, i = n // 2, n % 2
                    for m in range(2):
                        done = nc.tensor.matmul(sbank[m][:, 0:KEYS], qtb[64 * m:64 * m + 64, h, i * P:(i + 1) * P],
                                                ktb[64 * m:64 * m + 64, h, :], start=True, stop=True)
                elif is_a(n):
                    h = n - 16
                    for i in range(TT):
                        done = nc.tensor.matmul(sbank[i][:, 0:KEYS], qta[:, h, i * P:(i + 1) * P],
                                                kta[:, h // 4, :], start=True, stop=True)
                else:
                    h = n - ITEMS1
                    r = slice(64 * (h % 2), 64 * (h % 2) + 64)
                    for i in range(TT):
                        keys = P * (i + 1)
                        done = nc.tensor.matmul(sbank[i][:, 0:keys], q2t[r, h // 2, i * P:(i + 1) * P],
                                                k2t[r, h // 2, 0:keys], start=True, stop=True)
                done.then_inc(scores_ready, 1)

            def transpose_probs(n):
                pe.wait_ge(*((probs, n + 1) if is_b(n) else (exped, n + 1)))
                if n < ITEMS1:
                    for i in range(1 if is_b(n) else 2):
                        bank = aux_bank()
                        p = pslot(n)[:, i, :]
                        for k in range(2):
                            nc.tensor.transpose(bank[:, k * P:(k + 1) * P], p[:, k * P:(k + 1) * P], ident)
                        nc.tensor.transpose(bank[0:META, TOK:TOK + P], p[:, TOK:KEYS], ident).then_inc(aux_ready, 1)
                        aux_used(("pt", n, i), (pt_ready, n + 1))
                else:
                    bank = aux_bank()
                    nc.tensor.transpose(bank[:, 0:P], pslot(n)[:, 0, 0:P], ident)
                    for k in range(2):
                        done = nc.tensor.transpose(bank[:, (k + 1) * P:(k + 2) * P], pslot(n)[:, 1, k * P:(k + 1) * P], ident)
                    done.then_inc(aux_ready, 1)
                    aux_used(("pt", n, 0), (pt_ready, n + 1))

            def attend(n):
                bank = aux_bank()
                pe.wait_ge(pt_ready, n + 1)
                if n < ITEMS1:
                    h = n // 2 if is_b(n) else (n - 16) // 4
                    v, vm = (vb, vbm) if is_b(n) else (va, vam)
                    c = slice(h * HD, (h + 1) * HD)
                    for i in range(1 if is_b(n) else 2):
                        o, w = bank[:, i * HD:(i + 1) * HD], pt[:, i, :]
                        for k in range(2):
                            nc.tensor.matmul(o, w[:, k * P:(k + 1) * P], v[:, k, c], start=k == 0, stop=False)
                        done = nc.tensor.matmul(o, w[0:META, TOK:TOK + P], vm[0:META, c], start=False, stop=True)
                else:
                    c = slice((n - ITEMS1) * 64, (n - ITEMS1 + 1) * 64)
                    nc.tensor.matmul(bank[:, 0:64], pt[:, 0, 0:P], v2[:, 0, c], start=True, stop=True)
                    nc.tensor.matmul(bank[:, 64:128], pt[:, 0, P:2 * P], v2[:, 0, c], start=True, stop=False)
                    done = nc.tensor.matmul(bank[:, 64:128], pt[:, 0, 2 * P:3 * P], v2[:, 1, c], start=False, stop=True)
                done.then_inc(aux_ready, 1)
                aux_used(("o", n), (attended, n + 1))

            def attention(g):
                n = item_at(g, 5, 4)
                if n is not None:
                    transpose_probs(n)
                n = item_at(g, 0)
                if n is not None:
                    scores(n)
                n = item_at(g, 6, 5)
                if n is not None:
                    attend(n)

            taken = [0]

            def transpose_heads(name, tiles):
                bank = aux_bank()
                at = 0
                for tile, rows in tiles:
                    done = nc.tensor.transpose(bank[:, at:at + rows], tile, ident[0:rows, 0:rows])
                    at += rows
                done.then_inc(aux_ready, 1)
                taken[0] += 1
                aux_used(name, (qk_taken, taken[0]))

            def head_pair(name, c):
                transpose_heads(name, [(stg[:, i, (c + k) * P:(c + k + 1) * P], P) for k in range(2) for i in range(TT)])

            pe.wait_ge(mhl_zero, 1)
            for _ in range(8):
                nc.tensor.matmul(acc[1][0][:], mhl[:, 0:P], mhl[:, 0:CW], start=True, stop=True)
            pe.wait_ge(start_in, 16)
            for s in range(2):
                pe.wait_ge(x_in[0], 16)
                transpose_group(G_X + s, xres, 2 * s)

            for _ in range(8):
                nc.tensor.matmul(acc[1][0][:], mhl[:, 0:P], mhl[:, 0:CW], start=True, stop=True)

            def meta_transposes():
                pe.wait_ge(meta_in, 16)
                bank = aux_bank()
                for kt in range(KT):
                    done = nc.tensor.transpose(bank[:, kt * META:(kt + 1) * META], metax[:, kt * P:(kt + 1) * P],
                                               ident[0:META, 0:META])
                done.then_inc(aux_ready, 1)
                aux_used("meta", (meta_scaled, 1))

            for b in range(Q_WOUT):
                for j in range(8):
                    g = 8 * b + j
                    attention(g)
                    if b == 0 and j in (1, 2, 4):
                        pe.wait_ge(x_in[j // 2 + 1], 16)
                        for s in (j // 2 * 2 + 2, j // 2 * 2 + 3):
                            transpose_group(G_X + s, xres, 2 * s)
                    if b == 0 and j == 6:
                        meta_transposes()
                    if b == Q_WOUT - 1 and j in (1, 2, 6):
                        k = (1, 2, 6).index(j)
                        pe.wait_ge(attended, (20, 20, 22)[k])
                        transpose_group(G_Y + k, ybuf, 2 * k)
                    prev = b - 1
                    if prev in W1_META and j == 2:
                        m = W1_META.index(prev)
                        pe.wait_ge(meta_raw, m + 1)
                        if m == 0:
                            pe.wait_ge(consts_in, 96)
                        nc.tensor.matmul(aux_bank()[0:META, :], foldm[:], msb[:], start=True, stop=True).then_inc(aux_ready, 1)
                        aux_used(("fold", m), (meta_evicted, m + 1))
                    what = W1[prev][0] if b else None
                    if b == 1 and j == 1:
                        pe.wait_ge(rstd1, 1)
                        broadcast_r(ss, "rbc", meta=True)
                    if what == "kva" and j == 6:
                        pe.wait_ge(roped, 3)
                        head_pair(("ka", 0), 0)
                        transpose_heads(("kam", 0), [(stgm[:, k * P:(k + 1) * P], META) for k in range(2)])
                    if what == "qa" and j == 7:
                        pe.wait_ge(roped, 3 + 2 * (prev - 6))
                        head_pair(("t", prev, 0), 0)
                    if b >= 2 and W1[b - 2][0] == "qa" and j == 0:
                        head_pair(("t", b - 2, 1), 2)
                    if b == 0:
                        pe.wait_ge(stat_ready, G_X + j + 1)
                    if is_kb(b):
                        if (b, j) == (1, 0):
                            pe.wait_ge(meta_stat, 1)
                        if (b, j) in ((1, 4), (2, 0), (2, 4)):
                            pe.wait_ge(turned, {(1, 4): TURNED[0, 1], (2, 0): TURNED[1, 0], (2, 4): TURNED[1, 1]}[b, j])
                    elif j == 0 and b in (3, 4):
                        pe.wait_ge(turned, TURNED[2, b - 3])
                    elif j == 0 and b > 4:
                        pe.wait_ge(*block_taken(b - 2))
                    if j == 0 and b in W1_META:
                        m = W1_META.index(b)
                        if m >= 2:
                            pe.wait_ge(meta_raw, m - 1)
                    pe.wait_ge(lo_ready, g + 1)
                    if is_kb(b):
                        piece_kb(j)
                    elif (b, 1) in TURNED:
                        piece_turned(j, acc[b % 2], xhi, xlo)
                    else:
                        piece(g, g % 4, j == 0, j == 7, acc[b % 2], x_stat, 2 * j,
                              meta=sbank[W1_META.index(b) % 2] if b in W1_META else None)

            def y_group(s):
                if s == G_Y + 3:
                    pe.wait_ge(attended, ITEMS1)
                elif s > G_Y + 3:
                    pe.wait_ge(gated, 3 + (s - G_Y) // 6)
                transpose_group(s, ybuf, 2 * (s - G_Y))

            for c in range(4):
                b = Q_WOUT + c
                for j in range(8):
                    g = 8 * b + j
                    if c == 0 and j in (0, 1, 5):
                        for s in {0: (3, 4), 1: (5,), 5: (6, 7)}[j]:
                            y_group(G_Y + s)
                    if c == 0:
                        pe.wait_ge(stat_ready, G_Y + j + 1)
                    if j == 0:
                        pe.wait_ge(*(block_taken(b - 2) if b - 2 < Q_WOUT else (post_scaled, b - 2 - Q_WOUT + 1)))
                    pe.wait_ge(lo_ready, g + 1)
                    piece(g, g % 4, j == 0, j == 7, acc[b % 2], y_stat, 2 * j)

            def h1_chunk(s):
                pe.wait_ge(h1_ready, 2 * ((s - G_H1) // 2 + 1))

            for s in range(G_H1, G_H1 + 2):
                h1_chunk(s)
                transpose_group(s, xres, 2 * (s - G_H1))
            for c in range(12):
                b = B_W2 + c
                for j in range(8):
                    g = 8 * b + j
                    attention(g)
                    prev = c - 1
                    if c == 0 and 1 <= j < 7:
                        h1_chunk(G_H1 + j + 1)
                        transpose_group(G_H1 + j + 1, xres, 2 * (j + 1))
                    if c == 1 and j == 1:
                        pe.wait_ge(h1rstd, 1)
                        broadcast_r(r2, "rbc2")
                    late(b, j, transpose_group, aux_bank, aux_used, pe)
                    if c == 0:
                        pe.wait_ge(stat_ready, G_H1 + j + 1)
                    if j == 0:
                        pe.wait_ge(*((post_scaled, b - 2 - Q_WOUT + 1) if c < 2 else block_taken(b - 2)))
                    pe.wait_ge(lo_ready, g + 1)
                    if (b, 1) in TURNED:
                        piece_turned(j, acc[b % 2], hhi, hlo)
                    else:
                        piece(g, g % 4, j == 0, j == 7, acc[b % 2], h_stat, 2 * j)

            for c in range(4):
                for half_q in range(2):
                    q = Q_MIX + 2 * c + half_q
                    for j in range(8):
                        g = 8 * q + j
                        late(q, j, transpose_group, aux_bank, aux_used, pe)
                        b = B_MIX + 3 * c + (0 if half_q == 0 else 1 + j // 4)
                        if j == 0 or (half_q == 1 and j == 4):
                            pe.wait_ge(*taken_mix(b - 2))
                        pe.wait_ge(lo_ready, g + 1)
                        if half_q == 0:
                            piece(g, g % 4, j == 0, j == 7, acc[b % 2], h_stat, 2 * j)
                        else:
                            if c == 0 and j == 0:
                                pe.wait_ge(stat_ready, G_ATT + 4)
                            piece(g, g % 4, j % 4 == 0, j % 4 == 3, acc[b % 2], a_stat if j < 4 else b_stat, 2 * (j % 4))

            for c in range(4):
                q, b = Q_WO2 + c, B_WO2 + c
                for j in range(8):
                    g = 8 * q + j
                    late(q, j, transpose_group, aux_bank, aux_used, pe)
                    if c == 0 and j % 2 == 0:
                        pe.wait_ge(stat_ready, G_MERGED + j + 2)
                    if j == 0:
                        pe.wait_ge(*(taken_mix(b - 2) if c < 2 else (h2_added, c - 1)))
                    pe.wait_ge(lo_ready, g + 1)
                    piece(g, g % 4, j == 0, j == 7, acc[b % 2], m_stat, 2 * j)

            for c in range(3):
                q, b = Q_FF + c, B_FF + c
                for j in range(8):
                    g = 8 * q + j
                    late(q, j, transpose_group, aux_bank, aux_used, pe)
                    if c == 0 and j % 2 == 0:
                        pe.wait_ge(stat_ready, G_H2 + j + 2)
                    if c == 1 and j == 2:
                        pe.wait_ge(h2rstd, 1)
                        broadcast_r(r3, "rbc3")
                    if j == 0:
                        pe.wait_ge(*((h2_added, c + 3) if c < 2 else (ff_out, 1)))
                    pe.wait_ge(lo_ready, g + 1)
                    piece_turned(j, acc[b % 2], hhi, hlo)

            def f_stat(buf):
                return lambda kt, i: (fhi[buf][:, kt, i * P:(i + 1) * P], flo[buf][:, kt, i * P:(i + 1) * P])

            with pe.Fori(0, LOOPS) as i:
                g0 = 8 * Q_LOOP + 24 * i
                for j in range(8):
                    m = j // 2
                    if j == 0:
                        pe.wait_ge(stat_ready, G_FF + i + 1)
                        pe.wait_ge(ff_up, i + 1)
                    if j == 2:
                        pe.wait_ge(ff_out, i + 2)
                    if j in (4, 6):
                        pe.wait_ge(down_added, 4 * i + m - 1)
                    pe.wait_ge(lo_ready, g0 + j + 1)
                    piece(None, j % 4, j % 2 == 0, j % 2 == 1, acc[m % 2], f_stat(0), 2 * (j % 2))
                for j in range(8):
                    if j == 0:
                        pe.wait_ge(down_added, 4 * i + 3)
                    pe.wait_ge(lo_ready, g0 + 8 + j + 1)
                    piece_turned(j, acc[0], hhi, hlo)
                for j in range(8):
                    if j == 0:
                        pe.wait_ge(down_added, 4 * i + 4)
                    pe.wait_ge(lo_ready, g0 + 16 + j + 1)
                    piece_turned(j, acc[1], hhi, hlo)

            last = FF_CHUNKS - 1
            for j in range(8):
                if j == 0:
                    pe.wait_ge(ff_up, last)
                pe.wait_ge(lo_ready, 8 * Q_TAIL + j + 1)
                piece_turned(j, acc[0], hhi, hlo)
            for j in range(8):
                m = j // 2
                if j == 0:
                    pe.wait_ge(ff_out, last + 1)
                if j == 2:
                    pe.wait_ge(ff_up, last + 1)
                if j in (4, 6):
                    pe.wait_ge(down_added, 4 * (last - 1) + m - 1)
                pe.wait_ge(lo_ready, 8 * (Q_TAIL + 1) + j + 1)
                piece(None, j % 4, j % 2 == 0, j % 2 == 1, acc[(m + 1) % 2], f_stat(0), 2 * (j % 2))
            for j in range(8):
                m = j // 2
                if j == 0:
                    pe.wait_ge(stat_ready, G_FF + last + 1)
                if j % 2 == 0:
                    pe.wait_ge(down_added, 4 * last + m - 1)
                pe.wait_ge(lo_ready, 8 * (Q_TAIL + 2) + j + 1)
                piece(None, j % 4, j % 2 == 0, j % 2 == 1, acc[(m + 1) % 2], f_stat(1), 2 * (j % 2))

        @block.sync
        def _(sp):
            def rows(ap, n):
                return bass.AP(tensor=ap.tensor, offset=0, ap=[[0, P], [1, n]])

            def quad(q, srcs):
                for u in range(4):
                    sp.wait_ge(lo_ready, 8 * (q - 1) + 2 * u + 2)
                    sp.dma_start(raw[:, u], srcs[u].rearrange("(k p) n -> p k n", p=P)).then_inc(raw_in[u], 16)

            def column_block(w, c0):
                return [w[u * CW:(u + 1) * CW, bass.ds(c0, CW)] for u in range(4)]

            def row_block(w, r0):
                return [w[bass.ds(r0, CW), u * CW:(u + 1) * CW] for u in range(4)]

            w1, w2, wgu, wdn = t["w_in"][0], t["w_in_2"][0], t["w_gate_up_2"][0], t["w_down_2"][0]
            sp.dma_start(start_c[:], t["start_c"]).then_inc(start_in, 16)
            first = column_block(w1, W1[0][2] * CW)
            xs = t["x"][0].rearrange("(i p) d -> p i d", p=P)
            for u in range(4):
                sp.dma_start(xres[:, :, u * CW:(u + 1) * CW], xs[:, :, u * CW:(u + 1) * CW]).then_inc(x_in[u], 16)
                sp.dma_start(raw[:, u], first[u].rearrange("(k p) n -> p k n", p=P)).then_inc(raw_in[u], 16)
            for name, dst in (("rope_t", rope[:]), ("dist_t", dist[:]), ("fold_t", foldm[:])):
                sp.dma_start(dst, t[name]).then_inc(consts_in, 16)
            sp.dma_start(gq[:, 0, :], rows(t["q_norm_g"], P)).then_inc(consts_in, 16)
            sp.dma_start(gq[:, 1, :], rows(t["k_norm_g"], P)).then_inc(consts_in, 16)
            sp.dma_start(subg[:], rows(t["subln_g"], P)).then_inc(consts_in, 16)
            for n, name in enumerate(("lambda_q1", "lambda_k1", "lambda_q2", "lambda_k2")):
                sp.dma_start(lamt[:, n, :], rows(t[name], 64)).then_inc(lam_in, 16)
            for q in range(1, Q_WOUT):
                c0 = W1[q][2] * CW
                if not is_kb(q):
                    quad(q, column_block(w1, c0))
                    continue
                for u in range(4):
                    sp.wait_ge(lo_ready, 8 * (q - 1) + 2 * u + 2)
                    src = w1[u % 2 * 1024:(u % 2 + 1) * 1024, c0 + u // 2 * 256:c0 + (u // 2 + 1) * 256]
                    sp.dma_start(raw[:, u].rearrange("p a (b n) -> p (a b) n", n=256),
                                 src.rearrange("(k p) n -> p k n", p=P)).then_inc(raw_in[u], 16)
            for c in range(4):
                quad(Q_WOUT + c, column_block(t["w_out"][0], c * CW))
            for c in range(12):
                quad(Q_W2 + c, column_block(w2, c * CW))
                if c == 1:
                    sp.wait_ge(stat_ready, G_Y + 8)
                    sp.dma_start(invc[:], t["invc_t"]).then_inc(poolw_in, 16)
                    sp.dma_start(poolw[:], t["pool_w_2"][0].rearrange("g (k p) e -> p (g k) e", p=P)).then_inc(poolw_in, 16)
            for c in range(4):
                quad(Q_MIX + 2 * c, column_block(w2, (12 + c) * CW))
                wa, wb = t["w_branch_a_2"][0], t["w_branch_b_2"][0]
                cs = slice(c * CW, (c + 1) * CW)
                quad(Q_MIX + 2 * c + 1, [wa[0:CW, cs], wa[CW:2 * CW, cs], wb[0:CW, cs], wb[CW:2 * CW, cs]])
            for c in range(4):
                quad(Q_WO2 + c, column_block(t["w_out_2"][0], c * CW))
            quad(Q_FF, column_block(wgu, 0))
            quad(Q_FF + 1, column_block(wgu, DFF))
            quad(Q_FF + 2, column_block(wgu, CW))
            sp.wait_ge(merged, 4)
            sp.dma_start(gfin[:], rows(t["norm_final_2"], D)).then_inc(gfin_in, 16)
            with sp.Fori(0, LOOPS) as i:
                quad(Q_LOOP + 3 * i, row_block(wdn, i * CW))
                quad(Q_LOOP + 1 + 3 * i, column_block(wgu, DFF + (i + 1) * CW))
                quad(Q_LOOP + 2 + 3 * i, column_block(wgu, (i + 2) * CW))
            quad(Q_TAIL, column_block(wgu, DFF + 10 * CW))
            quad(Q_TAIL + 1, row_block(wdn, 9 * CW))
            quad(Q_TAIL + 2, row_block(wdn, 10 * CW))
            for n, (i, c) in enumerate(((0, 0), (0, 1), (1, 0))):
                cs = slice(c * 1024, (c + 1) * 1024)
                sp.wait_ge(out_ready, n + 1)
                sp.dma_start(out[0, i * P:(i + 1) * P, cs], outb[:, i, cs]).then_inc(out_done, 16)
            sp.wait_ge(out_done, 16 * 4)

        @block.scalar
        def _(act):
            chain = Chain(act, act_steps)

            def split(q, j):
                g = 8 * q + j
                if j % 2 == 0:
                    act.wait_ge(raw_in[j // 2], 16 * (q + 1))
                if not isinstance(g, int) or g >= 4:
                    act.wait_ge(piece_used, g - 3)
                nc.scalar.activation(whi[:, j % 4], raw[:, j // 2, 2 * (j % 2):2 * (j % 2) + 2, :], ACT.Copy).then_inc(hi_ready, 1)

            def stat_group(s):
                hi, _, g = stat_home(s)
                act.wait_ge(aux_ready, use["stat", s])
                bank = aux[(use["stat", s] - 1) % 2]
                if g is None:
                    nc.scalar.activation(hi, bank[:], ACT.Copy).then_inc(stat_hi, 1)
                else:
                    nc.scalar.activation(hi[:, 0, :], bank[:, 0:TOK], ACT.Copy, scale=gcol[:, g:g + 1])
                    nc.scalar.activation(hi[:, 1, :], bank[:, TOK:CW], ACT.Copy, scale=gcol[:, g + 1:g + 2]).then_inc(stat_hi, 1)

            def attention_early(g):
                n = item_at(g, 7, 6)
                if n is not None:
                    for i in range(2 if is_a(n) else 1):
                        act.wait_ge(aux_ready, use["pt", n, i])
                        bank = aux[(use["pt", n, i] - 1) % 2]
                        if n < ITEMS1:
                            nc.scalar.activation(pt[:, i, 0:TOK], bank[:, 0:TOK], ACT.Copy)
                            done = nc.scalar.activation(pt[0:META, i, TOK:TOK + P], bank[0:META, TOK:TOK + P], ACT.Copy)
                        else:
                            done = nc.scalar.activation(pt[:, 0, :], bank[:, 0:3 * P], ACT.Copy)
                    done.then_inc(pt_ready, 1)
                n = item_at(g, 8)
                if n is not None and is_b(n):
                    act.wait_ge(aux_ready, use["o", n])
                    nc.scalar.activation(junk2[:], aux[(use["o", n] - 1) % 2][:, 0:HD], ACT.Square,
                                         accum_out=sm[:, n, 4:5]).then_inc(osq, 1)

            def attention(g):
                b, a = item_at(g, 4, 3), item_at(g, 3)
                n = a if a is not None and is_a(a) else b if b is not None and not is_a(b) else None
                if n is not None:
                    act.wait_ge(negmax, n + 1)
                    for i in range(2):
                        keys = KEYS if n < ITEMS1 else P * (i + 1)
                        e = pslot(n)[:, i, 0:keys]
                        done = nc.scalar.activation(e, sbank[i][:, 0:KEYS] if is_a(n) else e, ACT.Exp,
                                                    bias=sm[:, n, i:i + 1], scale=SCALE_A if is_a(n) else 1.0,
                                                    accum_out=sm[:, n, 2 + i:3 + i])
                    done.then_inc(exped, 1)

            act.wait_ge(half_set, 1)
            nc.scalar.activation(sm[:, 0, :], half[:, 0:5], ACT.Exp)
            act.dma_start(metax[:], t["meta_tokens"]).then_inc(meta_in, 16)
            mview = mhl[:, 0:KT * 2 * META].rearrange("p (k m) -> p k m", m=2 * META)
            act.wait_ge(start_in, 16)
            stat_group(G_X)

            def meta_hi_part():
                mview = mhl[:, 0:KT * 2 * META].rearrange("p (k m) -> p k m", m=2 * META)
                act.wait_ge(meta_scaled, 1)
                act.wait_ge(mhl_zero, 1)
                nc.scalar.activation(mview[:, :, 0:META], mtmp[:], ACT.Copy)
                nc.scalar.activation(xhi[:, :, TOK:KEYS], mtmp[:], ACT.Copy).then_inc(meta_hi, 1)

            def block1_side(b, j):
                prev = b - 1
                if j == 2 and prev in EVICTED:
                    act.wait_ge(piece_used, 8 * b)
                    if prev == 3:
                        act.wait_ge(rstd1, 1)
                        act.wait_ge(nrstd1, 1)
                    if prev in W1_META:
                        m = W1_META.index(prev)
                        if m:
                            act.wait_ge(meta_evicted, m)
                        nc.scalar.activation(msb[:], sbank[m % 2][0:2 * META, :], ACT.Copy).then_inc(meta_raw, 1)
                    what, part = W1[prev][:2]
                    cs = slice(part * CW, (part + 1) * CW)
                    if what in ("ga", "gb"):
                        act.wait_ge(*((roped, 7) if (what, part) == ("ga", 0) else (gated, prev - 9)))
                    for i in range(TT):
                        src, r = acc[prev % 2][i], ss[:, i:i + 1]
                        if what == "kva":
                            nc.scalar.activation(va[:, i, :], src[:, 256:512], ACT.Copy, scale=r)
                            done = nc.scalar.activation(stg[:, i, 0:256], src[:, 0:256], ACT.Copy, scale=r)
                        elif what == "vb":
                            done = nc.scalar.activation(vb[:, i, cs], src[:], ACT.Copy, scale=r)
                        elif what == "gb":
                            done = nc.scalar.activation(stg[:, i, :], src[:], ACT.Silu, scale=r)
                        else:
                            if what == "ga":
                                nc.scalar.activation(tmp[:, i, :], src[:], ACT.Exp, scale=nr1[:, i:i + 1])
                            done = nc.scalar.activation(stg[:, i, :], src[:], ACT.Copy, scale=r)
                    done.then_inc(evicted, 1)
                if prev in W1_META and j == 4:
                    m = W1_META.index(prev)
                    act.wait_ge(aux_ready, use["fold", m])
                    bank, r = aux[(use["fold", m] - 1) % 2], ss[0:META, 2:3]
                    what, part = W1[prev][:2]
                    if what == "kva":
                        nc.scalar.activation(vam[:], bank[0:META, 256:512], ACT.Copy, scale=r)
                        done = nc.scalar.activation(stgm[:, 0:256], bank[0:META, 0:256], ACT.Copy, scale=r)
                    elif what == "vb":
                        done = nc.scalar.activation(vbm[:, part * CW:(part + 1) * CW], bank[0:META, :], ACT.Copy, scale=r)
                    else:
                        done = nc.scalar.activation(stgm[:], bank[0:META, :], ACT.Copy, scale=r)
                    done.then_inc(meta_evicted, 1)

            def rope_sums(r, src, rows, heads):
                for h in range(heads):
                    done = nc.scalar.activation(junk[0:rows, :], src[:, h * HD:(h + 1) * HD], ACT.Square, accum_out=rss[0:rows, r, h:h + 1])
                    if h < heads - 1:
                        chain.after(chain.step(done))
                done.then_inc(rope_squares, 1)
                act.wait_ge(rope_squares, r + 1)

            def block1_rope(b, j):
                prev = b - 1
                if W1[prev][0] == "kva" and j == 3:
                    act.wait_ge(evicted, EVICTED[prev])
                    for i in range(TT):
                        rope_sums(i, stg[:, i, 0:256], P, 2)
                if W1[prev][0] == "kva" and j == 4:
                    act.wait_ge(meta_evicted, W1_META.index(prev) + 1)
                    rope_sums(2, stgm[:, 0:256], META, 2)
                if W1[prev][0] == "qa" and j in (3, 4):
                    act.wait_ge(evicted, EVICTED[prev])
                    rope_sums(3 + 2 * (prev - 7) + j - 3, stg[:, j - 3, :], P, 4)

            def take(name, dst, width, done=None):
                act.wait_ge(aux_ready, use[name])
                nc.scalar.activation(dst, aux[(use[name] - 1) % 2][:, 0:width], ACT.Copy).then_inc(done or qk_taken, 1)

            def block1_take(b, j):
                prev = b - 1
                if W1[prev][0] == "kva" and j == 7:
                    take(("ka", 0), kta[:, :, 0:TOK], CW)
                    take(("kam", 0), kta[:, :, TOK:KEYS], 2 * META)

            def block1_take_late(b, j):
                if b >= 2 and W1[b - 2][0] == "qa" and j in (1, 2):
                    h = 4 * (b - 9) + 2 * (j - 1)
                    take(("t", b - 2, j - 1), qta[:, h:h + 2, :], CW)

            for b in range(Q_WOUT):
                for j in range(8):
                    if b == Q_WOUT - 1 and j in (4, 5):
                        stat_group(G_Y + j - 4)
                    split(b, j)
                    attention_early(8 * b + j)
                    if b == 0 and j == 0:
                        stat_group(G_X + 1)
                    if b == 0 and j in (1, 3, 5):
                        stat_group(G_X + j + 1)
                        stat_group(G_X + j + 2)
                    if b == 0 and j == 7:
                        meta_hi_part()
                    if b == 0 and j in (5, 6, 7):
                        i = j - 5
                        if i < TT:
                            nc.scalar.activation((qtb, qta)[i][:].rearrange("p a b -> p (a b)"), xres[:, i, :], ACT.Square, accum_out=ss[:, i:i + 1]).then_inc(squares1, 1)
                        else:
                            nc.scalar.activation(vb[0:META].rearrange("p a b -> p (a b)"), metax[:], ACT.Square, accum_out=ss[0:META, 2:3]).then_inc(squares1, 1)
                    if b == 1 and j == 3:
                        take("rbc", rbc[:], KEYS, rbc_ready)
                    if b == 2 and j == 0:
                        act.wait_ge(lam_sums, 1)
                        nc.scalar.activation(lsum, lsum, ACT.Exp).then_inc(lam_exp, 1)
                    block1_take_late(b, j)
                    attention(8 * b + j)
                    if b:
                        block1_side(b, j)
                        block1_rope(b, j)
                        block1_take(b, j)

            for c in range(4):
                b = Q_WOUT + c
                for j in range(8):
                    split(b, j)
                    if c == 0 and j == 1:
                        stat_group(G_Y + 2)
                    if c == 0 and j == 2:
                        block1_side(b, 2)
                        act.dma_start(grow[:], bass.AP(tensor=t["post_norm_g"].tensor, offset=0, ap=[[0, P], [1, D]])).then_inc(grow_in, 16)
                        stat_group(G_Y + 3)
                        stat_group(G_Y + 4)
                    if c == 0 and j == 3:
                        stat_group(G_Y + 5)
                    if c == 0 and j == 7:
                        stat_group(G_Y + 6)
                        stat_group(G_Y + 7)
                    if c and j == 2:
                        y_squares(act, b - 1)

            for c in range(12):
                b = B_W2 + c
                for j in range(8):
                    split(b, j)
                    attention_early(8 * b + j)
                    if c == 0 and j == 2:
                        y_squares(act, b - 1)
                        stat_group(G_H1)
                        stat_group(G_H1 + 1)
                    if c == 1 and j == 0:
                        stat_group(G_H1 + 7)
                    if c == 0 and j > 2:
                        stat_group(G_H1 + j - 1)
                        if j >= 4:
                            k = j - 4
                            for i in range(TT):
                                act.wait_ge(h1_ready, TT * k + i + 1)
                                done = nc.scalar.activation(tmp[:, 0, :], xres[:, i, k * CW:(k + 1) * CW], ACT.Square,
                                                            accum_out=ssx[:, i, k:k + 1])
                                chain.after(chain.step(done)) if (i, k) != (TT - 1, 3) else done.then_inc(h1sq, 1)
                    attention(8 * b + j)
                    prev = c - 1
                    if c == 1 and j == 3:
                        act.wait_ge(stat_ready, G_H1)
                        act.wait_ge(h1_ready, 8)
                        act.dma_start(reltab[:, 127:REL], t["rel_rev"]).then_inc(rel_in, 16)
                    if c == 1 and j == 7:
                        row = HEADS2 * REL
                        scratch = t["rel_scratch"].tensor
                        act.wait_ge(rel_filled, 1)
                        act.dma_start(bass.AP(tensor=scratch, offset=0, ap=[[REL, HEADS2], [row, P], [1, REL]]),
                                      dims(reltab[:], [0, P], [1, REL])).then_inc(rel_out, 16)
                    if c == 2 and j == 7:
                        act.wait_ge(rel_out, 16)
                        act.dma_start(bias2[:], bass.AP(tensor=scratch, offset=127,
                                                        ap=[[row - 1, P], [REL, HEADS2], [1, TOK]])).then_inc(bias2_in, 16)
                    if c == 1 and j == 3:
                        take("rbc2", rbc2[:], TOK, rbc_ready)
                    if b - 1 in EVICTED and j == 2:
                        evict2(act, prev, acc[(b - 1) % 2], 8 * b)
                    if b in LATE and j == 6:
                        stat_group(LATE[b])
                        stat_group(LATE[b] + 1)

            for c in range(4):
                for half_q in range(2):
                    q = Q_MIX + 2 * c + half_q
                    for j in range(8):
                        split(q, j)
                        if c == 0 and half_q == 0 and j == 2:
                            evict2(act, 11, acc[(B_MIX - 1) % 2], 8 * q)
                        if half_q == 1 and j == 2:
                            act.wait_ge(piece_used, 8 * q)
                            if c:
                                act.wait_ge(merged, c)
                            b = B_MIX + 3 * c
                            for i in range(TT):
                                done = nc.scalar.activation(stg[:, i, :], acc[b % 2][i][:], ACT.Sigmoid, scale=r2[:, i:i + 1])
                            done.then_inc(gate_b, 1)
                        if q in LATE and j == 6:
                            stat_group(LATE[q])
                            stat_group(LATE[q] + 1)

            def h2_squares(k):
                act.wait_ge(h2_added, k + 1)
                for i in range(TT):
                    done = nc.scalar.activation(sqj[:], xres[:, i, k * CW:(k + 1) * CW], ACT.Square, accum_out=ssf[:, i, k:k + 1])
                    if (i, k) == (TT - 1, 3):
                        done.then_inc(h2sq, 1)
                    else:
                        chain.after(chain.step(done))

            def gate_silu(i):
                act.wait_ge(ff_out, i + 1)
                nc.scalar.activation(fgate[:], fgate[:], ACT.Silu).then_inc(ff_silu, 1)

            def ff_stat(i, buf):
                act.wait_ge(ff_up, i + 1)
                nc.scalar.activation(fhi[buf][:], fprod[:], ACT.Copy).then_inc(stat_hi, 1)

            for c in range(4):
                q = Q_WO2 + c
                for j in range(8):
                    split(q, j)
                    if q in LATE and j == 6:
                        stat_group(LATE[q])
                        stat_group(LATE[q] + 1)
                    if c and j == 7:
                        h2_squares(c - 1)
            for c in range(3):
                q = Q_FF + c
                for j in range(8):
                    split(q, j)
                    if q in LATE and j == 6:
                        stat_group(LATE[q])
                        stat_group(LATE[q] + 1)
                    if c == 0 and j == 7:
                        h2_squares(3)
                    if c == 1 and j == 4:
                        take("rbc3", rbc3[:], TOK, rbc_ready)
                    if c == 1 and j == 6:
                        gate_silu(0)
                    if c == 2 and j == 4:
                        ff_stat(0, 0)

            with act.Fori(0, LOOPS) as i:
                q0 = Q_LOOP + 3 * i
                for j in range(8):
                    split(q0, j)
                    if j == 3:
                        gate_silu(i + 1)
                for j in range(8):
                    split(q0 + 1, j)
                for j in range(8):
                    split(q0 + 2, j)
                    if j == 4:
                        ff_stat(i + 1, 0)
            last = FF_CHUNKS - 1
            for j in range(8):
                split(Q_TAIL, j)
                if j == 3:
                    gate_silu(last)
            for j in range(8):
                split(Q_TAIL + 1, j)
                if j == 4:
                    ff_stat(last, 1)
            for j in range(8):
                split(Q_TAIL + 2, j)
            for k in range(4):
                act.wait_ge(down_added, 4 * last + k + 1)
                for i in range(TT):
                    done = nc.scalar.activation(sqj[:], xres[:, i, k * CW:(k + 1) * CW], ACT.Square, accum_out=sso[:, i, k:k + 1])
                    if (i, k) == (TT - 1, 3):
                        done.then_inc(last_sq, 1)
                    else:
                        chain.after(chain.step(done))
            act.wait_ge(last_rstd, 1)
            act.wait_ge(out_gained, 1)
            o = outb[:, 1, 1024:2048]
            nc.scalar.activation(o, o, ACT.Copy, scale=r4[:, 1:2]).then_inc(out_last, 1)
            act.wait_ge(out_last, 1)
            act.dma_start(out[0, P:2 * P, 1024:2048], o).then_inc(out_done, 16)

        @block.vector
        def _(dve):
            chain = Chain(dve, dve_steps)

            def split(q, j):
                g = 8 * q + j
                dve.wait_ge(hi_ready, g + 1)
                nc.vector.tensor_tensor(wlo[:, j % 4], raw[:, j // 2, 2 * (j % 2):2 * (j % 2) + 2, :],
                                        whi[:, j % 4].bitcast(F32), ALU.subtract).then_inc(lo_ready, 1)

            def stat_group(s):
                hi, lo, g = stat_home(s)
                dve.wait_ge(stat_hi, s + 1)
                bank = aux[(use["stat", s] - 1) % 2]
                if g is None:
                    nc.vector.tensor_tensor(lo, bank[:], hi.bitcast(F32), ALU.subtract).then_inc(stat_ready, 1)
                else:
                    nc.vector.scalar_tensor_tensor(lo[:, 0, :], bank[:, 0:TOK], gcol[:, g:g + 1], hi[:, 0, :].bitcast(F32),
                                                   ALU.mult, ALU.subtract)
                    nc.vector.scalar_tensor_tensor(lo[:, 1, :], bank[:, TOK:CW], gcol[:, g + 1:g + 2], hi[:, 1, :].bitcast(F32),
                                                   ALU.mult, ALU.subtract).then_inc(stat_ready, 1)

            def part1(n):
                dve.wait_ge(scores_ready, n + 1)
                mx = sm[:, n, 0:2]
                if is_a(n):
                    for i in range(2):
                        s = chain.step(nc.vector.reduce_max(mx[:, i:i + 1], sbank[i][:, 0:KEYS], AX))
                    chain.after(s)
                else:
                    if is_b(n):
                        dve.wait_ge(alibi_ready, n + 1)
                    else:
                        dve.wait_ge(bias2_in, 16)
                        dve.wait_ge(mask_set, 1)
                    for i in range(2):
                        if is_b(n):
                            bias, keys = alibi[:, n % 4, :], KEYS
                        else:
                            keys = P * (i + 1)
                            bias = bias2[:, n - ITEMS1, TOK - keys:TOK]
                        done = nc.vector.tensor_tensor_reduce(pslot(n)[:, i, 0:keys], sbank[i][:, 0:keys], bias, 1.0, -3e38,
                                                              ALU.add, ALU.max, mx[:, i:i + 1])
                        if i == 0:
                            s = chain.step(done)
                    done.then_inc(biased, 1)
                    chain.after(s)
                    dve.wait_ge(biased, n + 1 if is_b(n) else n - 7)
                nc.vector.tensor_scalar(mx, mx, -SCALE_A if is_a(n) else -1.0, None, ALU.mult).then_inc(negmax, 1)

            rinv_step = {}

            def part2(n):
                dve.wait_ge(exped, n + 1)
                rs = sm[:, n, 2:4]
                s = chain.step(nc.vector.reciprocal(rs, rs))
                rinv_step[n] = s
                if is_b(n):
                    if n == 0:
                        dve.wait_ge(lam_ready, 1)
                    chain.after(s)
                    chain.after(chain.step(nc.vector.tensor_tensor(rs[:, 1:2], rs[:, 1:2], lam, ALU.mult)))
                    p = pslot(n)
                    chain.after(chain.step(nc.vector.tensor_scalar(p[:, 1, :], p[:, 1, :], rs[:, 1:2], None, ALU.mult)))
                    nc.vector.scalar_tensor_tensor(p[:, 0, :], p[:, 0, :], rs[:, 0:1], p[:, 1, :],
                                                   ALU.mult, ALU.subtract).then_inc(probs, 1)

            def part3(n):
                dve.wait_ge(aux_ready, use["o", n])
                bank = aux[(use["o", n] - 1) % 2]
                if is_b(n):
                    h, i = n // 2, n % 2
                    done = nc.vector.tensor_tensor(ybuf[:, i, 1024 + h * HD:1024 + (h + 1) * HD], bank[:, 0:HD], subg[:], ALU.mult)
                elif is_a(n):
                    h = n - 16
                    dve.wait_ge(gated, 1 + h // 4)
                    chain.after(rinv_step[n])
                    for i in range(TT):
                        y = ybuf[:, i, h * HD:(h + 1) * HD]
                        done = nc.vector.scalar_tensor_tensor(y, bank[:, i * HD:(i + 1) * HD], sm[:, n, 2 + i:3 + i], y,
                                                              ALU.mult, ALU.mult)
                else:
                    h = n - ITEMS1
                    chain.after(rinv_step[n])
                    for i in range(TT):
                        done = nc.vector.tensor_scalar(ya[:, i, h * 64:(h + 1) * 64], bank[:, i * 64:(i + 1) * 64],
                                                       sm[:, n, 2 + i:3 + i], None, ALU.mult)
                done.then_inc(attended, 1)

            def attention_early(g):
                n = item_at(g, 8)
                if n is not None and is_b(n):
                    dve.wait_ge(osq, n + 1)
                    nc.vector.tensor_scalar(sm[:, n, 4:5], sm[:, n, 4:5], 1.0 / HD, EPS, ALU.mult, ALU.add).then_inc(ovar, 1)
                    part3(n)
                n = item_at(g, 8)
                if n is not None and not is_b(n):
                    part3(n)

            def attention(g):
                n = item_at(g, 3)
                if n is not None:
                    part1(n)
                n = item_at(g, 5)
                if n is not None:
                    part2(n)

            nc.vector.memset(half, -0.5).then_inc(half_set, 1)
            nc.vector.memset(mhl[:].bitcast(F32), 0.0).then_inc(mhl_zero, 1)
            dve.wait_ge(start_in, 16)
            stat_group(G_X)

            def meta_parts():
                mview = mhl[:, 0:KT * 2 * META].rearrange("p (k m) -> p k m", m=2 * META)
                dve.wait_ge(aux_ready, use["meta"])
                nc.vector.tensor_tensor(mtmp[:], aux[(use["meta"] - 1) % 2][:, 0:KT * META].rearrange("p (k m) -> p k m", m=META),
                                        dims(gcol[:, 0:KT], [1, KT], [0, META]), ALU.mult).then_inc(meta_scaled, 1)
                dve.wait_ge(meta_scaled, 1)
                dve.wait_ge(mhl_zero, 1)
                dve.wait_ge(meta_hi, 1)
                nc.vector.tensor_tensor(mview[:, :, META:2 * META], mtmp[:], mview[:, :, 0:META].bitcast(F32),
                                        ALU.subtract)
                nc.vector.tensor_tensor(xlo[:, :, TOK:KEYS], mtmp[:], xhi[:, :, TOK:KEYS].bitcast(F32),
                                        ALU.subtract).then_inc(meta_stat, 1)

            def gate1(prev, part):
                if part == 0:
                    dve.wait_ge(evicted, EVICTED[prev])
                e = tmp[:, part // 2, part % 2 * 256:(part % 2 + 1) * 256]
                chain.after(chain.step(nc.vector.tensor_scalar(e, e, 1.0, None, ALU.add)))
                nc.vector.reciprocal(e, e).then_inc(gate_parts, 1)

            def block1_side(b, j):
                prev = b - 1
                what = W1[prev][0]
                if what == "ga" and 3 <= j < 7:
                    gate1(prev, j - 3)

            def take_turned(pieces, parts, r, scale=1.0):
                dve.wait_ge(piece_used, pieces)
                for dst, src in parts:
                    done = nc.vector.scalar_tensor_tensor(dst, src, scale, r, ALU.mult, ALU.mult)
                done.then_inc(turned, 1)

            def four_tiles(dst, banks):
                return [(dst[:, c, :], banks[c // 2][:, c % 2 * TOK:(c % 2 + 1) * TOK]) for c in range(4)]

            def turned1(b, j):
                if j == 6 and is_kb(b):
                    half = 0
                    kb, pieces = b, 8 * b + 4
                elif j == 3 and b and is_kb(b - 1):
                    half = 1
                    kb, pieces = b - 1, 8 * b
                else:
                    if j == 3 and b and W1[b - 1][0] == "qb":
                        if b == 1:
                            dve.wait_ge(rbc_ready, 1)
                        h = 4 * W1[b - 1][1]
                        take_turned(8 * b, four_tiles(qtb[:, h:h + 4, :], acc[(b - 1) % 2]), rbc[:, 0:TOK], SCALE_B)
                    return
                h = 4 * W1[kb][1] + 2 * half
                take_turned(pieces, [(ktb[:, h + i, :], acc[1 - half][i][:, 0:KEYS]) for i in range(2)], rbc[:])

            for b in range(Q_WOUT):
                for j in range(8):
                    if b == Q_WOUT - 1 and j in (4, 5):
                        stat_group(G_Y + j - 4)
                    split(b, j)
                    attention_early(8 * b + j)
                    if b == 0 and j == 0:
                        stat_group(G_X + 1)
                    if b == 0 and j in (1, 3, 5):
                        stat_group(G_X + j + 1)
                        stat_group(G_X + j + 2)
                    if b == 0 and j == 7:
                        meta_parts()
                    turned1(b, j)
                    if b == 1 and j == 5:
                        dve.wait_ge(lam_in, 64)
                        for k in range(2):
                            done = nc.vector.tensor_tensor_reduce(junk[:, 64 * k:64 * k + 64], lamt[:, 2 * k, :], lamt[:, 2 * k + 1, :], 1.0, 0.0,
                                                                  ALU.mult, ALU.add, lsum[:, k:k + 1])
                            if k == 0:
                                s = chain.step(done)
                        done.then_inc(lam_sums, 1)
                    if b == 1 and j == 6:
                        dve.wait_ge(consts_in, 96)
                        for n in range(10):
                            g = gq[:, 0 if n < 4 else 1, :]
                            tab = rope[:, n, :]
                            if n in (0, 1, 4, 5, 6):
                                s = chain.step(nc.vector.tensor_tensor(tab, tab, g, ALU.mult))
                            else:
                                tv = tab.rearrange("p (c s i) -> p c s i", c=2, s=2)
                                gv = g.rearrange("p (c s i) -> p c s i", c=2, s=2)
                                for k in range(2):
                                    s = chain.step(nc.vector.tensor_tensor(tv[:, :, k, :], tv[:, :, k, :], gv[:, :, 1 - k, :], ALU.mult))
                        chain.after(s)
                        nc.vector.tensor_scalar(subg[:], subg[:], 1.0 - LAMBDA_INIT, None, ALU.mult).then_inc(rope_tables, 1)
                    if b == 1 and j == 0:
                        dve.wait_ge(squares1, 3)
                        chain.after(chain.step(nc.vector.tensor_scalar(ss[:, 0:2], ss[:, 0:2], 1.0 / D, EPS, ALU.mult, ALU.add)))
                        nc.vector.tensor_scalar(ss[0:META, 2:3], ss[0:META, 2:3], 1.0 / D, EPS, ALU.mult, ALU.add).then_inc(var1, 1)
                        dve.wait_ge(rstd1, 1)
                        nc.vector.tensor_scalar(nr1, ss[:, 0:2], -1.0, None, ALU.mult).then_inc(nrstd1, 1)
                    if b == 2 and j == 1:
                        dve.wait_ge(lam_exp, 1)
                        chain.after(chain.step(nc.vector.tensor_tensor(lam, lsum[:, 0:1], lsum[:, 1:2], ALU.subtract)))
                        nc.vector.tensor_scalar(lam, lam, LAMBDA_INIT, None, ALU.add).then_inc(lam_ready, 1)
                    attention(8 * b + j)
                    if b:
                        block1_side(b, j)

            def post_scale(b):
                c = b - Q_WOUT
                if c == 0:
                    dve.wait_ge(grow_in, 16)
                    dve.wait_ge(stat_ready, G_Y + 8)
                cs = slice(c * CW, (c + 1) * CW)
                for i in range(TT):
                    dve.wait_ge(ysq, TT * c + i + 1)
                    done = nc.vector.tensor_tensor(ybuf[:, i, cs], acc[b % 2][i][:], grow[:, cs], ALU.mult)
                    if c == 3 and i == 0:
                        chain.step(done)
                        total(ssy, rp, yvar, ysq, 8)
                done.then_inc(post_scaled, 1)

            def total(src, dst, sem_out, sq, n):
                dve.wait_ge(sq, n)
                chain.after(chain.step(nc.vector.reduce_sum(dst, src, AX)))
                nc.vector.tensor_scalar(dst, dst, 1.0 / D, EPS, ALU.mult, ALU.add).then_inc(sem_out, 1)

            for c in range(4):
                b = Q_WOUT + c
                for j in range(8):
                    split(b, j)
                    if c == 0 and j == 1:
                        stat_group(G_Y + 2)
                    if c == 0 and j == 2:
                        stat_group(G_Y + 3)
                        stat_group(G_Y + 4)
                    if c == 0 and j == 3:
                        stat_group(G_Y + 5)
                        dve.wait_ge(evicted, EVICTED[12])
                        dve.wait_ge(y_scaled, 16)
                        y = ybuf[:, :, 1024 + CW:2048]
                        nc.vector.tensor_tensor(y, y, stg[:], ALU.mult).then_inc(gated, 1)
                    if c == 0 and j == 7:
                        stat_group(G_Y + 6)
                        stat_group(G_Y + 7)
                    if c and j == 2:
                        post_scale(b - 1)

            def h1_chunk(c):
                cs = slice(c * CW, (c + 1) * CW)
                for i in range(TT):
                    x = xres[:, i, cs]
                    nc.vector.scalar_tensor_tensor(x, ybuf[:, i, cs], rp[:, i:i + 1], x, ALU.mult, ALU.add).then_inc(h1_ready, 1)

            for c in range(12):
                b = B_W2 + c
                for j in range(8):
                    split(b, j)
                    attention_early(8 * b + j)
                    if c == 0 and j == 2:
                        post_scale(b - 1)
                        dve.wait_ge(post_scaled, 4)
                        dve.wait_ge(yrstd, 1)
                        h1_chunk(0)
                        stat_group(G_H1)
                        stat_group(G_H1 + 1)
                        h1_chunk(1)
                    if c == 0 and j > 2:
                        stat_group(G_H1 + j - 1)
                        if j in (3, 5):
                            h1_chunk((j + 1) // 2)
                    if c == 1 and j == 0:
                        stat_group(G_H1 + 7)
                    if c == 1 and j == 0:
                        total(ssx, r2, h1var, h1sq, 1)
                    if (b - 1, 1) in TURNED and j == (4 if c == 1 else 3):
                        if c == 1:
                            dve.wait_ge(rbc_ready, 2)
                        h = (c - 1) % 2 * 4
                        dst, scale = ((q2t, SCALE_B), (k2t, 1.0), None, (ut, 1.0))[(c - 1) // 2]
                        take_turned(8 * b, four_tiles(dst[:, h:h + 4, :], acc[(b - 1) % 2]), rbc2[:], scale)
                    if c == 3 and j == 4:
                        dve.wait_ge(bias2_in, 16)
                        nc.vector.memset(bias2[0:64, :, 192:256], MASKED).then_inc(mask_set, 1)
                    attention(8 * b + j)
                    if b in LATE and j == 6:
                        stat_group(LATE[b])
                        stat_group(LATE[b] + 1)

            for c in range(4):
                for half_q in range(2):
                    q = Q_MIX + 2 * c + half_q
                    for j in range(8):
                        split(q, j)
                        if half_q == 1 and j == 6:
                            branch_a(dve, c)
                        if half_q == 0 and c and j == 2:
                            branch_b(dve, chain, c - 1)
                        if q in LATE and j == 6:
                            stat_group(LATE[q])
                            stat_group(LATE[q] + 1)

            def h2_add(c):
                dve.wait_ge(piece_used, 8 * (Q_WO2 + c) + 8)
                for i in range(TT):
                    x = xres[:, i, c * CW:(c + 1) * CW]
                    done = nc.vector.tensor_tensor(x, acc[(B_WO2 + c) % 2][i][:], x, ALU.add)
                done.then_inc(h2_added, 1)

            def gate_out(piece):
                dve.wait_ge(piece_used, piece)
                for i in range(TT):
                    done = nc.vector.tensor_tensor(fgate[:, 2 * i:2 * i + 2, :], acc[1][i][:].rearrange("p (c t) -> p c t", t=TOK),
                                                   dims(rbc3[:], [0, 2], [1, TOK]), ALU.mult)
                done.then_inc(ff_out, 1)

            def up_times_gate(i, piece):
                dve.wait_ge(piece_used, piece)
                dve.wait_ge(ff_gate, i + 1)
                for k in range(TT):
                    done = nc.vector.tensor_tensor(fprod[:, 2 * k:2 * k + 2, :], acc[0][k][:].rearrange("p (c t) -> p c t", t=TOK),
                                                   fgate[:, 2 * k:2 * k + 2, :], ALU.mult)
                done.then_inc(ff_up, 1)

            def ff_stat(i, buf):
                dve.wait_ge(stat_hi, G_FF + i + 1)
                nc.vector.tensor_tensor(flo[buf][:], fprod[:], fhi[buf][:].bitcast(F32), ALU.subtract).then_inc(stat_ready, 1)

            def down_add(m, par, piece):
                dve.wait_ge(piece_used, piece)
                for i in range(TT):
                    x = xres[:, i, m * CW:(m + 1) * CW]
                    done = nc.vector.tensor_tensor(x, acc[par][i][:], x, ALU.add)
                done.then_inc(down_added, 1)

            for c in range(4):
                q = Q_WO2 + c
                for j in range(8):
                    split(q, j)
                    if c == 0 and j == 2:
                        branch_b(dve, chain, 3)
                    if c and j == 2:
                        h2_add(c - 1)
                    if q in LATE and j == 6:
                        stat_group(LATE[q])
                        stat_group(LATE[q] + 1)
            for c in range(3):
                q = Q_FF + c
                for j in range(8):
                    split(q, j)
                    if c == 0 and j == 2:
                        h2_add(3)
                    if q in LATE and j == 6:
                        stat_group(LATE[q])
                        stat_group(LATE[q] + 1)
                    if c == 1 and j == 0:
                        total(ssf, r3, h2var, h2sq, 1)
                    if c == 1 and j == 5:
                        dve.wait_ge(rbc_ready, 3)
                        gate_out(8 * q)
                    if c == 2 and j == 2:
                        up_times_gate(0, 8 * q)
                        dve.wait_ge(h2_added, 4)
                    if c == 2 and j == 5:
                        ff_stat(0, 0)
            with dve.Fori(0, LOOPS) as i:
                q0 = Q_LOOP + 3 * i
                for j in range(8):
                    split(q0, j)
                    if j == 2:
                        gate_out(8 * q0)
                    if j in (4, 6):
                        m = (j - 4) // 2
                        down_add(m, m, 8 * q0 + 2 * m + 2)
                for j in range(8):
                    split(q0 + 1, j)
                    if j in (0, 2):
                        m = 2 + j // 2
                        down_add(m, m % 2, 8 * q0 + 2 * m + 2)
                for j in range(8):
                    split(q0 + 2, j)
                    if j == 2:
                        up_times_gate(i + 1, 8 * q0 + 16)
                    if j == 5:
                        ff_stat(i + 1, 0)
            last = FF_CHUNKS - 1
            gained = [0]

            def times_gain(m):
                cs = slice(m * CW, (m + 1) * CW)
                dve.wait_ge(down_added, 4 * last + m + 1)
                if m == 0:
                    dve.wait_ge(gfin_in, 16)
                for i in range(TT):
                    done = nc.vector.tensor_tensor(outb[:, i, cs], xres[:, i, cs], gfin[:, cs], ALU.mult)
                    if m == 3 and i == TT - 1:
                        done.then_inc(out_gained, 1)
                    else:
                        gained[0] = chain.step(done)

            for j in range(8):
                split(Q_TAIL, j)
                if j == 2:
                    gate_out(8 * Q_TAIL)
            for j in range(8):
                split(Q_TAIL + 1, j)
                if j == 2:
                    up_times_gate(last, 8 * Q_TAIL + 8)
                if j in (4, 6):
                    m = (j - 4) // 2
                    down_add(m, (m + 1) % 2, 8 * (Q_TAIL + 1) + 2 * m + 2)
                if j == 5:
                    ff_stat(last, 1)
            for j in range(8):
                split(Q_TAIL + 2, j)
                if j in (0, 2):
                    m = 2 + j // 2
                    down_add(m, (m + 1) % 2, 8 * (Q_TAIL + 1) + 2 * m + 2)
                if j in (4, 6):
                    m = (j - 4) // 2
                    down_add(m, (m + 1) % 2, 8 * (Q_TAIL + 2) + 2 * m + 2)
                    times_gain(m)
            down_add(2, 1, 8 * (Q_TAIL + 2) + 6)
            times_gain(2)
            down_add(3, 0, 8 * (Q_TAIL + 2) + 8)
            times_gain(3)
            total(sso, r4, last_var, last_sq, 1)
            dve.wait_ge(last_rstd, 1)
            chain.after(gained[0])
            dve.wait_ge(out_gained, 1)
            for i, c in ((0, 0), (0, 1), (1, 0)):
                o = outb[:, i, c * 1024:(c + 1) * 1024]
                nc.vector.tensor_scalar(o, o, r4[:, i:i + 1], None, ALU.mult).then_inc(out_ready, 1)

        @block.gpsimd
        def _(pool):
            chain = Chain(pool, pool_steps)

            def rsqrt(v):
                shape = v.shape[1]
                return nc.gpsimd.tensor_tensor(v, v, half[0:v.shape[0], 0:shape], ALU.pow)

            def rotate(r, src, rows, heads, table):
                pool.wait_ge(rope_squares, r + 1)
                if r == 0:
                    pool.wait_ge(rope_tables, 1)
                if r:
                    pool.wait_ge(roped, r)
                rs = rss[0:rows, r, 0:heads]
                chain.after(chain.step(nc.gpsimd.tensor_scalar(rs, rs, 1.0 / HD, EPS, ALU.mult, ALU.add)))
                chain.step(rsqrt(rs))
                w = heads * HD
                cos, sin = rope[0:rows, table[0], :], rope[0:rows, table[1], :]
                t0, t1 = tmp[0:rows, 0, 0:w], tmp[0:rows, 1, 0:w]

                def by_head(ap):
                    return ap.rearrange("p (h d) -> p h d", d=HD)

                chain.step(nc.gpsimd.tensor_tensor(by_head(t0), by_head(src), dims(cos, [0, heads], [1, HD]), ALU.mult))
                for c in range(2):
                    for k in range(2):
                        at = c * 64 + k * 32
                        other = c * 64 + (1 - k) * 32
                        s = chain.step(nc.gpsimd.tensor_tensor(dims(t1[:, at:at + 32], [HD, heads], [1, 32]), dims(src[:, other:other + 32], [HD, heads], [1, 32]),
                                                               dims(sin[:, at:at + 32], [0, heads], [1, 32]), ALU.mult))
                chain.after(s)
                chain.after(chain.step(nc.gpsimd.tensor_tensor(t0, t0, t1, ALU.add)))
                nc.gpsimd.tensor_tensor(by_head(src), by_head(t0), dims(rs, [1, heads], [0, HD]), ALU.mult).then_inc(roped, 1)

            def block1(g):
                n = item_at(g, -6)
                if n is not None and is_b(n):
                    if n == 0:
                        pool.wait_ge(consts_in, 96)
                    if n >= 4:
                        pool.wait_ge(biased, n - 3)
                    nc.gpsimd.tensor_scalar(alibi[:, n % 4, :], dist[:, n % 2, :], -(2.0 ** -(n // 2 + 1)), None, ALU.mult).then_inc(alibi_ready, 1)
                n = item_at(g, 8)
                if n is not None and is_b(n):
                    pool.wait_ge(ovar, n + 1)
                    r = sm[:, n, 4:5]
                    chain.after(chain.step(rsqrt(r)))
                    pool.wait_ge(attended, n + 1)
                    y = ybuf[:, n % 2, 1024 + n // 2 * HD:1024 + (n // 2 + 1) * HD]
                    nc.gpsimd.tensor_scalar(y, y, r, None, ALU.mult).then_inc(y_scaled, 1)
                b, j = g // 8, g % 8
                if b == 1:
                    if j == 0:
                        pool.wait_ge(var1, 1)
                        chain.after(chain.step(rsqrt(ss[:, 0:2])))
                        rsqrt(ss[0:META, 2:3]).then_inc(rstd1, 1)
                if b == KVA + 1:
                    if j in (3, 4):
                        rotate(j - 3, stg[:, j - 3, 0:256], P, 2, (4 + j - 3, 7 + j - 3))
                    if j == 5:
                        rotate(2, stgm[:, 0:256], META, 2, (6, 9))
                if b and W1[b - 1][0] == "ga" and j == 7:
                    prev = b - 1
                    pool.wait_ge(gate_parts, 4 * (prev - 8))
                    nc.gpsimd.tensor_tensor(ybuf[:, :, (prev - 9) * CW:(prev - 8) * CW], stg[:], tmp[:], ALU.mult).then_inc(gated, 1)
                if b == 12 and j == 3:
                    pool.wait_ge(evicted, EVICTED[11])
                    pool.wait_ge(y_scaled, 8)
                    y = ybuf[:, :, 1024:1024 + CW]
                    nc.gpsimd.tensor_tensor(y, y, stg[:], ALU.mult).then_inc(gated, 1)
                if b and W1[b - 1][0] == "qa" and j in (3, 4):
                    rotate(3 + 2 * (b - 8) + j - 3, stg[:, j - 3, :], P, 4, (j - 3, 2 + j - 3))

            pool.wait_ge(half_set, 1)
            for g in range(8 * Q_WOUT):
                block1(g)
            pool.wait_ge(yvar, 1)
            rsqrt(rp).then_inc(yrstd, 1)
            pool.wait_ge(h1var, 1)
            rsqrt(r2).then_inc(h1rstd, 1)
            pool.wait_ge(rel_in, 16)
            nc.gpsimd.tensor_copy(reltab[:, 0:127], dims(reltab[:, 127:128], [0, 127])).then_inc(rel_filled, 1)
            pool.wait_ge(poolw_in, 32)
            for w in range(4):
                pool.wait_ge(turned, TURNED[Q_W2 + 6 + w // 2, 1])
                u = ut[:, 2 * w:2 * w + 2, :]
                bufs = [wina[:], winb[:]]
                src = u
                if w:
                    pool.wait_ge(pooled, w)
                for level in range(w + 1):
                    d = 1 << level
                    dst = bufs[level % 2]
                    s1 = chain.step(nc.gpsimd.tensor_copy(dst[:, :, 0:d], src[:, :, 0:d]))
                    s2 = chain.step(nc.gpsimd.tensor_tensor(dst[:, :, d:TOK], src[:, :, d:TOK], src[:, :, 0:TOK - d], ALU.add))
                    chain.after(s2)
                    src = dst
                win = 2 << w
                s1 = chain.step(nc.gpsimd.tensor_tensor(src[:, :, 0:16], src[:, :, 0:16],
                                                        dims(invc[:, w, :], [0, 2], [1, 16]), ALU.mult))
                s2 = chain.step(nc.gpsimd.tensor_scalar(src[:, :, 16:TOK], src[:, :, 16:TOK], 1.0 / win, None, ALU.mult))
                chain.after(s2)
                nc.gpsimd.tensor_tensor(u, src, u, ALU.subtract).then_inc(pooled, 1)
            pool.wait_ge(h2var, 1)
            rsqrt(r3).then_inc(h2rstd, 1)
            with pool.Fori(0, FF_CHUNKS) as i:
                pool.wait_ge(ff_silu, i + 1)
                nc.gpsimd.tensor_tensor(fgate[:], fgate[:], dims(rbc3[:], [0, 4], [1, TOK]), ALU.mult).then_inc(ff_gate, 1)
            pool.wait_ge(last_var, 1)
            rsqrt(r4).then_inc(last_rstd, 1)


def tables():
    f = np.float32
    inv_freq = (np.float64(10000.0) ** (-np.arange(0, 64, 2) / 64.0)).astype(f)
    real = np.arange(TOK)
    row = np.concatenate([real // 64, np.zeros(META)]).astype(f)
    col = np.concatenate([real % 64, np.zeros(META)]).astype(f)
    ang = [(v[:, None] * inv_freq[None, :]).astype(f).astype(np.float64) for v in (row, col)]
    cos = np.concatenate([np.cos(a) for a in ang for _ in range(2)], 1).astype(f)
    sin = np.concatenate([s * np.sin(a) for a in ang for s in (-1, 1)], 1).astype(f)
    rope = np.zeros((P, 10, P), f)
    for n, (tab, i) in enumerate([(cos, 0), (cos, 1), (sin, 0), (sin, 1), (cos, 0), (cos, 1), (cos, 2), (sin, 0), (sin, 1), (sin, 2)]):
        part = tab[i * P:(i + 1) * P]
        rope[:len(part), n] = part
    qpos = META + np.arange(TOK).reshape(TT, P).T
    kpos = np.concatenate([META + np.arange(TOK), np.arange(META)])
    dist = np.abs(qpos[:, :, None] - kpos[None, None, :]).astype(f)
    fold = np.concatenate([np.eye(META)] * 2).astype(f)
    count = np.minimum(np.arange(16)[None, :] + 1, 2 << np.arange(4)[:, None])
    invc = np.broadcast_to((1.0 / count).astype(f), (P, 4, 16)).copy()
    return {"rope_t": rope, "dist_t": dist, "fold_t": fold, "invc_t": invc}


INPUTS = ("x", "meta_tokens", "w_in", "q_norm_g", "k_norm_g", "lambda_q1", "lambda_k1", "lambda_q2",
          "lambda_k2", "subln_g", "w_out", "post_norm_g", "w_in_2", "pool_w_2",
          "w_branch_a_2", "w_branch_b_2", "w_out_2", "w_gate_up_2", "w_down_2", "norm_final_2")


def kernel(**inputs):
    import numpy as np
    from concourse import bacc
    from concourse.bass_utils import run_bass_kernel_spmd

    nc = bacc.Bacc("TRN2", target_bir_lowering=False, num_devices=1)
    arrays = {name: np.ascontiguousarray(inputs[name]) for name in INPUTS}
    arrays["rel_rev"] = np.ascontiguousarray(inputs["rel_bias_2"][0][:, ::-1])
    arrays.update(tables())
    gains = [inputs[n].reshape(-1, P).T for n in ("pre_norm_g", "norm_mix_2", "norm_ffn_2", "pool_scale_2")]
    arrays["start_c"] = np.ascontiguousarray(np.concatenate([np.eye(P, dtype=np.float32)] + gains, axis=1))
    t = {name: nc.dram_tensor(name, a.shape, F32, kind="ExternalInput").ap() for name, a in arrays.items()}
    t["rel_scratch"] = nc.dram_tensor("rel_scratch", (P, HEADS2, REL), F32, kind="Internal").ap()
    out = nc.dram_tensor("out", (1, TOK, D), F32, kind="ExternalOutput").ap()
    build(nc, t, out)
    return run_bass_kernel_spmd(nc, [arrays], core_ids=[0]).results[0]["out"]
```

```python
import numpy as np

import concourse.bass as bass
from concourse import mybir
from concourse.alu_op_type import AluOpType as ALU

F32 = mybir.dt.float32
F32R = mybir.dt.float32r
ACT = mybir.ActivationFunctionType
AX = mybir.AxisListType.X

P = 128
D = 2048
KT = D // P
TOK = 256
TT = TOK // P
META = 16
KEYS = TOK + META
CW = 512
EPS = 1e-6
HD = 128
B_HEADS = 8
LAMBDA_INIT = 0.2
SCALE_A = float(1.0 / np.sqrt(np.float32(HD)))
SCALE_B = 0.125
HEADS2 = 16
REL = 384
DFF = 5632
FF_CHUNKS = DFF // CW
MASKED = -1e30

W1 = (("qb", 0, 5), ("kb", 0, 7), ("kb", 1, 8), ("vb", 0, 9), ("kva", 0, 2), ("vb", 1, 10), ("qb", 1, 6),
      ("qa", 0, 0), ("qa", 1, 1), ("ga", 0, 3), ("ga", 1, 4), ("gb", 0, 11), ("gb", 1, 12))
KVA = 4
Q_WOUT = len(W1)
Q_W2 = Q_WOUT + 4
Q_MIX = Q_W2 + 12
Q_WO2 = Q_MIX + 8
Q_FF = Q_WO2 + 4
Q_LOOP = Q_FF + 3
LOOPS = FF_CHUNKS - 2
Q_TAIL = Q_LOOP + 3 * LOOPS
B_W2 = Q_W2
B_MIX = Q_MIX
B_WO2 = B_MIX + 12
B_FF = B_WO2 + 4
B_LOOP = B_FF + 3
B_TAIL = B_LOOP + 6 * LOOPS

HALVED = (1, 2, 3, 4, 5, 6)
TURNED_ORDER = ((0, 1),) + tuple((b, half) for b in HALVED for half in range(2)) + tuple((Q_W2 + c, 1) for c in (0, 1, 2, 3, 6, 7, 8, 9, 10, 11))
TURNED = {key: n + 1 for n, key in enumerate(TURNED_ORDER)}
BACK = {key: n for n, key in enumerate((b, half) for b in (3, 4, 5) for half in range(2))}
EVICTED = {b: n + 1 for n, b in enumerate((7, 8, 9, 10, 11, 12) + tuple(Q_W2 + c for c in (4, 5)))}


ITEMS1, ITEMS = 24, 40
START1, START2 = 43, 8 * 21 + 6


def start_of(n):
    return START1 + 2 * n if n < ITEMS1 else START2 + 2 * (n - ITEMS1)


def item_at(g, after1, after2=None):
    for n in range(ITEMS):
        if start_of(n) + (after1 if n < ITEMS1 or after2 is None else after2) == g:
            return n
    return None


def is_b(n):
    return n < 16


def is_a(n):
    return 16 <= n < ITEMS1


GATE_STEPS = ((11, 6), (12, 2), (12, 3))

G_X, G_Y, G_H1, G_POOL, G_ATT, G_MERGED, G_H2, G_FF = 0, 8, 16, 24, 28, 32, 40, 48
LATE = {26: G_POOL, 27: G_POOL + 2, 28: G_ATT, 29: G_ATT + 2}
LATE.update({31 + 2 * c: G_MERGED + 2 * c for c in range(4)})
LATE.update({Q_WO2 + 1 + c: G_H2 + 2 * c for c in range(4)})


OUT_V = ((0, 0), (0, 1), (0, 2), (0, 3), (1, 0))
OUT_S = ((1, 1), (1, 2), (1, 3))
OUT_ORDER = (("V", 0), ("S", 0), ("V", 1), ("V", 2), ("S", 1), ("V", 3), ("V", 4), ("S", 2))


def dims(ap, *free):
    return bass.AP(tensor=ap.tensor, offset=ap.offset, ap=[list(ap.ap[0])] + [list(f) for f in free])


class Chain:

    def __init__(self, engine, sem):
        self.engine, self.sem, self.n = engine, sem, 0

    def step(self, instruction):
        instruction.then_inc(self.sem, 1)
        self.n = self.n + 1
        return self.n

    def after(self, n):
        self.engine.wait_ge(self.sem, n)


def build(nc, t, out):
    from contextlib import ExitStack

    ctx = ExitStack()
    with ctx:
        base = (nc.sbuf_base + 63) // 64 * 64
        top = [base]

        def place(name, shape, dt=F32, at=None):
            size = 4 * int(np.prod(shape[1:]))
            if at is None:
                at = top[0]
                top[0] = at + (size + 31) // 32 * 32
            return nc.alloc_sbuf_tensor_at(name, shape, dt, offset=at)

        raw = place("raw", [P, 4, 4, CW])
        whi = place("whi", [P, 4, 2, CW], F32R)
        wlo = place("wlo", [P, 4, 2, CW], F32R)
        xres = place("xres", [P, TT, D])
        o_ybuf = top[0]
        ybuf = place("ybuf", [P, TT, D])
        o_h = top[0]
        hhi = place("hhi", [P, KT, TOK], F32R)
        hlo = place("hlo", [P, KT, TOK], F32R)
        o_r = top[0]
        place("region", [P, 64 * 256])
        o_s = top[0]
        place("small", [P, 640])
        o_stg = top[0]
        stg = place("stg", [P, TT, CW])
        start_c = place("start_c", [P, P + 56])
        ident, gcol = start_c[:, 0:P], start_c[:, P:P + 56]
        pbuf = place("pbuf", [P, 2, 2, KEYS])
        o_pt = top[0]
        pt = place("pt", [P, 2, 3 * P])
        sm = place("sm", [P, ITEMS, 5])
        st = place("st", [P, 112])
        assert top[0] <= nc.sbuf_usable_end, (top[0], nc.sbuf_usable_end)
        xhi = place("xhi", [P, KT, KEYS], F32R, at=o_h)
        xlo = place("xlo", [P, KT, KEYS], F32R, at=o_h + 4 * KT * KEYS)
        o_1 = o_r + 2 * 4 * KT * META
        qtb = place("qtb", [P, B_HEADS, TOK], at=o_1)
        ktb = place("ktb", [P, B_HEADS, KEYS], at=o_1 + 8192)
        vb = place("vb", [P, TT, 1024], at=o_1 + 16896)
        vbm = place("vbm", [META, 1024], at=o_1 + 25088)
        qta = place("qta", [P, 8, TOK], at=o_1 + 29184)
        kta = place("kta", [P, 2, KEYS], at=o_1 + 37376)
        va = place("va", [P, TT, 256], at=o_1 + 39552)
        vam = place("vam", [META, 256], at=o_1 + 41600)
        rope = place("rope", [P, 10, P], at=o_1 + 42624)
        dist = place("dist", [P, TT, KEYS], at=o_1 + 47744)
        alibi = place("alibi", [P, 4, KEYS], at=o_1 + 49920)
        junk = place("junk", [P, P], at=o_1 + 54272)
        junk2 = place("junk2", [P, P], at=o_1 + 62656)
        subg = place("subg", [P, P], at=o_1 + 54784)
        tmp = place("tmp", [P, TT, CW], at=o_1 + 55296)
        pbuf3 = place("pbuf3", [P, 2, KEYS], at=o_1 + 59392)
        rbc = place("rbc", [P, KEYS], at=o_1 + 61568)
        grow = place("grow", [P, D], at=o_h)
        yhi = place("yhi", [P, 8, TOK], F32R, at=o_1)
        ylo = place("ylo", [P, 8, TOK], F32R, at=o_1 + 8192)
        metax = place("metax", [META, D], at=o_ybuf)
        mtmp = place("mtmp", [P, KT, META], at=o_ybuf + 8704)
        turn = [place("turn0", [P, 2, KEYS], at=o_ybuf), place("turn1", [P, 2, KEYS], at=o_s)]
        zeros = place("zeros", [P, CW], F32R, at=o_s)
        stgm = place("stgm", [META, CW], at=o_ybuf + 11776)
        lamt = place("lamt", [P, 4, 64], at=o_ybuf + 13824)
        gq = place("gq", [P, 2, P], at=o_ybuf + 14848)
        q2t = place("q2t", [P, 8, TOK], at=o_r)
        k2t = place("k2t", [P, 8, TOK], at=o_r + 8192)
        v2 = place("v2", [P, TT, 1024], at=o_r + 16384)
        ya = place("ya", [P, TT, 1024], at=o_r + 24576)
        ut = place("ut", [P, 8, TOK], at=o_r + 32768)
        poolw = place("poolw", [P, 8, TOK], at=o_r + 40960)
        ahi = place("ahi", [P, 8, TOK], F32R, at=o_r + 32768)
        alo = place("alo", [P, 8, TOK], F32R, at=o_r + 40960)
        bhi = place("bhi", [P, 8, TOK], F32R, at=o_r + 49152)
        blo = place("blo", [P, 8, TOK], F32R, at=o_r + 57344)
        mhi = place("mhi", [P, KT, TOK], F32R, at=o_r)
        mlo = place("mlo", [P, KT, TOK], F32R, at=o_r + 16384)
        bias2 = place("bias2", [P, HEADS2, TOK], at=o_ybuf)
        wina = place("wina", [P, 2, TOK], at=o_s)
        winb = place("winb", [P, 2, TOK], at=o_r + 57344 + 6144)
        rbc2 = place("rbc2", [P, TOK], at=o_pt + 4 * 3 * P)
        gates = place("gates", [P, KT, TOK], at=o_ybuf)
        gate_now = place("gate_now", [P, 4, TOK], at=o_stg)
        reltab = place("reltab", [HEADS2, REL], at=o_r + 32768)
        fhi = [place(f"fhi{i}", [P, 4, TOK], F32R, at=o_r + 49152 + 8192 * i) for i in range(2)]
        flo = [place(f"flo{i}", [P, 4, TOK], F32R, at=o_r + 53248 + 8192 * i) for i in range(2)]
        gfin = place("gfin", [P, D], at=o_r + 32768)
        fgate = place("fgate", [P, 4, TOK], at=o_ybuf)
        fprod = place("fprod", [P, 4, TOK], at=o_ybuf + 4096)
        rbc3 = place("rbc3", [P, TOK], at=o_ybuf + 10240)
        sqj = place("sqj", [P, CW], at=o_ybuf + 8192)
        outb = place("outb", [P, TT, D], at=o_r)
        invc = place("invc", [P, 4, 16], at=o_s + 2048)

        acc = [[ctx.enter_context(nc.psum_tensor(f"acc{p}{i}", [P, CW], F32)) for i in range(TT)] for p in range(2)]
        sbank = [ctx.enter_context(nc.psum_tensor(f"scores{i}", [P, CW], F32)) for i in range(2)]
        aux = [ctx.enter_context(nc.psum_tensor(f"aux{i}", [P, CW], F32)) for i in range(2)]

        def pslot(n):
            if n < ITEMS1 and n % 3 == 2:
                return pbuf3
            return pbuf[:, n % 3 if n < ITEMS1 else n % 2]

        ss = st[:, 0:3]
        lam = st[:, 6:7]
        lsum = st[:, 8:10]
        half = st[:, 12:32]
        rss = st[:, 32:60].rearrange("p (r h) -> p r h", h=4)
        ssy = st[:, 60:68].rearrange("p (i c) -> p i c", c=4)
        rp = st[:, 68:70]
        ssx = st[:, 70:78].rearrange("p (i c) -> p i c", c=4)
        r2 = st[:, 78:80]
        ssf = st[:, 82:90].rearrange("p (i c) -> p i c", c=4)
        r3 = st[:, 90:92]
        sso = st[:, 92:100].rearrange("p (i c) -> p i c", c=4)
        r4 = st[:, 100:102]

        def sem(name):
            return ctx.enter_context(nc.semaphore(name))

        raw_in = [sem(f"raw_in{u}") for u in range(4)]
        hi_ready, lo_ready, piece_used = sem("hi_ready"), sem("lo_ready"), sem("piece_used")
        stat_hi, stat_ready = sem("stat_hi"), sem("stat_ready")
        meta_scaled, meta_hi, meta_stat = sem("meta_scaled"), sem("meta_hi"), sem("meta_stat")
        rows_taken = sem("rows_taken")
        aux_ready = sem("aux_ready")
        x_in = [sem(f"x_in{c}") for c in range(4)]
        meta_in, start_in, consts_in = sem("meta_in"), sem("start_in"), sem("consts_in")
        lam_in, grow_in, poolw_in, gfin_in = sem("lam_in"), sem("grow_in"), sem("poolw_in"), sem("gfin_in")
        rel_in, rel_out, bias2_in = sem("rel_in"), sem("rel_out"), sem("bias2_in")
        out_done = sem("out_done")
        squares1, var1, rstd1 = sem("squares1"), sem("var1"), sem("rstd1")
        rope_tables, zeroed, half_set, lam_sums, lam_exp, lam_ready = (
            sem("rope_tables"), sem("zeroed"), sem("half_set"), sem("lam_sums"), sem("lam_exp"), sem("lam_ready"))
        evicted = sem("evicted")
        turned = sem("turned")
        rbc_ready = sem("rbc_ready")
        scores_ready, biased, negmax, exped, probs = sem("scores_ready"), sem("biased"), sem("negmax"), sem("exped"), sem("probs")
        pt_ready, osq, ovar, attended, y_scaled = sem("pt_ready"), sem("osq"), sem("ovar"), sem("attended"), sem("y_scaled")
        alibi_ready, rope_squares, roped = sem("alibi_ready"), sem("rope_squares"), sem("roped")
        qk_taken = sem("qk_taken")
        silu_a, gated = sem("silu_a"), sem("gated")
        ysq, post_scaled, yvar, yrstd, h1_ready, h1sq, h1var, h1rstd = (
            sem("ysq"), sem("post_scaled"), sem("yvar"), sem("yrstd"), sem("h1_ready"), sem("h1sq"), sem("h1var"),
            sem("h1rstd"))
        rel_filled, mask_set, pooled, gate_b, merged_a, merged = (
            sem("rel_filled"), sem("mask_set"), sem("pooled"), sem("gate_b"), sem("merged_a"),
            sem("merged"))
        gate_a, gate_b_out = sem("gate_a"), sem("gate_b_out")
        h2_added, h2sq, h2var, h2rstd = sem("h2_added"), sem("h2sq"), sem("h2var"), sem("h2rstd")
        ff_out, ff_silu, ff_gate, ff_up = sem("ff_out"), sem("ff_silu"), sem("ff_gate"), sem("ff_up")
        down_added, half_added = sem("down_added"), sem("half_added")
        last_sq, last_var, last_rstd, out_ready = sem("last_sq"), sem("last_var"), sem("last_rstd"), sem("out_ready")
        out_gained, out_last = sem("out_gained"), sem("out_last")
        dve_steps, pool_steps, act_steps = sem("dve_steps"), sem("pool_steps"), sem("act_steps")

        block = ctx.enter_context(nc.Block())
        use = {}

        def block_taken(b):
            return (evicted, EVICTED[b]) if b in EVICTED else (turned, TURNED[b, 1])

        def taken_mix(b):
            if b < B_MIX:
                return block_taken(b)
            c, what = (b - B_MIX) // 3, (b - B_MIX) % 3
            return ((gate_b_out, c + 1), (merged_a, c + 1), (merged, c + 1))[what]

        def late(pe, q, j, transpose_group, aux_bank, aux_used):
            if q not in LATE or j != 4:
                return
            for s in (LATE[q], LATE[q] + 1):
                if s < G_ATT:
                    w = s - G_POOL
                    pe.wait_ge(pooled, w + 1)
                    pe.wait_ge(poolw_in, 32)
                    bank = aux_bank()
                    for e in range(2):
                        for k in range(2):
                            done = nc.tensor.matmul(bank[:, e * TOK:(e + 1) * TOK], poolw[:, 2 * w + k, e * P:(e + 1) * P],
                                                    ut[:, 2 * w + k, :], start=k == 0, stop=k == 1)
                    done.then_inc(aux_ready, 1)
                    aux_used(("stat", s), (stat_ready, s + 1))
                elif s < G_MERGED:
                    pe.wait_ge(attended, ITEMS)
                    transpose_group(s, ya, 2 * (s - G_ATT))
                elif s < G_H2:
                    continue
                else:
                    pe.wait_ge(h2_added, (s - G_H2) // 2 + 1)
                    transpose_group(s, xres, 2 * (s - G_H2))

        def stat_home(s):
            if s < G_Y:
                return xhi[:, 2 * s:2 * s + 2, 0:TOK], xlo[:, 2 * s:2 * s + 2, 0:TOK], 2 * s
            if s < G_H1:
                k = 2 * (s - G_Y)
                if k < 8:
                    return yhi[:, k:k + 2, :], ylo[:, k:k + 2, :], None
                return hhi[:, k:k + 2, :], hlo[:, k:k + 2, :], None
            if s < G_POOL:
                k = 2 * (s - G_H1)
                return hhi[:, k:k + 2, :], hlo[:, k:k + 2, :], 16 + k
            if s < G_ATT:
                k = 2 * (s - G_POOL)
                return bhi[:, k:k + 2, :], blo[:, k:k + 2, :], 48 + k
            if s < G_MERGED:
                k = 2 * (s - G_ATT)
                return ahi[:, k:k + 2, :], alo[:, k:k + 2, :], None
            if s < G_H2:
                k = 2 * (s - G_MERGED)
                return mhi[:, k:k + 2, :], mlo[:, k:k + 2, :], None
            k = 2 * (s - G_H2)
            return hhi[:, k:k + 2, :], hlo[:, k:k + 2, :], 32 + k

        def y_squares(act, b):
            act.wait_ge(piece_used, 8 * b + 8)
            c = b - Q_WOUT
            for i in range(TT):
                if c or i:
                    act.wait_ge(ysq, TT * c + i)
                nc.scalar.activation(tmp[:, 0, :], acc[b % 2][i][:], ACT.Square, accum_out=ssy[:, i, c:c + 1]).then_inc(ysq, 1)

        def evict2(act, prev, banks, pieces):
            act.wait_ge(piece_used, pieces)
            if prev == 4:
                act.wait_ge(h1rstd, 1)
            for i in range(TT):
                done = nc.scalar.activation(v2[:, i, (prev - 4) * CW:(prev - 3) * CW], banks[i][:], ACT.Copy, scale=r2[:, i:i + 1])
            done.then_inc(evicted, 1)

        def sigmoid_a(act, c):
            act.wait_ge(turned, TURNED[Q_W2 + 8 + c, 1])
            y = gates[:, 4 * c:4 * c + 4, :]
            nc.scalar.activation(y, y, ACT.Sigmoid).then_inc(gate_a, 1)

        def pair(ap):
            return ap.rearrange("p (c t) -> p c t", t=TOK)

        def branch_a(dve, c):
            dve.wait_ge(piece_used, 8 * (Q_MIX + 2 * c + 1) + 4)
            dve.wait_ge(gate_a, c + 1)
            for i in range(TT):
                y = gates[:, 4 * c + 2 * i:4 * c + 2 * i + 2, :]
                done = nc.vector.tensor_tensor(y, pair(acc[(B_MIX + 3 * c + 1) % 2][i][:]), y, ALU.mult)
            done.then_inc(merged_a, 1)

        def branch_b(dve, chain, c):
            dve.wait_ge(piece_used, 8 * (Q_MIX + 2 * c + 2))
            dve.wait_ge(gate_b, c + 1)
            dve.wait_ge(merged_a, c + 1)
            for i in range(TT):
                g = gate_now[:, 2 * i:2 * i + 2, :]
                s = chain.step(nc.vector.tensor_tensor(g, pair(acc[(B_MIX + 3 * c + 2) % 2][i][:]), g, ALU.mult))
            chain.after(s)
            y = gates[:, 4 * c:4 * c + 4, :]
            nc.vector.tensor_tensor(y, y, gate_now[:], ALU.add).then_inc(merged, 1)

        @block.tensor
        def _(pe):
            uses = [0]
            free_at = [None, None]

            def aux_bank():
                b = uses[0] % 2
                if free_at[b] is not None:
                    pe.wait_ge(*free_at[b])
                return aux[b]

            def aux_used(name, free):
                free_at[uses[0] % 2] = free
                use[name] = uses[0] + 1
                uses[0] += 1

            def piece(slot, first, last, banks, stat, kt0):
                for k in range(2):
                    start, stop = first and k == 0, last and k == 1
                    hi, lo = whi[:, slot, k, :], wlo[:, slot, k, :]
                    for i in range(TT):
                        sh, sl = stat(kt0 + k, i)
                        nc.tensor.matmul(banks[i][:], sh, hi, start=start, stop=False)
                        nc.tensor.matmul(banks[i][:], sh, lo, start=False, stop=False)
                        done = nc.tensor.matmul(banks[i][:], sl, hi, start=False, stop=stop)
                done.then_inc(piece_used, 1)

            def piece_turned(j, banks, hi_of, lo_of, tiles=KT):
                for k in range(2):
                    kt = 2 * j + k
                    for c in range(4):
                        o = banks[c // 2][:, c % 2 * TOK:(c % 2 + 1) * TOK]
                        hi, lo = (w[:, j % 4, k, c * P:(c + 1) * P] for w in (whi, wlo))
                        nc.tensor.matmul(o, hi, hi_of[:, kt, 0:TOK], start=kt == 0 and c % 2 == 0, stop=False)
                        nc.tensor.matmul(o, hi, lo_of[:, kt, 0:TOK], start=False, stop=False)
                        done = nc.tensor.matmul(o, lo, hi_of[:, kt, 0:TOK], start=False, stop=kt == tiles - 1 and c % 2 == 1)
                done.then_inc(piece_used, 1)

            def piece_halved(j, width):
                banks = acc[1 - j // 4]
                for k in range(4):
                    kt = 4 * (j % 4) + k
                    for c in range(2):
                        at = 256 * (k % 2) + c * P
                        hi, lo = (w[:, j % 4, k // 2, at:at + P] for w in (whi, wlo))
                        o = banks[c][:, 0:width]
                        nc.tensor.matmul(o, hi, xhi[:, kt, 0:width], start=kt == 0, stop=False)
                        nc.tensor.matmul(o, hi, xlo[:, kt, 0:width], start=False, stop=False)
                        done = nc.tensor.matmul(o, lo, xhi[:, kt, 0:width], start=False, stop=kt == KT - 1)
                done.then_inc(piece_used, 1)

            def back_to_rows(b, half):
                n = BACK[b, half]
                src = turn[n % 2]
                pe.wait_ge(turned, TURNED[b, half])
                bank = aux_bank()
                for i in range(TT):
                    for c in range(2):
                        done = nc.tensor.transpose(bank[:, i * 256 + c * P:i * 256 + (c + 1) * P], src[:, c, i * P:(i + 1) * P], ident)
                done.then_inc(aux_ready, 1)
                aux_used(("rows", n), (rows_taken, n + 1))
                bank = aux_bank()
                for c in range(2):
                    done = nc.tensor.transpose(bank[0:META, c * P:(c + 1) * P], src[:, c, TOK:KEYS], ident)
                done.then_inc(aux_ready, 1)
                aux_used(("meta rows", n), (rows_taken, n + 1))

            def broadcast_r(r, name, meta=False):
                bank = aux_bank()
                for i in range(TT):
                    done = nc.tensor.matmul(bank[:, i * P:(i + 1) * P], dims(r[:, i:i + 1], [0, P]), ident, start=True, stop=True)
                if meta:
                    done = nc.tensor.matmul(bank[:, TOK:KEYS], dims(r[0:META, 2:3], [0, P]), ident[0:META, 0:META], start=True, stop=True)
                done.then_inc(aux_ready, 1)
                aux_used(name, (rbc_ready, {"rbc": 1, "rbc2": 2, "rbc3": 3}[name]))

            def x_stat(kt, i):
                return xhi[:, kt, i * P:(i + 1) * P], xlo[:, kt, i * P:(i + 1) * P]

            def h_stat(kt, i):
                return hhi[:, kt, i * P:(i + 1) * P], hlo[:, kt, i * P:(i + 1) * P]

            def y_stat(kt, i):
                hi, lo = (yhi, ylo) if kt < 8 else (hhi, hlo)
                return hi[:, kt, i * P:(i + 1) * P], lo[:, kt, i * P:(i + 1) * P]

            def m_stat(kt, i):
                return mhi[:, kt, i * P:(i + 1) * P], mlo[:, kt, i * P:(i + 1) * P]

            def transpose_group(s, src, kt):
                bank = aux_bank()
                for k in range(2):
                    for i in range(TT):
                        done = nc.tensor.transpose(bank[:, k * TOK + i * P:k * TOK + (i + 1) * P],
                                                   src[:, i, (kt + k) * P:(kt + k + 1) * P], ident)
                done.then_inc(aux_ready, 1)
                aux_used(("stat", s), (stat_ready, s + 1))

            def scores(n):
                if n in (0, 8):
                    pe.wait_ge(turned, TURNED[(2, 6)[n // 8], 1])
                if n in (ITEMS1, ITEMS1 + 8):
                    pe.wait_ge(turned, TURNED[Q_W2 + 2 + (n - ITEMS1) // 8, 1])
                if n:
                    pe.wait_ge(*((exped, n) if is_a(n - 1) else (biased, n if n <= 16 else n - 8)))
                if is_b(n):
                    h, i = n // 2, n % 2
                    for m in range(2):
                        done = nc.tensor.matmul(sbank[m][:, 0:KEYS], qtb[64 * m:64 * m + 64, h, i * P:(i + 1) * P],
                                                ktb[64 * m:64 * m + 64, h, :], start=True, stop=True)
                elif is_a(n):
                    h = n - 16
                    for i in range(TT):
                        done = nc.tensor.matmul(sbank[i][:, 0:KEYS], qta[:, h, i * P:(i + 1) * P],
                                                kta[:, h // 4, :], start=True, stop=True)
                else:
                    h = n - ITEMS1
                    r = slice(64 * (h % 2), 64 * (h % 2) + 64)
                    for i in range(TT):
                        keys = P * (i + 1)
                        done = nc.tensor.matmul(sbank[i][:, 0:keys], q2t[r, h // 2, i * P:(i + 1) * P],
                                                k2t[r, h // 2, 0:keys], start=True, stop=True)
                done.then_inc(scores_ready, 1)

            def transpose_probs(n):
                pe.wait_ge(*((probs, n + 1) if is_b(n) else (exped, n + 1)))
                if n < ITEMS1:
                    for i in range(1 if is_b(n) else 2):
                        bank = aux_bank()
                        p = pslot(n)[:, i, :]
                        for k in range(2):
                            nc.tensor.transpose(bank[:, k * P:(k + 1) * P], p[:, k * P:(k + 1) * P], ident)
                        nc.tensor.transpose(bank[0:META, TOK:TOK + P], p[:, TOK:KEYS], ident).then_inc(aux_ready, 1)
                        aux_used(("pt", n, i), (pt_ready, n + 1))
                else:
                    bank = aux_bank()
                    nc.tensor.transpose(bank[:, 0:P], pslot(n)[:, 0, 0:P], ident)
                    for k in range(2):
                        done = nc.tensor.transpose(bank[:, (k + 1) * P:(k + 2) * P], pslot(n)[:, 1, k * P:(k + 1) * P], ident)
                    done.then_inc(aux_ready, 1)
                    aux_used(("pt", n, 0), (pt_ready, n + 1))

            def attend(n):
                bank = aux_bank()
                if n in (0, 8):
                    pe.wait_ge(rows_taken, (2, len(BACK))[n // 8])
                pe.wait_ge(pt_ready, n + 1)
                if n < ITEMS1:
                    h = n // 2 if is_b(n) else (n - 16) // 4
                    v, vm = (vb, vbm) if is_b(n) else (va, vam)
                    c = slice(h * HD, (h + 1) * HD)
                    for i in range(1 if is_b(n) else 2):
                        o, w = bank[:, i * HD:(i + 1) * HD], pt[:, i, :]
                        for k in range(2):
                            nc.tensor.matmul(o, w[:, k * P:(k + 1) * P], v[:, k, c], start=k == 0, stop=False)
                        done = nc.tensor.matmul(o, w[0:META, TOK:TOK + P], vm[0:META, c], start=False, stop=True)
                else:
                    c = slice((n - ITEMS1) * 64, (n - ITEMS1 + 1) * 64)
                    nc.tensor.matmul(bank[:, 0:64], pt[:, 0, 0:P], v2[:, 0, c], start=True, stop=True)
                    nc.tensor.matmul(bank[:, 64:128], pt[:, 0, P:2 * P], v2[:, 0, c], start=True, stop=False)
                    done = nc.tensor.matmul(bank[:, 64:128], pt[:, 0, 2 * P:3 * P], v2[:, 1, c], start=False, stop=True)
                done.then_inc(aux_ready, 1)
                aux_used(("o", n), (attended, n + 1))

            def attention(g):
                n = item_at(g, 5, 4)
                if n is not None:
                    transpose_probs(n)
                n = item_at(g, 0)
                if n is not None:
                    scores(n)
                n = item_at(g, 6, 5)
                if n is not None:
                    attend(n)

            taken = [0]

            def transpose_heads(name, tiles):
                bank = aux_bank()
                at = 0
                for tile, rows in tiles:
                    done = nc.tensor.transpose(bank[:, at:at + rows], tile, ident[0:rows, 0:rows])
                    at += rows
                done.then_inc(aux_ready, 1)
                taken[0] += 1
                aux_used(name, (qk_taken, taken[0]))

            def head_pair(name, c):
                transpose_heads(name, [(stg[:, i, (c + k) * P:(c + k + 1) * P], P) for k in range(2) for i in range(TT)])

            pe.wait_ge(zeroed, 1)
            for _ in range(8):
                nc.tensor.matmul(acc[1][0][:], zeros[:, 0:P], zeros[:], start=True, stop=True)
            pe.wait_ge(start_in, 16)
            for s in range(2):
                pe.wait_ge(x_in[0], 16)
                transpose_group(G_X + s, xres, 2 * s)

            for _ in range(8):
                nc.tensor.matmul(acc[1][0][:], zeros[:, 0:P], zeros[:], start=True, stop=True)

            def meta_transposes():
                pe.wait_ge(meta_in, 16)
                bank = aux_bank()
                for kt in range(KT):
                    done = nc.tensor.transpose(bank[:, kt * META:(kt + 1) * META], metax[:, kt * P:(kt + 1) * P],
                                               ident[0:META, 0:META])
                done.then_inc(aux_ready, 1)
                aux_used("meta", (meta_scaled, 1))

            for b in range(Q_WOUT):
                for j in range(8):
                    g = 8 * b + j
                    attention(g)
                    if b == 0 and j in (1, 2, 4):
                        pe.wait_ge(x_in[j // 2 + 1], 16)
                        for s in (j // 2 * 2 + 2, j // 2 * 2 + 3):
                            transpose_group(G_X + s, xres, 2 * s)
                    if b == 0 and j == 6:
                        meta_transposes()
                    if b == Q_WOUT - 1 and j in (1, 2, 6):
                        k = (1, 2, 6).index(j)
                        pe.wait_ge(gated, (1, 1, 2)[k])
                        transpose_group(G_Y + k, ybuf, 2 * k)
                    prev = b - 1
                    if j == 7 and (b, 0) in BACK:
                        back_to_rows(b, 0)
                    if j == 4 and (prev, 1) in BACK:
                        back_to_rows(prev, 1)
                    what = W1[prev][0] if b else None
                    if b == 1 and j == 1:
                        pe.wait_ge(rstd1, 1)
                        broadcast_r(ss, "rbc", meta=True)
                    if what == "kva" and j == 6:
                        pe.wait_ge(roped, 3)
                        head_pair(("ka", 0), 0)
                        transpose_heads(("kam", 0), [(stgm[:, k * P:(k + 1) * P], META) for k in range(2)])
                    if what == "qa" and j == 7:
                        pe.wait_ge(roped, 3 + 2 * (prev - 6))
                        head_pair(("t", prev, 0), 0)
                    if b >= 2 and W1[b - 2][0] == "qa" and j == 0:
                        head_pair(("t", b - 2, 1), 2)
                    if b == 0:
                        pe.wait_ge(stat_ready, G_X + j + 1)
                    if b == 1 and j == 0:
                        pe.wait_ge(meta_stat, 1)
                    if b in HALVED and j in (0, 4) and (b, j) != (1, 0):
                        pe.wait_ge(turned, TURNED[b - 1, j // 4] if b > 1 else TURNED[0, 1])
                    if j == 0 and b in (7, 8):
                        pe.wait_ge(turned, TURNED[6, b - 7])
                    if j == 0 and b > 8:
                        pe.wait_ge(*block_taken(b - 2))
                    pe.wait_ge(lo_ready, g + 1)
                    if b in HALVED:
                        piece_halved(j, TOK if W1[b][0] == "qb" else KEYS)
                    elif b == 0:
                        piece_turned(j, acc[0], xhi, xlo)
                    else:
                        piece(g % 4, j == 0, j == 7, acc[b % 2], x_stat, 2 * j)

            def y_group(s):
                pe.wait_ge(gated, (s - G_Y) // 2 + 1)
                transpose_group(s, ybuf, 2 * (s - G_Y))

            for c in range(4):
                b = Q_WOUT + c
                for j in range(8):
                    g = 8 * b + j
                    if c == 0 and j in (0, 1, 5):
                        for s in {0: (3, 4), 1: (5,), 5: (6, 7)}[j]:
                            y_group(G_Y + s)
                    if c == 0:
                        pe.wait_ge(stat_ready, G_Y + j + 1)
                    if j == 0:
                        pe.wait_ge(*(block_taken(b - 2) if b - 2 < Q_WOUT else (post_scaled, b - 2 - Q_WOUT + 1)))
                    pe.wait_ge(lo_ready, g + 1)
                    piece(g % 4, j == 0, j == 7, acc[b % 2], y_stat, 2 * j)

            def h1_chunk(s):
                k = s - G_H1
                pe.wait_ge(h1_ready, 2 * (k + 1 if k < 2 else k // 2 + 2))

            for s in range(G_H1, G_H1 + 2):
                h1_chunk(s)
                transpose_group(s, xres, 2 * (s - G_H1))
            for c in range(12):
                b = B_W2 + c
                for j in range(8):
                    g = 8 * b + j
                    attention(g)
                    prev = c - 1
                    if c == 0 and 1 <= j < 7:
                        h1_chunk(G_H1 + j + 1)
                        transpose_group(G_H1 + j + 1, xres, 2 * (j + 1))
                    if c == 1 and j == 1:
                        pe.wait_ge(h1rstd, 1)
                        broadcast_r(r2, "rbc2")
                    late(pe, b, j, transpose_group, aux_bank, aux_used)
                    if c == 0:
                        pe.wait_ge(stat_ready, G_H1 + j + 1)
                    if j == 0:
                        pe.wait_ge(*((post_scaled, b - 2 - Q_WOUT + 1) if c < 2 else block_taken(b - 2)))
                    pe.wait_ge(lo_ready, g + 1)
                    if (b, 1) in TURNED:
                        piece_turned(j, acc[b % 2], hhi, hlo)
                    else:
                        piece(g % 4, j == 0, j == 7, acc[b % 2], h_stat, 2 * j)

            for c in range(4):
                for half_q in range(2):
                    q = Q_MIX + 2 * c + half_q
                    for j in range(8):
                        g = 8 * q + j
                        late(pe, q, j, transpose_group, aux_bank, aux_used)
                        b = B_MIX + 3 * c + (0 if half_q == 0 else 1 + j // 4)
                        if j == 0 or (half_q == 1 and j == 4):
                            pe.wait_ge(*taken_mix(b - 2))
                        pe.wait_ge(lo_ready, g + 1)
                        if half_q == 0:
                            piece_turned(j, acc[b % 2], hhi, hlo)
                        else:
                            if c == 0 and j == 0:
                                pe.wait_ge(stat_ready, G_ATT + 4)
                            piece_turned(j % 4, acc[b % 2], ahi if j < 4 else bhi, alo if j < 4 else blo, tiles=8)

            for c in range(4):
                q, b = Q_WO2 + c, B_WO2 + c
                for j in range(8):
                    g = 8 * q + j
                    late(pe, q, j, transpose_group, aux_bank, aux_used)
                    if c == 0 and j % 2 == 0:
                        pe.wait_ge(stat_ready, G_MERGED + j + 2)
                    if j == 0:
                        pe.wait_ge(*(taken_mix(b - 2) if c < 2 else (h2_added, c - 1)))
                    pe.wait_ge(lo_ready, g + 1)
                    piece(g % 4, j == 0, j == 7, acc[b % 2], m_stat, 2 * j)

            for c in range(3):
                q, b = Q_FF + c, B_FF + c
                for j in range(8):
                    g = 8 * q + j
                    late(pe, q, j, transpose_group, aux_bank, aux_used)
                    if c == 0 and j % 2 == 0:
                        pe.wait_ge(stat_ready, G_H2 + j + 2)
                    if c == 1 and j == 2:
                        pe.wait_ge(h2rstd, 1)
                        broadcast_r(r3, "rbc3")
                    if j == 0:
                        pe.wait_ge(*((h2_added, c + 3) if c < 2 else (ff_out, 1)))
                    pe.wait_ge(lo_ready, g + 1)
                    piece_turned(j, acc[b % 2], hhi, hlo)

            def f_stat(buf):
                return lambda kt, i: (fhi[buf][:, kt, i * P:(i + 1) * P], flo[buf][:, kt, i * P:(i + 1) * P])

            with pe.Fori(0, LOOPS) as i:
                g0 = 8 * Q_LOOP + 24 * i
                for j in range(8):
                    m = j // 2
                    if j == 0:
                        pe.wait_ge(stat_ready, G_FF + i + 1)
                        pe.wait_ge(ff_up, i + 1)
                    if j == 2:
                        pe.wait_ge(ff_out, i + 2)
                    if j in (4, 6):
                        pe.wait_ge(down_added, 4 * i + m - 1)
                    pe.wait_ge(lo_ready, g0 + j + 1)
                    piece(j % 4, j % 2 == 0, j % 2 == 1, acc[m % 2], f_stat(0), 2 * (j % 2))
                for j in range(8):
                    if j == 0:
                        pe.wait_ge(down_added, 4 * i + 3)
                    pe.wait_ge(lo_ready, g0 + 8 + j + 1)
                    piece_turned(j, acc[0], hhi, hlo)
                for j in range(8):
                    if j == 0:
                        pe.wait_ge(down_added, 4 * i + 4)
                    pe.wait_ge(lo_ready, g0 + 16 + j + 1)
                    piece_turned(j, acc[1], hhi, hlo)

            last = FF_CHUNKS - 1
            for j in range(8):
                if j == 0:
                    pe.wait_ge(ff_up, last)
                pe.wait_ge(lo_ready, 8 * Q_TAIL + j + 1)
                piece_turned(j, acc[0], hhi, hlo)
            for j in range(8):
                m = j // 2
                if j == 0:
                    pe.wait_ge(ff_out, last + 1)
                if j == 2:
                    pe.wait_ge(ff_up, last + 1)
                if j in (4, 6):
                    pe.wait_ge(down_added, 4 * (last - 1) + m - 1)
                pe.wait_ge(lo_ready, 8 * (Q_TAIL + 1) + j + 1)
                piece(j % 4, j % 2 == 0, j % 2 == 1, acc[(m + 1) % 2], f_stat(0), 2 * (j % 2))
            for j in range(8):
                m = j // 2
                if j == 0:
                    pe.wait_ge(stat_ready, G_FF + last + 1)
                if j % 2 == 0:
                    pe.wait_ge(down_added, 4 * last + m - 1)
                pe.wait_ge(lo_ready, 8 * (Q_TAIL + 2) + j + 1)
                piece(j % 4, j % 2 == 0, j % 2 == 1, acc[(m + 1) % 2], f_stat(1), 2 * (j % 2))

        @block.sync
        def _(sp):
            def rows(ap, n):
                return bass.AP(tensor=ap.tensor, offset=0, ap=[[0, P], [1, n]])

            def quad(q, srcs):
                for u in range(4):
                    sp.wait_ge(lo_ready, 8 * (q - 1) + 2 * u + 2)
                    sp.dma_start(raw[:, u], srcs[u].rearrange("(k p) n -> p k n", p=P)).then_inc(raw_in[u], 16)

            def column_block(w, c0):
                return [w[u * CW:(u + 1) * CW, bass.ds(c0, CW)] for u in range(4)]

            def row_block(w, r0):
                return [w[bass.ds(r0, CW), u * CW:(u + 1) * CW] for u in range(4)]

            w1, w2, wgu, wdn = t["w_in"][0], t["w_in_2"][0], t["w_gate_up_2"][0], t["w_down_2"][0]
            sp.dma_start(start_c[:], t["start_c"]).then_inc(start_in, 16)
            first = column_block(w1, W1[0][2] * CW)
            xs = t["x"][0].rearrange("(i p) d -> p i d", p=P)
            for u in range(4):
                sp.dma_start(xres[:, :, u * CW:(u + 1) * CW], xs[:, :, u * CW:(u + 1) * CW]).then_inc(x_in[u], 16)
                sp.dma_start(raw[:, u], first[u].rearrange("(k p) n -> p k n", p=P)).then_inc(raw_in[u], 16)
            for name, dst in (("rope_t", rope[:]), ("dist_t", dist[:])):
                sp.dma_start(dst, t[name]).then_inc(consts_in, 16)
            sp.dma_start(gq[:, 0, :], rows(t["q_norm_g"], P)).then_inc(consts_in, 16)
            sp.dma_start(gq[:, 1, :], rows(t["k_norm_g"], P)).then_inc(consts_in, 16)
            sp.dma_start(subg[:], rows(t["subln_g"], P)).then_inc(consts_in, 16)
            for n, name in enumerate(("lambda_q1", "lambda_k1", "lambda_q2", "lambda_k2")):
                sp.dma_start(lamt[:, n, :], rows(t[name], 64)).then_inc(lam_in, 16)
            for q in range(1, Q_WOUT):
                c0 = W1[q][2] * CW
                if q not in HALVED:
                    quad(q, column_block(w1, c0))
                    continue
                for u in range(4):
                    sp.wait_ge(lo_ready, 8 * (q - 1) + 2 * u + 2)
                    src = w1[u % 2 * 1024:(u % 2 + 1) * 1024, c0 + u // 2 * 256:c0 + (u // 2 + 1) * 256]
                    sp.dma_start(raw[:, u].rearrange("p a (b n) -> p (a b) n", n=256),
                                 src.rearrange("(k p) n -> p k n", p=P)).then_inc(raw_in[u], 16)
            for c in range(4):
                quad(Q_WOUT + c, column_block(t["w_out"][0], c * CW))
            for c in range(12):
                quad(Q_W2 + c, column_block(w2, c * CW))
                if c == 1:
                    sp.wait_ge(stat_ready, G_Y + 8)
                    sp.dma_start(invc[:], t["invc_t"]).then_inc(poolw_in, 16)
                    sp.dma_start(poolw[:], t["pool_w_2"][0].rearrange("g (k p) e -> p (g k) e", p=P)).then_inc(poolw_in, 16)
            for c in range(4):
                quad(Q_MIX + 2 * c, column_block(w2, (12 + c) * CW))
                wa, wb = t["w_branch_a_2"][0], t["w_branch_b_2"][0]
                cs = slice(c * CW, (c + 1) * CW)
                quad(Q_MIX + 2 * c + 1, [wa[0:CW, cs], wa[CW:2 * CW, cs], wb[0:CW, cs], wb[CW:2 * CW, cs]])
            for c in range(4):
                quad(Q_WO2 + c, column_block(t["w_out_2"][0], c * CW))
            quad(Q_FF, column_block(wgu, 0))
            quad(Q_FF + 1, column_block(wgu, DFF))
            quad(Q_FF + 2, column_block(wgu, CW))
            sp.wait_ge(merged, 4)
            sp.dma_start(gfin[:], rows(t["norm_final_2"], D)).then_inc(gfin_in, 16)
            with sp.Fori(0, LOOPS) as i:
                quad(Q_LOOP + 3 * i, row_block(wdn, i * CW))
                quad(Q_LOOP + 1 + 3 * i, column_block(wgu, DFF + (i + 1) * CW))
                quad(Q_LOOP + 2 + 3 * i, column_block(wgu, (i + 2) * CW))
            quad(Q_TAIL, column_block(wgu, DFF + 10 * CW))
            quad(Q_TAIL + 1, row_block(wdn, 9 * CW))
            quad(Q_TAIL + 2, row_block(wdn, 10 * CW))
            for scaled, n in OUT_ORDER:
                i, c = (OUT_V if scaled == "V" else OUT_S)[n]
                cs = slice(c * CW, (c + 1) * CW)
                sp.wait_ge(out_ready if scaled == "V" else out_last, n + 1)
                sp.dma_start(out[0, i * P:(i + 1) * P, cs], outb[:, i, cs]).then_inc(out_done, 16)
            sp.wait_ge(out_done, 16 * len(OUT_ORDER))

        @block.scalar
        def _(act):
            chain = Chain(act, act_steps)

            def split(q, j):
                g = 8 * q + j
                if j % 2 == 0:
                    act.wait_ge(raw_in[j // 2], 16 * (q + 1))
                if not isinstance(g, int) or g >= 4:
                    act.wait_ge(piece_used, g - 3)
                nc.scalar.activation(whi[:, j % 4], raw[:, j // 2, 2 * (j % 2):2 * (j % 2) + 2, :], ACT.Copy).then_inc(hi_ready, 1)

            def stat_group(s):
                hi, _, g = stat_home(s)
                if G_MERGED <= s < G_H2:
                    act.wait_ge(merged, (s - G_MERGED) // 2 + 1)
                    nc.scalar.activation(hi, gates[:, 2 * (s - G_MERGED):2 * (s - G_MERGED) + 2, :], ACT.Copy).then_inc(stat_hi, 1)
                    return
                act.wait_ge(aux_ready, use["stat", s])
                bank = aux[(use["stat", s] - 1) % 2]
                if g is None:
                    nc.scalar.activation(hi, bank[:], ACT.Copy).then_inc(stat_hi, 1)
                else:
                    nc.scalar.activation(hi[:, 0, :], bank[:, 0:TOK], ACT.Copy, scale=gcol[:, g:g + 1])
                    nc.scalar.activation(hi[:, 1, :], bank[:, TOK:CW], ACT.Copy, scale=gcol[:, g + 1:g + 2]).then_inc(stat_hi, 1)

            def attention_early(g):
                n = item_at(g, 7, 6)
                if n is not None:
                    for i in range(2 if is_a(n) else 1):
                        act.wait_ge(aux_ready, use["pt", n, i])
                        bank = aux[(use["pt", n, i] - 1) % 2]
                        if n < ITEMS1:
                            nc.scalar.activation(pt[:, i, 0:TOK], bank[:, 0:TOK], ACT.Copy)
                            done = nc.scalar.activation(pt[0:META, i, TOK:TOK + P], bank[0:META, TOK:TOK + P], ACT.Copy)
                        else:
                            done = nc.scalar.activation(pt[:, 0, :], bank[:, 0:3 * P], ACT.Copy)
                    done.then_inc(pt_ready, 1)
                n = item_at(g, 8)
                if n is not None and is_b(n):
                    act.wait_ge(aux_ready, use["o", n])
                    nc.scalar.activation(junk2[:], aux[(use["o", n] - 1) % 2][:, 0:HD], ACT.Square,
                                         accum_out=sm[:, n, 4:5]).then_inc(osq, 1)

            def attention(g):
                b, a = item_at(g, 4, 3), item_at(g, 3)
                n = a if a is not None and is_a(a) else b if b is not None and not is_a(b) else None
                if n is not None:
                    act.wait_ge(negmax, n + 1)
                    for i in range(2):
                        keys = KEYS if n < ITEMS1 else P * (i + 1)
                        e = pslot(n)[:, i, 0:keys]
                        done = nc.scalar.activation(e, sbank[i][:, 0:KEYS] if is_a(n) else e, ACT.Exp,
                                                    bias=sm[:, n, i:i + 1], scale=SCALE_A if is_a(n) else 1.0,
                                                    accum_out=sm[:, n, 2 + i:3 + i])
                    done.then_inc(exped, 1)

            act.wait_ge(half_set, 1)
            nc.scalar.activation(sm[:, 0, :], half[:, 0:5], ACT.Exp)
            act.dma_start(metax[:], t["meta_tokens"]).then_inc(meta_in, 16)
            act.wait_ge(meta_in, 16)
            nc.scalar.activation(vb[0:META].rearrange("p a b -> p (a b)"), metax[:], ACT.Square, accum_out=ss[0:META, 2:3]).then_inc(squares1, 1)
            act.wait_ge(start_in, 16)
            stat_group(G_X)

            def meta_hi_part():
                act.wait_ge(meta_scaled, 1)
                nc.scalar.activation(xhi[:, :, TOK:KEYS], mtmp[:], ACT.Copy).then_inc(meta_hi, 1)

            def block1_side(b, j):
                prev = b - 1
                if j == 2 and prev in EVICTED:
                    act.wait_ge(piece_used, 8 * b)
                    if prev == 7:
                        act.wait_ge(rstd1, 1)
                    what = W1[prev][0]
                    dst = tmp if prev in (9, 11) else stg
                    if prev == 9:
                        act.wait_ge(roped, 7)
                    if prev >= 11:
                        act.wait_ge(gated, prev - 10)
                    for i in range(TT):
                        done = nc.scalar.activation(dst[:, i, :], acc[prev % 2][i][:], ACT.Silu if what == "gb" else ACT.Copy,
                                                    scale=ss[:, i:i + 1])
                    done.then_inc(evicted, 1)

            def take_rows(b, half):
                n = BACK[b, half]
                what, part = W1[b][:2]
                if what == "vb":
                    at = part * CW + half * 256
                    dst, dst_meta = vb[:, :, at:at + 256], vbm[:, at:at + 256]
                elif half == 0:
                    dst, dst_meta = stg[:, :, 0:256], stgm[:, 0:256]
                else:
                    dst, dst_meta = va[:], vam[:]
                act.wait_ge(aux_ready, use["rows", n])
                nc.scalar.activation(dst, aux[(use["rows", n] - 1) % 2][:].rearrange("p (i c) -> p i c", c=256), ACT.Copy)
                act.wait_ge(aux_ready, use["meta rows", n])
                nc.scalar.activation(dst_meta, aux[(use["meta rows", n] - 1) % 2][0:META, 0:256], ACT.Copy).then_inc(rows_taken, 1)

            def rope_sums(r, src, rows, heads):
                for h in range(heads):
                    done = nc.scalar.activation(junk[0:rows, :], src[:, h * HD:(h + 1) * HD], ACT.Square, accum_out=rss[0:rows, r, h:h + 1])
                    if h < heads - 1:
                        chain.after(chain.step(done))
                done.then_inc(rope_squares, 1)
                act.wait_ge(rope_squares, r + 1)

            def block1_rope(b, j):
                prev = b - 1
                if W1[prev][0] == "kva" and j == 3:
                    act.wait_ge(rows_taken, BACK[prev, 0] + 1)
                    for i in range(TT):
                        rope_sums(i, stg[:, i, 0:256], P, 2)
                if W1[prev][0] == "kva" and j == 4:
                    rope_sums(2, stgm[:, 0:256], META, 2)
                if W1[prev][0] == "qa" and j in (3, 4):
                    act.wait_ge(evicted, EVICTED[prev])
                    rope_sums(3 + 2 * (prev - 7) + j - 3, stg[:, j - 3, :], P, 4)

            def take(name, dst, width, done=None):
                act.wait_ge(aux_ready, use[name])
                nc.scalar.activation(dst, aux[(use[name] - 1) % 2][:, 0:width], ACT.Copy).then_inc(done or qk_taken, 1)

            def block1_take(b, j):
                prev = b - 1
                if W1[prev][0] == "kva" and j == 7:
                    take(("ka", 0), kta[:, :, 0:TOK], CW)
                    take(("kam", 0), kta[:, :, TOK:KEYS], 2 * META)

            def block1_take_late(b, j):
                if b >= 2 and W1[b - 2][0] == "qa" and j in (1, 2):
                    h = 4 * (b - 9) + 2 * (j - 1)
                    take(("t", b - 2, j - 1), qta[:, h:h + 2, :], CW)

            for b in range(Q_WOUT):
                for j in range(8):
                    if b == Q_WOUT - 1 and j in (4, 5):
                        stat_group(G_Y + j - 4)
                    split(b, j)
                    attention_early(8 * b + j)
                    if b == 0 and j == 0:
                        stat_group(G_X + 1)
                    if b == 0 and j in (1, 3, 5):
                        stat_group(G_X + j + 1)
                        stat_group(G_X + j + 2)
                    if b == 0 and j == 7:
                        meta_hi_part()
                    if b == 0 and j in (5, 6):
                        i = j - 5
                        nc.scalar.activation((qtb, qta)[i][:].rearrange("p a b -> p (a b)"), xres[:, i, :], ACT.Square,
                                             accum_out=ss[:, i:i + 1]).then_inc(squares1, 1)
                    if b == 1 and j == 3:
                        take("rbc", rbc[:], KEYS, rbc_ready)
                    if b == 2 and j == 0:
                        act.wait_ge(lam_sums, 1)
                        nc.scalar.activation(lsum, lsum, ACT.Exp).then_inc(lam_exp, 1)
                    block1_take_late(b, j)
                    attention(8 * b + j)
                    if b:
                        if j == 1 and (b - 1, 0) in BACK:
                            take_rows(b - 1, 0)
                        if j == 6 and (b - 1, 1) in BACK:
                            take_rows(b - 1, 1)
                        block1_side(b, j)
                        if b == 11 and j == 5:
                            act.wait_ge(evicted, EVICTED[10])
                            for k, gate in enumerate((tmp, stg)):
                                nc.scalar.activation(gate[:], gate[:], ACT.Silu).then_inc(silu_a, 1)
                        block1_rope(b, j)
                        block1_take(b, j)

            for c in range(4):
                b = Q_WOUT + c
                for j in range(8):
                    split(b, j)
                    if c == 0 and j == 1:
                        stat_group(G_Y + 2)
                    if c == 0 and j == 2:
                        block1_side(b, 2)
                        act.dma_start(grow[:], bass.AP(tensor=t["post_norm_g"].tensor, offset=0, ap=[[0, P], [1, D]])).then_inc(grow_in, 16)
                        stat_group(G_Y + 3)
                        stat_group(G_Y + 4)
                    if c == 0 and j == 3:
                        stat_group(G_Y + 5)
                    if c == 0 and j == 7:
                        stat_group(G_Y + 6)
                        stat_group(G_Y + 7)
                    if c and j == 2:
                        y_squares(act, b - 1)

            for c in range(12):
                b = B_W2 + c
                for j in range(8):
                    split(b, j)
                    attention_early(8 * b + j)
                    if c == 0 and j == 2:
                        y_squares(act, b - 1)
                        stat_group(G_H1)
                        stat_group(G_H1 + 1)
                    if c == 1 and j == 0:
                        stat_group(G_H1 + 7)
                    if c == 0 and j > 2:
                        stat_group(G_H1 + j - 1)
                        if j >= 4:
                            k = j - 4
                            for i in range(TT):
                                act.wait_ge(h1_ready, TT * (k + 1) + i + 1)
                                done = nc.scalar.activation(tmp[:, 0, :], xres[:, i, k * CW:(k + 1) * CW], ACT.Square,
                                                            accum_out=ssx[:, i, k:k + 1])
                                chain.after(chain.step(done)) if (i, k) != (TT - 1, 3) else done.then_inc(h1sq, 1)
                    attention(8 * b + j)
                    prev = c - 1
                    if c == 1 and j == 3:
                        act.wait_ge(stat_ready, G_H1)
                        act.wait_ge(h1_ready, 10)
                        act.dma_start(reltab[:, 127:REL], t["rel_rev"]).then_inc(rel_in, 16)
                    if c == 1 and j == 7:
                        row = HEADS2 * REL
                        scratch = t["rel_scratch"].tensor
                        act.wait_ge(rel_filled, 1)
                        act.dma_start(bass.AP(tensor=scratch, offset=0, ap=[[REL, HEADS2], [row, P], [1, REL]]),
                                      dims(reltab[:], [0, P], [1, REL])).then_inc(rel_out, 16)
                    if c == 2 and j == 7:
                        act.wait_ge(rel_out, 16)
                        act.dma_start(bias2[:], bass.AP(tensor=scratch, offset=127,
                                                        ap=[[row - 1, P], [REL, HEADS2], [1, TOK]])).then_inc(bias2_in, 16)
                    if c == 1 and j == 3:
                        take("rbc2", rbc2[:], TOK, rbc_ready)
                    if b - 1 in EVICTED and j == 2:
                        evict2(act, prev, acc[(b - 1) % 2], 8 * b)
                    if prev >= 8 and j == 4:
                        sigmoid_a(act, prev - 8)
                    if b in LATE and j == 6:
                        stat_group(LATE[b])
                        stat_group(LATE[b] + 1)

            for c in range(4):
                for half_q in range(2):
                    q = Q_MIX + 2 * c + half_q
                    for j in range(8):
                        split(q, j)
                        if c == 0 and half_q == 0 and j == 4:
                            sigmoid_a(act, 3)
                        if half_q == 1 and j == 3:
                            act.wait_ge(gate_b_out, c + 1)
                            nc.scalar.activation(gate_now[:], gate_now[:], ACT.Sigmoid).then_inc(gate_b, 1)
                        if q in LATE and j == 6:
                            stat_group(LATE[q])
                            stat_group(LATE[q] + 1)

            def h2_squares(k):
                act.wait_ge(h2_added, k + 1)
                for i in range(TT):
                    done = nc.scalar.activation(sqj[:], xres[:, i, k * CW:(k + 1) * CW], ACT.Square, accum_out=ssf[:, i, k:k + 1])
                    if (i, k) == (TT - 1, 3):
                        done.then_inc(h2sq, 1)
                    else:
                        chain.after(chain.step(done))

            def gate_silu(i):
                act.wait_ge(ff_out, i + 1)
                nc.scalar.activation(fgate[:], fgate[:], ACT.Silu).then_inc(ff_silu, 1)

            def ff_stat(i, buf):
                act.wait_ge(ff_up, i + 1)
                nc.scalar.activation(fhi[buf][:], fprod[:], ACT.Copy).then_inc(stat_hi, 1)

            for c in range(4):
                q = Q_WO2 + c
                for j in range(8):
                    split(q, j)
                    if q in LATE and j == 6:
                        stat_group(LATE[q])
                        stat_group(LATE[q] + 1)
                    if c and j == 7:
                        h2_squares(c - 1)
            for c in range(3):
                q = Q_FF + c
                for j in range(8):
                    split(q, j)
                    if q in LATE and j == 6:
                        stat_group(LATE[q])
                        stat_group(LATE[q] + 1)
                    if c == 0 and j == 7:
                        h2_squares(3)
                    if c == 1 and j == 4:
                        take("rbc3", rbc3[:], TOK, rbc_ready)
                    if c == 1 and j == 6:
                        gate_silu(0)
                    if c == 2 and j == 4:
                        ff_stat(0, 0)

            with act.Fori(0, LOOPS) as i:
                q0 = Q_LOOP + 3 * i
                for j in range(8):
                    split(q0, j)
                    if j == 3:
                        gate_silu(i + 1)
                for j in range(8):
                    split(q0 + 1, j)
                for j in range(8):
                    split(q0 + 2, j)
                    if j == 4:
                        ff_stat(i + 1, 0)
            last = FF_CHUNKS - 1
            for j in range(8):
                split(Q_TAIL, j)
                if j == 3:
                    gate_silu(last)
            for j in range(8):
                split(Q_TAIL + 1, j)
                if j == 4:
                    ff_stat(last, 1)
            for j in range(8):
                split(Q_TAIL + 2, j)
            for k in range(4):
                for i in range(TT):
                    if (i, k) == (0, 3):
                        act.wait_ge(half_added, 1)
                    else:
                        act.wait_ge(down_added, 4 * last + k + 1)
                    done = nc.scalar.activation(sqj[:], xres[:, i, k * CW:(k + 1) * CW], ACT.Square, accum_out=sso[:, i, k:k + 1])
                    if (i, k) == (TT - 1, 3):
                        done.then_inc(last_sq, 1)
                    else:
                        chain.after(chain.step(done))
            act.wait_ge(last_rstd, 1)
            act.wait_ge(out_gained, 1)
            for i, c in OUT_S:
                o = outb[:, i, c * CW:(c + 1) * CW]
                nc.scalar.activation(o, o, ACT.Copy, scale=r4[:, i:i + 1]).then_inc(out_last, 1)

        @block.vector
        def _(dve):
            chain = Chain(dve, dve_steps)

            def split(q, j):
                g = 8 * q + j
                dve.wait_ge(hi_ready, g + 1)
                nc.vector.tensor_tensor(wlo[:, j % 4], raw[:, j // 2, 2 * (j % 2):2 * (j % 2) + 2, :],
                                        whi[:, j % 4].bitcast(F32), ALU.subtract).then_inc(lo_ready, 1)

            def stat_group(s):
                hi, lo, g = stat_home(s)
                dve.wait_ge(stat_hi, s + 1)
                if G_MERGED <= s < G_H2:
                    nc.vector.tensor_tensor(lo, gates[:, 2 * (s - G_MERGED):2 * (s - G_MERGED) + 2, :], hi.bitcast(F32), ALU.subtract).then_inc(stat_ready, 1)
                    return
                bank = aux[(use["stat", s] - 1) % 2]
                if g is None:
                    nc.vector.tensor_tensor(lo, bank[:], hi.bitcast(F32), ALU.subtract).then_inc(stat_ready, 1)
                else:
                    nc.vector.scalar_tensor_tensor(lo[:, 0, :], bank[:, 0:TOK], gcol[:, g:g + 1], hi[:, 0, :].bitcast(F32),
                                                   ALU.mult, ALU.subtract)
                    nc.vector.scalar_tensor_tensor(lo[:, 1, :], bank[:, TOK:CW], gcol[:, g + 1:g + 2], hi[:, 1, :].bitcast(F32),
                                                   ALU.mult, ALU.subtract).then_inc(stat_ready, 1)

            def part1(n):
                dve.wait_ge(scores_ready, n + 1)
                mx = sm[:, n, 0:2]
                if is_a(n):
                    for i in range(2):
                        s = chain.step(nc.vector.reduce_max(mx[:, i:i + 1], sbank[i][:, 0:KEYS], AX))
                    chain.after(s)
                else:
                    if is_b(n):
                        dve.wait_ge(alibi_ready, n + 1)
                    else:
                        dve.wait_ge(bias2_in, 16)
                        dve.wait_ge(mask_set, 1)
                    for i in range(2):
                        if is_b(n):
                            bias, keys = alibi[:, n % 4, :], KEYS
                        else:
                            keys = P * (i + 1)
                            bias = bias2[:, n - ITEMS1, TOK - keys:TOK]
                        done = nc.vector.tensor_tensor_reduce(pslot(n)[:, i, 0:keys], sbank[i][:, 0:keys], bias, 1.0, -3e38,
                                                              ALU.add, ALU.max, mx[:, i:i + 1])
                        if i == 0:
                            s = chain.step(done)
                    done.then_inc(biased, 1)
                    chain.after(s)
                    dve.wait_ge(biased, n + 1 if is_b(n) else n - 7)
                nc.vector.tensor_scalar(mx, mx, -SCALE_A if is_a(n) else -1.0, None, ALU.mult).then_inc(negmax, 1)

            rinv_step = {}

            def part2(n):
                dve.wait_ge(exped, n + 1)
                rs = sm[:, n, 2:4]
                s = chain.step(nc.vector.reciprocal(rs, rs))
                rinv_step[n] = s
                if is_b(n):
                    if n == 0:
                        dve.wait_ge(lam_ready, 1)
                    chain.after(s)
                    chain.after(chain.step(nc.vector.tensor_tensor(rs[:, 1:2], rs[:, 1:2], lam, ALU.mult)))
                    p = pslot(n)
                    chain.after(chain.step(nc.vector.tensor_scalar(p[:, 1, :], p[:, 1, :], rs[:, 1:2], None, ALU.mult)))
                    nc.vector.scalar_tensor_tensor(p[:, 0, :], p[:, 0, :], rs[:, 0:1], p[:, 1, :],
                                                   ALU.mult, ALU.subtract).then_inc(probs, 1)

            def part3(n):
                dve.wait_ge(aux_ready, use["o", n])
                bank = aux[(use["o", n] - 1) % 2]
                if is_b(n):
                    h, i = n // 2, n % 2
                    done = nc.vector.tensor_tensor(ybuf[:, i, 1024 + h * HD:1024 + (h + 1) * HD], bank[:, 0:HD], subg[:], ALU.mult)
                elif is_a(n):
                    h = n - 16
                    chain.after(rinv_step[n])
                    for i in range(TT):
                        y = ybuf[:, i, h * HD:(h + 1) * HD]
                        done = nc.vector.tensor_scalar(y, bank[:, i * HD:(i + 1) * HD], sm[:, n, 2 + i:3 + i], None, ALU.mult)
                else:
                    h = n - ITEMS1
                    chain.after(rinv_step[n])
                    for i in range(TT):
                        done = nc.vector.tensor_scalar(ya[:, i, h * 64:(h + 1) * 64], bank[:, i * 64:(i + 1) * 64],
                                                       sm[:, n, 2 + i:3 + i], None, ALU.mult)
                done.then_inc(attended, 1)

            def attention_early(g):
                n = item_at(g, 8)
                if n is not None and is_b(n):
                    dve.wait_ge(osq, n + 1)
                    nc.vector.tensor_scalar(sm[:, n, 4:5], sm[:, n, 4:5], 1.0 / HD, EPS, ALU.mult, ALU.add).then_inc(ovar, 1)
                    part3(n)
                n = item_at(g, 8)
                if n is not None and not is_b(n):
                    part3(n)

            def attention(g):
                n = item_at(g, 3)
                if n is not None:
                    part1(n)
                n = item_at(g, 5)
                if n is not None:
                    part2(n)

            nc.vector.memset(half, -0.5).then_inc(half_set, 1)
            nc.vector.memset(zeros[:].bitcast(F32), 0.0).then_inc(zeroed, 1)
            dve.wait_ge(start_in, 16)
            stat_group(G_X)

            def meta_parts():
                dve.wait_ge(aux_ready, use["meta"])
                nc.vector.tensor_tensor(mtmp[:], aux[(use["meta"] - 1) % 2][:, 0:KT * META].rearrange("p (k m) -> p k m", m=META),
                                        dims(gcol[:, 0:KT], [1, KT], [0, META]), ALU.mult).then_inc(meta_scaled, 1)
                dve.wait_ge(meta_scaled, 1)
                dve.wait_ge(meta_hi, 1)
                nc.vector.tensor_tensor(xlo[:, :, TOK:KEYS], mtmp[:], xhi[:, :, TOK:KEYS].bitcast(F32),
                                        ALU.subtract).then_inc(meta_stat, 1)

            def times_gate(k):
                if k < 2:
                    dve.wait_ge(silu_a, k + 1)
                    dve.wait_ge(attended, 20 + 4 * k)
                else:
                    dve.wait_ge(evicted, EVICTED[9 + k])
                    dve.wait_ge(y_scaled, 8 * (k - 1))
                y = ybuf[:, :, k * CW:(k + 1) * CW]
                nc.vector.tensor_tensor(y, y, (tmp, stg)[k % 2][:], ALU.mult).then_inc(gated, 1)

            def take_turned(pieces, parts, r, scale=1.0):
                dve.wait_ge(piece_used, pieces)
                for dst, src in parts:
                    done = nc.vector.scalar_tensor_tensor(dst, src, scale, r, ALU.mult, ALU.mult)
                done.then_inc(turned, 1)

            def four_tiles(dst, banks):
                return [(dst[:, c, :], banks[c // 2][:, c % 2 * TOK:(c % 2 + 1) * TOK]) for c in range(4)]

            def turned1(b, j):
                if b == 1 and j == 3:
                    dve.wait_ge(rbc_ready, 1)
                    take_turned(8, four_tiles(qtb, acc[0]), rbc[:, 0:TOK], SCALE_B)
                if j == 6 and b in HALVED:
                    block, half, pieces = b, 0, 8 * b + 4
                elif j == 2 and b - 1 in HALVED:
                    block, half, pieces = b - 1, 1, 8 * b
                else:
                    return
                what, part = W1[block][:2]
                width = TOK if what == "qb" else KEYS
                if (block, half) in BACK:
                    n = BACK[block, half]
                    if n >= 2:
                        dve.wait_ge(rows_taken, n - 1)
                    dst = turn[n % 2][:]
                else:
                    h = 4 * part + 2 * half
                    dst = (qtb if what == "qb" else ktb)[:, h:h + 2, :]
                take_turned(pieces, [(dst[:, c, :], acc[1 - half][c][:, 0:width]) for c in range(2)], rbc[:, 0:width],
                            SCALE_B if what == "qb" else 1.0)

            for b in range(Q_WOUT):
                for j in range(8):
                    if b == Q_WOUT - 1 and j in (4, 5):
                        stat_group(G_Y + j - 4)
                    split(b, j)
                    attention_early(8 * b + j)
                    if b == 0 and j == 0:
                        stat_group(G_X + 1)
                    if b == 0 and j in (1, 3, 5):
                        stat_group(G_X + j + 1)
                        stat_group(G_X + j + 2)
                    if b == 0 and j == 7:
                        meta_parts()
                    turned1(b, j)
                    if b == 1 and j == 5:
                        dve.wait_ge(lam_in, 64)
                        for k in range(2):
                            done = nc.vector.tensor_tensor_reduce(junk[:, 64 * k:64 * k + 64], lamt[:, 2 * k, :], lamt[:, 2 * k + 1, :], 1.0, 0.0,
                                                                  ALU.mult, ALU.add, lsum[:, k:k + 1])
                            if k == 0:
                                s = chain.step(done)
                        done.then_inc(lam_sums, 1)
                    if b == 1 and j == 6:
                        dve.wait_ge(consts_in, 80)
                        for n in range(10):
                            g = gq[:, 0 if n < 4 else 1, :]
                            tab = rope[:, n, :]
                            if n in (0, 1, 4, 5, 6):
                                s = chain.step(nc.vector.tensor_tensor(tab, tab, g, ALU.mult))
                            else:
                                tv = tab.rearrange("p (c s i) -> p c s i", c=2, s=2)
                                gv = g.rearrange("p (c s i) -> p c s i", c=2, s=2)
                                for k in range(2):
                                    s = chain.step(nc.vector.tensor_tensor(tv[:, :, k, :], tv[:, :, k, :], gv[:, :, 1 - k, :], ALU.mult))
                        chain.after(s)
                        nc.vector.tensor_scalar(subg[:], subg[:], 1.0 - LAMBDA_INIT, None, ALU.mult).then_inc(rope_tables, 1)
                    if b == 1 and j == 0:
                        dve.wait_ge(squares1, 3)
                        chain.after(chain.step(nc.vector.tensor_scalar(ss[:, 0:2], ss[:, 0:2], 1.0 / D, EPS, ALU.mult, ALU.add)))
                        nc.vector.tensor_scalar(ss[0:META, 2:3], ss[0:META, 2:3], 1.0 / D, EPS, ALU.mult, ALU.add).then_inc(var1, 1)
                    if b == 2 and j == 1:
                        dve.wait_ge(lam_exp, 1)
                        chain.after(chain.step(nc.vector.tensor_tensor(lam, lsum[:, 0:1], lsum[:, 1:2], ALU.subtract)))
                        nc.vector.tensor_scalar(lam, lam, LAMBDA_INIT, None, ALU.add).then_inc(lam_ready, 1)
                    attention(8 * b + j)
                    if (b, j) in GATE_STEPS:
                        times_gate(GATE_STEPS.index((b, j)))

            def post_scale(b):
                c = b - Q_WOUT
                if c == 0:
                    dve.wait_ge(grow_in, 16)
                    dve.wait_ge(stat_ready, G_Y + 8)
                cs = slice(c * CW, (c + 1) * CW)
                for i in range(TT):
                    dve.wait_ge(ysq, TT * c + i + 1)
                    done = nc.vector.tensor_tensor(ybuf[:, i, cs], acc[b % 2][i][:], grow[:, cs], ALU.mult)
                    if c == 3 and i == 0:
                        chain.step(done)
                        total(ssy, rp, yvar, ysq, 8)
                done.then_inc(post_scaled, 1)

            def total(src, dst, sem_out, sq, n):
                dve.wait_ge(sq, n)
                chain.after(chain.step(nc.vector.reduce_sum(dst, src, AX)))
                nc.vector.tensor_scalar(dst, dst, 1.0 / D, EPS, ALU.mult, ALU.add).then_inc(sem_out, 1)

            for c in range(4):
                b = Q_WOUT + c
                for j in range(8):
                    split(b, j)
                    if c == 0 and j == 1:
                        stat_group(G_Y + 2)
                    if c == 0 and j == 2:
                        stat_group(G_Y + 3)
                        stat_group(G_Y + 4)
                    if c == 0 and j == 3:
                        stat_group(G_Y + 5)
                        times_gate(3)
                    if c == 0 and j == 7:
                        stat_group(G_Y + 6)
                        stat_group(G_Y + 7)
                    if c and j == 2:
                        post_scale(b - 1)

            def h1_chunk(c0, c1):
                cs = slice(c0, c1)
                for i in range(TT):
                    x = xres[:, i, cs]
                    nc.vector.scalar_tensor_tensor(x, ybuf[:, i, cs], rp[:, i:i + 1], x, ALU.mult, ALU.add).then_inc(h1_ready, 1)

            for c in range(12):
                b = B_W2 + c
                for j in range(8):
                    split(b, j)
                    attention_early(8 * b + j)
                    if c == 0 and j == 2:
                        post_scale(b - 1)
                        dve.wait_ge(post_scaled, 4)
                        dve.wait_ge(yrstd, 1)
                        h1_chunk(0, CW // 2)
                        h1_chunk(CW // 2, CW)
                        stat_group(G_H1)
                        stat_group(G_H1 + 1)
                        h1_chunk(CW, 2 * CW)
                    if c == 0 and j > 2:
                        stat_group(G_H1 + j - 1)
                        if j in (3, 5):
                            h1_chunk((j + 1) // 2 * CW, (j + 3) // 2 * CW)
                    if c == 1 and j == 0:
                        stat_group(G_H1 + 7)
                    if c == 1 and j == 0:
                        total(ssx, r2, h1var, h1sq, 1)
                    if (b - 1, 1) in TURNED and j == (4 if c == 1 else 3):
                        if c == 1:
                            dve.wait_ge(rbc_ready, 2)
                        h = (c - 1) % 2 * 4 if c < 9 else 4 * (c - 9)
                        dst, scale = ((q2t, SCALE_B), (k2t, 1.0), None, (ut, 1.0))[(c - 1) // 2] if c < 9 else (gates, 1.0)
                        take_turned(8 * b, four_tiles(dst[:, h:h + 4, :], acc[(b - 1) % 2]), rbc2[:], scale)
                    if c == 3 and j == 4:
                        dve.wait_ge(bias2_in, 16)
                        nc.vector.memset(bias2[0:64, :, 192:256], MASKED).then_inc(mask_set, 1)
                    attention(8 * b + j)
                    if b in LATE and j == 6:
                        stat_group(LATE[b])
                        stat_group(LATE[b] + 1)

            for c in range(4):
                for half_q in range(2):
                    q = Q_MIX + 2 * c + half_q
                    for j in range(8):
                        split(q, j)
                        if c == 0 and half_q == 0 and j == 3:
                            take_turned(8 * q, four_tiles(gates[:, 12:16, :], acc[(q - 1) % 2]), rbc2[:])
                        if half_q == 1 and j == 2:
                            dve.wait_ge(piece_used, 8 * q)
                            for i in range(TT):
                                done = nc.vector.tensor_tensor(gate_now[:, 2 * i:2 * i + 2, :], pair(acc[(B_MIX + 3 * c) % 2][i][:]),
                                                               dims(rbc2[:], [0, 2], [1, TOK]), ALU.mult)
                            done.then_inc(gate_b_out, 1)
                        if half_q == 1 and j == 6:
                            branch_a(dve, c)
                        if half_q == 0 and c and j == 2:
                            branch_b(dve, chain, c - 1)
                        if q in LATE and j == 6:
                            stat_group(LATE[q])
                            stat_group(LATE[q] + 1)

            def h2_add(c):
                dve.wait_ge(piece_used, 8 * (Q_WO2 + c) + 8)
                for i in range(TT):
                    x = xres[:, i, c * CW:(c + 1) * CW]
                    done = nc.vector.tensor_tensor(x, acc[(B_WO2 + c) % 2][i][:], x, ALU.add)
                done.then_inc(h2_added, 1)

            def gate_out(piece):
                dve.wait_ge(piece_used, piece)
                for i in range(TT):
                    done = nc.vector.tensor_tensor(fgate[:, 2 * i:2 * i + 2, :], acc[1][i][:].rearrange("p (c t) -> p c t", t=TOK),
                                                   dims(rbc3[:], [0, 2], [1, TOK]), ALU.mult)
                done.then_inc(ff_out, 1)

            def up_times_gate(i, piece):
                dve.wait_ge(piece_used, piece)
                dve.wait_ge(ff_gate, i + 1)
                for k in range(TT):
                    done = nc.vector.tensor_tensor(fprod[:, 2 * k:2 * k + 2, :], acc[0][k][:].rearrange("p (c t) -> p c t", t=TOK),
                                                   fgate[:, 2 * k:2 * k + 2, :], ALU.mult)
                done.then_inc(ff_up, 1)

            def ff_stat(i, buf):
                dve.wait_ge(stat_hi, G_FF + i + 1)
                nc.vector.tensor_tensor(flo[buf][:], fprod[:], fhi[buf][:].bitcast(F32), ALU.subtract).then_inc(stat_ready, 1)

            def down_add(m, par, piece, final=False):
                dve.wait_ge(piece_used, piece)
                for i in range(TT):
                    x = xres[:, i, m * CW:(m + 1) * CW]
                    done = nc.vector.tensor_tensor(x, acc[par][i][:], x, ALU.add)
                    if i == 0 and final:
                        done.then_inc(half_added, 1)
                done.then_inc(down_added, 1)

            for c in range(4):
                q = Q_WO2 + c
                for j in range(8):
                    split(q, j)
                    if c == 0 and j == 2:
                        branch_b(dve, chain, 3)
                    if c and j == 2:
                        h2_add(c - 1)
                    if q in LATE and j == 6:
                        stat_group(LATE[q])
                        stat_group(LATE[q] + 1)
            for c in range(3):
                q = Q_FF + c
                for j in range(8):
                    split(q, j)
                    if c == 0 and j == 2:
                        h2_add(3)
                    if q in LATE and j == 6:
                        stat_group(LATE[q])
                        stat_group(LATE[q] + 1)
                    if c == 1 and j == 0:
                        total(ssf, r3, h2var, h2sq, 1)
                    if c == 1 and j == 5:
                        dve.wait_ge(rbc_ready, 3)
                        gate_out(8 * q)
                    if c == 2 and j == 2:
                        up_times_gate(0, 8 * q)
                        dve.wait_ge(h2_added, 4)
                    if c == 2 and j == 5:
                        ff_stat(0, 0)
            with dve.Fori(0, LOOPS) as i:
                q0 = Q_LOOP + 3 * i
                for j in range(8):
                    split(q0, j)
                    if j == 2:
                        gate_out(8 * q0)
                    if j in (4, 6):
                        m = (j - 4) // 2
                        down_add(m, m, 8 * q0 + 2 * m + 2)
                for j in range(8):
                    split(q0 + 1, j)
                    if j in (0, 2):
                        m = 2 + j // 2
                        down_add(m, m % 2, 8 * q0 + 2 * m + 2)
                for j in range(8):
                    split(q0 + 2, j)
                    if j == 2:
                        up_times_gate(i + 1, 8 * q0 + 16)
                    if j == 5:
                        ff_stat(i + 1, 0)
            last = FF_CHUNKS - 1
            gained = [0]

            def times_gain(m):
                cs = slice(m * CW, (m + 1) * CW)
                dve.wait_ge(down_added, 4 * last + m + 1)
                if m == 0:
                    dve.wait_ge(gfin_in, 16)
                for i in range(TT):
                    if (m, i) == (3, 1):
                        total(sso, r4, last_var, last_sq, 1)
                    done = nc.vector.tensor_tensor(outb[:, i, cs], xres[:, i, cs], gfin[:, cs], ALU.mult)
                    if m == 3 and i == TT - 1:
                        done.then_inc(out_gained, 1)
                    else:
                        gained[0] = chain.step(done)

            for j in range(8):
                split(Q_TAIL, j)
                if j == 2:
                    gate_out(8 * Q_TAIL)
            for j in range(8):
                split(Q_TAIL + 1, j)
                if j == 2:
                    up_times_gate(last, 8 * Q_TAIL + 8)
                if j in (4, 6):
                    m = (j - 4) // 2
                    down_add(m, (m + 1) % 2, 8 * (Q_TAIL + 1) + 2 * m + 2)
                if j == 5:
                    ff_stat(last, 1)
            for j in range(8):
                split(Q_TAIL + 2, j)
                if j in (0, 2):
                    m = 2 + j // 2
                    down_add(m, (m + 1) % 2, 8 * (Q_TAIL + 1) + 2 * m + 2)
                if j in (4, 6):
                    m = (j - 4) // 2
                    down_add(m, (m + 1) % 2, 8 * (Q_TAIL + 2) + 2 * m + 2)
                    times_gain(m)
            down_add(2, 1, 8 * (Q_TAIL + 2) + 6)
            times_gain(2)
            down_add(3, 0, 8 * (Q_TAIL + 2) + 8, final=True)
            times_gain(3)
            dve.wait_ge(last_rstd, 1)
            chain.after(gained[0])
            dve.wait_ge(out_gained, 1)
            for i, c in OUT_V:
                o = outb[:, i, c * CW:(c + 1) * CW]
                nc.vector.tensor_scalar(o, o, r4[:, i:i + 1], None, ALU.mult).then_inc(out_ready, 1)

        @block.gpsimd
        def _(pool):
            chain = Chain(pool, pool_steps)

            def rsqrt(v):
                shape = v.shape[1]
                return nc.gpsimd.tensor_tensor(v, v, half[0:v.shape[0], 0:shape], ALU.pow)

            def rotate(r, src, rows, heads, table):
                pool.wait_ge(rope_squares, r + 1)
                if r == 0:
                    pool.wait_ge(rope_tables, 1)
                if r:
                    pool.wait_ge(roped, r)
                rs = rss[0:rows, r, 0:heads]
                chain.after(chain.step(nc.gpsimd.tensor_scalar(rs, rs, 1.0 / HD, EPS, ALU.mult, ALU.add)))
                chain.step(rsqrt(rs))
                w = heads * HD
                cos, sin = rope[0:rows, table[0], :], rope[0:rows, table[1], :]
                t0, t1 = tmp[0:rows, 0, 0:w], tmp[0:rows, 1, 0:w]

                def by_head(ap):
                    return ap.rearrange("p (h d) -> p h d", d=HD)

                chain.step(nc.gpsimd.tensor_tensor(by_head(t0), by_head(src), dims(cos, [0, heads], [1, HD]), ALU.mult))
                for c in range(2):
                    for k in range(2):
                        at = c * 64 + k * 32
                        other = c * 64 + (1 - k) * 32
                        s = chain.step(nc.gpsimd.tensor_tensor(dims(t1[:, at:at + 32], [HD, heads], [1, 32]), dims(src[:, other:other + 32], [HD, heads], [1, 32]),
                                                               dims(sin[:, at:at + 32], [0, heads], [1, 32]), ALU.mult))
                chain.after(s)
                chain.after(chain.step(nc.gpsimd.tensor_tensor(t0, t0, t1, ALU.add)))
                nc.gpsimd.tensor_tensor(by_head(src), by_head(t0), dims(rs, [1, heads], [0, HD]), ALU.mult).then_inc(roped, 1)

            def block1(g):
                n = item_at(g, -6)
                if n is not None and is_b(n):
                    if n == 0:
                        pool.wait_ge(consts_in, 80)
                    if n >= 4:
                        pool.wait_ge(biased, n - 3)
                    nc.gpsimd.tensor_scalar(alibi[:, n % 4, :], dist[:, n % 2, :], -(2.0 ** -(n // 2 + 1)), None, ALU.mult).then_inc(alibi_ready, 1)
                n = item_at(g, 8)
                if n is not None and is_b(n):
                    pool.wait_ge(ovar, n + 1)
                    r = sm[:, n, 4:5]
                    chain.after(chain.step(rsqrt(r)))
                    pool.wait_ge(attended, n + 1)
                    y = ybuf[:, n % 2, 1024 + n // 2 * HD:1024 + (n // 2 + 1) * HD]
                    nc.gpsimd.tensor_scalar(y, y, r, None, ALU.mult).then_inc(y_scaled, 1)
                b, j = g // 8, g % 8
                if b == 1:
                    if j == 0:
                        pool.wait_ge(var1, 1)
                        chain.after(chain.step(rsqrt(ss[:, 0:2])))
                        rsqrt(ss[0:META, 2:3]).then_inc(rstd1, 1)
                if b == KVA + 1:
                    if j in (3, 4):
                        rotate(j - 3, stg[:, j - 3, 0:256], P, 2, (4 + j - 3, 7 + j - 3))
                    if j == 5:
                        rotate(2, stgm[:, 0:256], META, 2, (6, 9))
                if b and W1[b - 1][0] == "qa" and j in (3, 4):
                    rotate(3 + 2 * (b - 8) + j - 3, stg[:, j - 3, :], P, 4, (j - 3, 2 + j - 3))

            pool.wait_ge(half_set, 1)
            for g in range(8 * Q_WOUT):
                block1(g)
            pool.wait_ge(yvar, 1)
            rsqrt(rp).then_inc(yrstd, 1)
            pool.wait_ge(h1var, 1)
            rsqrt(r2).then_inc(h1rstd, 1)
            pool.wait_ge(rel_in, 16)
            nc.gpsimd.tensor_copy(reltab[:, 0:127], dims(reltab[:, 127:128], [0, 127])).then_inc(rel_filled, 1)
            pool.wait_ge(poolw_in, 32)
            for w in range(4):
                pool.wait_ge(turned, TURNED[Q_W2 + 6 + w // 2, 1])
                u = ut[:, 2 * w:2 * w + 2, :]
                bufs = [wina[:], winb[:]]
                src = u
                if w:
                    pool.wait_ge(pooled, w)
                for level in range(w + 1):
                    d = 1 << level
                    dst = bufs[level % 2]
                    s1 = chain.step(nc.gpsimd.tensor_copy(dst[:, :, 0:d], src[:, :, 0:d]))
                    s2 = chain.step(nc.gpsimd.tensor_tensor(dst[:, :, d:TOK], src[:, :, d:TOK], src[:, :, 0:TOK - d], ALU.add))
                    chain.after(s2)
                    src = dst
                win = 2 << w
                s1 = chain.step(nc.gpsimd.tensor_tensor(src[:, :, 0:16], src[:, :, 0:16],
                                                        dims(invc[:, w, :], [0, 2], [1, 16]), ALU.mult))
                s2 = chain.step(nc.gpsimd.tensor_scalar(src[:, :, 16:TOK], src[:, :, 16:TOK], 1.0 / win, None, ALU.mult))
                chain.after(s2)
                nc.gpsimd.tensor_tensor(u, src, u, ALU.subtract).then_inc(pooled, 1)
            pool.wait_ge(h2var, 1)
            rsqrt(r3).then_inc(h2rstd, 1)
            with pool.Fori(0, FF_CHUNKS) as i:
                pool.wait_ge(ff_silu, i + 1)
                nc.gpsimd.tensor_tensor(fgate[:], fgate[:], dims(rbc3[:], [0, 4], [1, TOK]), ALU.mult).then_inc(ff_gate, 1)
            pool.wait_ge(last_var, 1)
            rsqrt(r4).then_inc(last_rstd, 1)


def tables():
    f = np.float32
    inv_freq = (np.float64(10000.0) ** (-np.arange(0, 64, 2) / 64.0)).astype(f)
    real = np.arange(TOK)
    row = np.concatenate([real // 64, np.zeros(META)]).astype(f)
    col = np.concatenate([real % 64, np.zeros(META)]).astype(f)
    ang = [(v[:, None] * inv_freq[None, :]).astype(f).astype(np.float64) for v in (row, col)]
    cos = np.concatenate([np.cos(a) for a in ang for _ in range(2)], 1).astype(f)
    sin = np.concatenate([s * np.sin(a) for a in ang for s in (-1, 1)], 1).astype(f)
    rope = np.zeros((P, 10, P), f)
    for n, (tab, i) in enumerate([(cos, 0), (cos, 1), (sin, 0), (sin, 1), (cos, 0), (cos, 1), (cos, 2), (sin, 0), (sin, 1), (sin, 2)]):
        part = tab[i * P:(i + 1) * P]
        rope[:len(part), n] = part
    qpos = META + np.arange(TOK).reshape(TT, P).T
    kpos = np.concatenate([META + np.arange(TOK), np.arange(META)])
    dist = np.abs(qpos[:, :, None] - kpos[None, None, :]).astype(f)
    count = np.minimum(np.arange(16)[None, :] + 1, 2 << np.arange(4)[:, None])
    invc = np.broadcast_to((1.0 / count).astype(f), (P, 4, 16)).copy()
    return {"rope_t": rope, "dist_t": dist, "invc_t": invc}


INPUTS = ("x", "meta_tokens", "w_in", "q_norm_g", "k_norm_g", "lambda_q1", "lambda_k1", "lambda_q2",
          "lambda_k2", "subln_g", "w_out", "post_norm_g", "w_in_2", "pool_w_2",
          "w_branch_a_2", "w_branch_b_2", "w_out_2", "w_gate_up_2", "w_down_2", "norm_final_2")


def kernel(**inputs):
    import numpy as np
    from concourse import bacc
    from concourse.bass_utils import run_bass_kernel_spmd

    nc = bacc.Bacc("TRN2", target_bir_lowering=False, num_devices=1)
    arrays = {name: np.ascontiguousarray(inputs[name]) for name in INPUTS}
    arrays["rel_rev"] = np.ascontiguousarray(inputs["rel_bias_2"][0][:, ::-1])
    arrays.update(tables())
    gains = [inputs[n].reshape(-1, P).T for n in ("pre_norm_g", "norm_mix_2", "norm_ffn_2", "pool_scale_2")]
    arrays["start_c"] = np.ascontiguousarray(np.concatenate([np.eye(P, dtype=np.float32)] + gains, axis=1))
    t = {name: nc.dram_tensor(name, a.shape, F32, kind="ExternalInput").ap() for name, a in arrays.items()}
    t["rel_scratch"] = nc.dram_tensor("rel_scratch", (P, HEADS2, REL), F32, kind="Internal").ap()
    out = nc.dram_tensor("out", (1, TOK, D), F32, kind="ExternalOutput").ap()
    build(nc, t, out)
    return run_bass_kernel_spmd(nc, [arrays], core_ids=[0]).results[0]["out"]
```
